# Optimizing a Trainium2 kernel written in Bass

```python
import jax, jax.numpy as jnp
from jax import lax
import numpy as np
import math

D_MODEL = 1024
BATCH = 1
SEQ = 256
DEPTH = 1

D_MIX = D_MODEL
MLSTM_WIDTH = D_MIX // 2
MLSTM_HEADS = 4
MLSTM_HEAD_DIM = MLSTM_WIDTH // MLSTM_HEADS
MLSTM_CHUNK = 64
CONV_WIDTH = 4
POOL_WIDTH = D_MIX - MLSTM_WIDTH
POOL_WINDOWS = (2, 4, 8, 16)
POOL_GROUPS = len(POOL_WINDOWS)
POOL_GROUP_DIM = POOL_WIDTH // POOL_GROUPS
N_IN = 4 * MLSTM_WIDTH + 2 * MLSTM_HEADS + POOL_WIDTH
N_EXPERTS = 32
TOP_K = 4
D_FF = D_MODEL
SWIGLU_LIMIT = 7.0
SWIGLU_ALPHA = 1.702
EXPERT_BLOCK = 128
EPS = 1e-5


def rmsnorm(x, g):
    xf = x.astype(jnp.float32)
    y = xf * lax.rsqrt(jnp.mean(xf * xf, axis=-1, keepdims=True) + EPS)
    return (y * g.astype(jnp.float32)).astype(x.dtype)

def causal_depthwise_conv(u, w):
    k = w.shape[0]
    return lax.conv_general_dilated(
        u, w[:, None, :].astype(u.dtype), window_strides=(1,), padding=[(k - 1, 0)],
        dimension_numbers=("NWC", "WIO", "NWC"), feature_group_count=u.shape[-1])

def mlstm_chunkwise(q, k, v, ig, lf):
    B, H, S, Dh = q.shape
    L = MLSTM_CHUNK
    NC = S // L
    q = q.reshape(B, H, NC, L, Dh)
    k = k.reshape(B, H, NC, L, Dh)
    v = v.reshape(B, H, NC, L, Dh)
    ig = ig.reshape(B, H, NC, L)
    lf = lf.reshape(B, H, NC, L)
    b = jnp.cumsum(lf, axis=-1)
    b_tot = b[..., -1]

    g = b_tot[..., None] - b + ig
    m_loc = jnp.max(g, axis=-1)
    w_loc = jnp.exp(g - m_loc[..., None])
    C_loc = jnp.einsum("bhclk,bhclv->bhckv", w_loc[..., None] * k, v)
    n_loc = jnp.einsum("bhcl,bhclk->bhck", w_loc, k)

    def step(carry, inp):
        C, n, m = carry
        C_l, n_l, m_l, bt = inp
        m_new = jnp.maximum(bt + m, m_l)
        s_old = jnp.exp(bt + m - m_new)
        s_loc = jnp.exp(m_l - m_new)
        C_new = s_old[..., None, None] * C + s_loc[..., None, None] * C_l
        n_new = s_old[..., None] * n + s_loc[..., None] * n_l
        return (C_new, n_new, m_new), (C, n, m)

    init = (jnp.zeros((B, H, Dh, Dh), jnp.float32),
            jnp.zeros((B, H, Dh), jnp.float32),
            jnp.zeros((B, H), jnp.float32))
    xs = (jnp.moveaxis(C_loc, 2, 0), jnp.moveaxis(n_loc, 2, 0),
          jnp.moveaxis(m_loc, 2, 0), jnp.moveaxis(b_tot, 2, 0))
    _, (C_in, n_in, m_in) = lax.scan(step, init, xs)
    C_in = jnp.moveaxis(C_in, 0, 2)
    n_in = jnp.moveaxis(n_in, 0, 2)
    m_in = jnp.moveaxis(m_in, 0, 2)

    causal = jnp.tril(jnp.ones((L, L), dtype=bool))
    log_d = b[..., :, None] - b[..., None, :] + ig[..., None, :]
    log_d = jnp.where(causal, log_d, -jnp.inf)
    a = b + m_in[..., None]
    m_out = jnp.maximum(a, jnp.max(log_d, axis=-1))
    s = jnp.einsum("bhcld,bhcrd->bhclr", q, k) * jnp.exp(log_d - m_out[..., None])
    inter = jnp.exp(a - m_out)
    num = (jnp.einsum("bhclr,bhcrv->bhclv", s, v)
           + inter[..., None] * jnp.einsum("bhcld,bhcdv->bhclv", q, C_in))
    den = jnp.sum(s, axis=-1) + inter * jnp.einsum("bhcld,bhcd->bhcl", q, n_in)
    h = num / jnp.maximum(jnp.abs(den), jnp.exp(-m_out))[..., None]
    return h.reshape(B, H, S, Dh)

def multiscale_pool(u, pool_w, pool_scale):
    B, S, _ = u.shape
    uf = u.astype(jnp.float32).reshape(B, S, POOL_GROUPS, POOL_GROUP_DIM)
    cs = jnp.concatenate([jnp.zeros((B, 1, POOL_GROUPS, POOL_GROUP_DIM), jnp.float32),
                          jnp.cumsum(uf, axis=1)], axis=1)
    t = jnp.arange(S)
    pooled = []
    for gi, w in enumerate(POOL_WINDOWS):
        c = cs[:, :, gi]
        c_lo = jnp.concatenate([jnp.zeros((B, w - 1, POOL_GROUP_DIM), jnp.float32),
                                c[:, :S - w + 1]], axis=1)
        cnt = jnp.minimum(t + 1, w).astype(jnp.float32)
        pooled.append((c[:, 1:] - c_lo) / cnt[None, :, None])
    pooled = jnp.stack(pooled, axis=2) - uf
    mixed = jnp.einsum("bsgc,gcd->bsgd", pooled, pool_w.astype(jnp.float32))
    mixed = mixed.reshape(B, S, POOL_WIDTH) * pool_scale.astype(jnp.float32)
    return mixed.astype(u.dtype)

def hybrid_mixer(h, w_in, ig_b, fg_b, conv_w, head_norm_g, pool_w, pool_scale, w_out):
    B, S, _ = h.shape
    W, H, Dh = MLSTM_WIDTH, MLSTM_HEADS, MLSTM_HEAD_DIM
    p = h @ w_in
    qk = p[..., :2 * W]
    v = p[..., 2 * W:3 * W]
    o = p[..., 3 * W:4 * W]
    gates = p[..., 4 * W:4 * W + 2 * H].astype(jnp.float32)
    u = p[..., 4 * W + 2 * H:]

    qk = jax.nn.silu(causal_depthwise_conv(qk, conv_w))

    def to_heads(t):
        return t.reshape(B, S, H, Dh).transpose(0, 2, 1, 3).astype(jnp.float32)

    q = to_heads(qk[..., :W])
    k = to_heads(qk[..., W:]) * (Dh ** -0.5)
    vh = to_heads(v)
    ig = (gates[..., :H] + ig_b.astype(jnp.float32)).transpose(0, 2, 1)
    lf = jax.nn.log_sigmoid(gates[..., H:] + fg_b.astype(jnp.float32)).transpose(0, 2, 1)
    hm = mlstm_chunkwise(q, k, vh, ig, lf)
    mu = jnp.mean(hm, axis=-1, keepdims=True)
    var = jnp.mean(jnp.square(hm - mu), axis=-1, keepdims=True)
    hm = (hm - mu) * lax.rsqrt(var + EPS)
    hm = hm.transpose(0, 2, 1, 3).reshape(B, S, W) * head_norm_g.astype(jnp.float32)
    y_m = (jax.nn.sigmoid(o.astype(jnp.float32)) * hm).astype(h.dtype)

    y_p = multiscale_pool(u, pool_w, pool_scale)

    return jnp.concatenate([y_m, y_p], axis=-1) @ w_out

def moe_ffn(h, w_router, b_router, w_gate, b_gate, w_up, b_up, w_down, b_down):
    B, S, D = h.shape
    T = B * S
    xt = h.reshape(T, D)
    logits = (xt @ w_router + b_router).astype(jnp.float32)
    top_vals, top_idx = lax.top_k(logits, TOP_K)
    top_gates = jax.nn.softmax(top_vals, axis=-1)

    A = T * TOP_K
    flat_expert = top_idx.reshape(A)
    flat_token = jnp.repeat(jnp.arange(T, dtype=jnp.int32), TOP_K)
    flat_gate = top_gates.reshape(A)
    order = jnp.argsort(flat_expert)
    s_expert = flat_expert[order]
    s_token = flat_token[order]
    s_gate = flat_gate[order]

    counts = jax.ops.segment_sum(jnp.ones((A,), jnp.int32), flat_expert, num_segments=N_EXPERTS)
    group_start = jnp.cumsum(counts) - counts
    padded = ((counts + EXPERT_BLOCK - 1) // EXPERT_BLOCK) * EXPERT_BLOCK
    padded_end = jnp.cumsum(padded)
    padded_start = padded_end - padded
    rank = jnp.arange(A, dtype=jnp.int32) - group_start[s_expert]
    dest = padded_start[s_expert] + rank

    n_blocks = -(-A // EXPERT_BLOCK) + N_EXPERTS
    P = n_blocks * EXPERT_BLOCK
    tok_buf = jnp.full((P,), T, jnp.int32).at[dest].set(s_token)
    gate_buf = jnp.zeros((P,), jnp.float32).at[dest].set(s_gate)
    block_start = jnp.arange(n_blocks, dtype=jnp.int32) * EXPERT_BLOCK
    block_expert = jnp.minimum(jnp.searchsorted(padded_end, block_start, side="right"),
                               N_EXPERTS - 1).astype(jnp.int32)

    x_pad = jnp.concatenate([xt, jnp.zeros((1, D), xt.dtype)], axis=0)
    x_buf = x_pad[tok_buf].reshape(n_blocks, EXPERT_BLOCK, D)

    def expert_block(args):
        xb, e = args
        gate = xb @ w_gate[e] + b_gate[e]
        up = xb @ w_up[e] + b_up[e]
        gate = jnp.minimum(gate, SWIGLU_LIMIT)
        up = jnp.clip(up, -SWIGLU_LIMIT, SWIGLU_LIMIT)
        glu = gate * jax.nn.sigmoid(SWIGLU_ALPHA * gate)
        return (glu * (up + 1.0)) @ w_down[e] + b_down[e]

    y_buf = lax.map(expert_block, (x_buf, block_expert)).reshape(P, D)
    y_buf = y_buf * gate_buf[:, None].astype(y_buf.dtype)
    out = jax.ops.segment_sum(y_buf, tok_buf, num_segments=T + 1)[:T]
    return out.reshape(B, S, D).astype(h.dtype)

def first_inputs(seed: int = 0) -> dict:
    key = jax.random.key(seed)
    ks = jax.random.split(key, 20)
    f32 = jnp.float32
    L_, D, E, F, H = DEPTH, D_MODEL, N_EXPERTS, D_FF, MLSTM_HEADS
    nrm = lambda k, shape, s: jax.random.normal(k, shape, f32) * s
    x = jax.random.normal(ks[0], (BATCH, SEQ, D), f32)
    norm1_g = 1.0 + nrm(ks[1], (L_, D), 0.02)
    w_in = nrm(ks[2], (L_, D, N_IN), D ** -0.5)
    ig_b = nrm(ks[3], (L_, H), 0.1)
    fg_b = jnp.broadcast_to(jnp.linspace(3.0, 6.0, H, dtype=f32), (L_, H)) + nrm(ks[4], (L_, H), 0.1)
    conv_w = nrm(ks[5], (L_, CONV_WIDTH, 2 * MLSTM_WIDTH), CONV_WIDTH ** -0.5)
    head_norm_g = 1.0 + nrm(ks[6], (L_, MLSTM_WIDTH), 0.02)
    pool_w = nrm(ks[7], (L_, POOL_GROUPS, POOL_GROUP_DIM, POOL_GROUP_DIM), POOL_GROUP_DIM ** -0.5)
    pool_scale = 1.0 + nrm(ks[8], (L_, POOL_WIDTH), 0.02)
    w_out = nrm(ks[9], (L_, D_MIX, D), D_MIX ** -0.5)
    norm2_g = 1.0 + nrm(ks[10], (L_, D), 0.02)
    w_router = nrm(ks[11], (L_, D, E), D ** -0.5)
    b_router = nrm(ks[12], (L_, E), 0.01)
    w_gate = nrm(ks[13], (L_, E, D, F), D ** -0.5)
    b_gate = nrm(ks[14], (L_, E, F), 0.01)
    w_up = nrm(ks[15], (L_, E, D, F), D ** -0.5)
    b_up = nrm(ks[16], (L_, E, F), 0.01)
    w_down = nrm(ks[17], (L_, E, F, D), F ** -0.5)
    b_down = nrm(ks[18], (L_, E, D), 0.01)
    normf_g = 1.0 + nrm(ks[19], (D,), 0.02)
    return {"x": x, "norm1_g": norm1_g, "w_in": w_in, "ig_b": ig_b, "fg_b": fg_b,
            "conv_w": conv_w, "head_norm_g": head_norm_g, "pool_w": pool_w,
            "pool_scale": pool_scale, "w_out": w_out, "norm2_g": norm2_g,
            "w_router": w_router, "b_router": b_router, "w_gate": w_gate,
            "b_gate": b_gate, "w_up": w_up, "b_up": b_up, "w_down": w_down,
            "b_down": b_down, "normf_g": normf_g}

def first_block(x, norm1_g, w_in, ig_b, fg_b, conv_w, head_norm_g, pool_w, pool_scale,
              w_out, norm2_g, w_router, b_router, w_gate, b_gate, w_up, b_up,
              w_down, b_down, normf_g):
    for l in range(DEPTH):
        h = rmsnorm(x, norm1_g[l])
        x = x + hybrid_mixer(h, w_in[l], ig_b[l], fg_b[l], conv_w[l], head_norm_g[l],
                             pool_w[l], pool_scale[l], w_out[l])
        h = rmsnorm(x, norm2_g[l])
        x = x + moe_ffn(h, w_router[l], b_router[l], w_gate[l], b_gate[l], w_up[l],
                        b_up[l], w_down[l], b_down[l])
    return rmsnorm(x, normf_g)


FOX_HEADS = 8
FOX_HEAD_DIM = 128
FOX_WIDTH = FOX_HEADS * FOX_HEAD_DIM
FOX_BLOCK = 128
GDN_HEADS = 8
GDN_HEAD_K = 128
GDN_HEAD_V = 128
GDN_K_WIDTH = GDN_HEADS * GDN_HEAD_K
GDN_V_WIDTH = GDN_HEADS * GDN_HEAD_V
GDN_CONV = 4
GDN_CONV_CH = 2 * GDN_K_WIDTH + GDN_V_WIDTH
GDN_CHUNK = 64
D_FF_2 = 2816
FFN_CONV = 3
EPS_2 = 1e-6

IN_SIZES = (FOX_WIDTH, FOX_WIDTH, FOX_WIDTH, FOX_HEADS,
            GDN_K_WIDTH, GDN_K_WIDTH, GDN_V_WIDTH, GDN_HEADS, GDN_HEADS, GDN_V_WIDTH,
            D_MODEL, D_MODEL)
D_IN = sum(IN_SIZES)


def rmsnorm_2(x, g):
    xf = x.astype(jnp.float32)
    xf = xf * lax.rsqrt(jnp.mean(xf * xf, axis=-1, keepdims=True) + EPS_2)
    return (xf * g.astype(jnp.float32)).astype(x.dtype)

def l2norm(x):
    xf = x.astype(jnp.float32)
    return xf * lax.rsqrt(jnp.sum(xf * xf, axis=-1, keepdims=True) + EPS_2)

def causal_dwconv(x, w):
    K = w.shape[0]
    S = x.shape[1]
    xp = jnp.pad(x, ((0, 0), (K - 1, 0), (0, 0)))
    return sum(xp[:, i:i + S, :] * w[i] for i in range(K))

def split_in(h):
    idx = np.cumsum(np.array(IN_SIZES))[:-1].tolist()
    return jnp.split(h, idx, axis=-1)

def fox_attention(q, k, v, log_f):
    B, S, H, Dh = q.shape
    nb = S // FOX_BLOCK
    scale = Dh ** -0.5
    c = jnp.cumsum(log_f.astype(jnp.float32), axis=1).transpose(0, 2, 1)
    kh = k.transpose(0, 2, 1, 3)
    vh = v.transpose(0, 2, 1, 3)
    qb = q.reshape(B, nb, FOX_BLOCK, H, Dh).transpose(1, 0, 3, 2, 4)
    cb = c.reshape(B, H, nb, FOX_BLOCK).transpose(2, 0, 1, 3)
    key_pos = jnp.arange(S)

    def block(args):
        qi, ci, i = args
        s = jnp.einsum('bhqd,bhkd->bhqk', qi, kh).astype(jnp.float32) * scale
        s = s + (ci[..., :, None] - c[..., None, :])
        q_pos = i * FOX_BLOCK + jnp.arange(FOX_BLOCK)
        causal = key_pos[None, :] <= q_pos[:, None]
        p = jax.nn.softmax(jnp.where(causal, s, -jnp.inf), axis=-1)
        return jnp.einsum('bhqk,bhkd->bhqd', p.astype(vh.dtype), vh)

    o = lax.map(block, (qb, cb, jnp.arange(nb)))
    return o.transpose(1, 0, 3, 2, 4).reshape(B, S, H * Dh)

def gated_delta_rule(q, k, v, g, beta):
    B, S, H, dk = q.shape
    dv = v.shape[-1]
    C = GDN_CHUNK
    N = S // C
    f32 = jnp.float32

    def chunk4(t):
        return t.astype(f32).reshape(B, N, C, H, t.shape[-1]).transpose(0, 3, 1, 2, 4)

    def chunk3(t):
        return t.astype(f32).reshape(B, N, C, H).transpose(0, 3, 1, 2)

    qc = chunk4(q) * (dk ** -0.5)
    kc = chunk4(k)
    vc = chunk4(v)
    bc = chunk3(beta)
    gc = jnp.cumsum(chunk3(g), axis=-1)

    tri_incl = jnp.tril(jnp.ones((C, C), dtype=bool))
    tri_strict = jnp.tril(jnp.ones((C, C), dtype=bool), k=-1)
    diff = gc[..., :, None] - gc[..., None, :]
    decay = jnp.exp(jnp.where(tri_incl, diff, -jnp.inf))

    kb = kc * bc[..., None]
    A = jnp.where(tri_strict, jnp.einsum('bhncd,bhnmd->bhncm', kb, kc) * decay, 0.0)
    lhs = A + jnp.eye(C, dtype=f32)
    rhs = jnp.concatenate([vc * bc[..., None], kb * jnp.exp(gc)[..., None]], axis=-1)
    sol = lax.linalg.triangular_solve(lhs, rhs, left_side=True, lower=True, unit_diagonal=True)
    u_hat, w = sol[..., :dv], sol[..., dv:]

    attn = jnp.einsum('bhncd,bhnmd->bhncm', qc, kc) * decay
    q_dec = qc * jnp.exp(gc)[..., None]
    k_dec = kc * jnp.exp(gc[..., -1:] - gc)[..., None]
    g_last = jnp.exp(gc[..., -1])

    xs = tuple(jnp.moveaxis(t, 2, 0) for t in (u_hat, w, attn, q_dec, k_dec, g_last))

    def step(state, inp):
        u_hat_i, w_i, attn_i, q_dec_i, k_dec_i, gl_i = inp
        u = u_hat_i - jnp.einsum('bhcd,bhdv->bhcv', w_i, state)
        o = jnp.einsum('bhcd,bhdv->bhcv', q_dec_i, state) + jnp.einsum('bhcm,bhmv->bhcv', attn_i, u)
        state = state * gl_i[..., None, None] + jnp.einsum('bhcd,bhcv->bhdv', k_dec_i, u)
        return state, o

    s0 = jnp.zeros((B, H, dk, dv), f32)
    _, o = lax.scan(step, s0, xs)
    return o.transpose(1, 0, 3, 2, 4).reshape(B, S, H, dv).astype(v.dtype)

def second_inputs(seed: int = 0) -> dict:
    key = jax.random.key(seed)
    ks = jax.random.split(key, 20)
    L, D = DEPTH, D_MODEL
    nrm = jax.random.normal
    x = nrm(ks[0], (BATCH, SEQ, D), jnp.float32)
    norm_mix = 1.0 + 0.05 * nrm(ks[1], (L, D), jnp.float32)
    w_in = nrm(ks[2], (L, D, D_IN), jnp.float32) * D ** -0.5
    fox_f_bias = 3.0 + 0.5 * nrm(ks[3], (L, FOX_HEADS), jnp.float32)
    gdn_conv_w = nrm(ks[4], (L, GDN_CONV, GDN_CONV_CH), jnp.float32) * GDN_CONV ** -0.5
    gdn_a_log = jnp.log(jax.random.uniform(ks[5], (L, GDN_HEADS), jnp.float32, 1.0, 16.0))
    dt = jnp.exp(jax.random.uniform(ks[6], (L, GDN_HEADS), jnp.float32, math.log(1e-3), math.log(1e-1)))
    gdn_dt_bias = dt + jnp.log(-jnp.expm1(-dt))
    gdn_norm = 1.0 + 0.05 * nrm(ks[7], (L, GDN_HEAD_V), jnp.float32)
    w_branch_fox = nrm(ks[8], (L, FOX_WIDTH, D), jnp.float32) * FOX_WIDTH ** -0.5
    w_branch_gdn = nrm(ks[9], (L, GDN_V_WIDTH, D), jnp.float32) * GDN_V_WIDTH ** -0.5
    w_out = nrm(ks[10], (L, D, D), jnp.float32) * D ** -0.5
    norm_ffn = 1.0 + 0.05 * nrm(ks[11], (L, D), jnp.float32)
    w_up = nrm(ks[12], (L, D, 2 * D_FF_2), jnp.float32) * D ** -0.5
    ffn_conv_w = nrm(ks[13], (L, FFN_CONV, 2 * D_FF_2), jnp.float32) * FFN_CONV ** -0.5
    w_down = nrm(ks[14], (L, D_FF_2, D), jnp.float32) * D_FF_2 ** -0.5
    norm_final = 1.0 + 0.05 * nrm(ks[15], (D,), jnp.float32)
    return {"x": x, "norm_mix": norm_mix, "w_in": w_in, "fox_f_bias": fox_f_bias,
            "gdn_conv_w": gdn_conv_w, "gdn_a_log": gdn_a_log, "gdn_dt_bias": gdn_dt_bias,
            "gdn_norm": gdn_norm, "w_branch_fox": w_branch_fox, "w_branch_gdn": w_branch_gdn,
            "w_out": w_out, "norm_ffn": norm_ffn, "w_up": w_up, "ffn_conv_w": ffn_conv_w,
            "w_down": w_down, "norm_final": norm_final}

def second_block(x, norm_mix, w_in, fox_f_bias, gdn_conv_w, gdn_a_log, gdn_dt_bias, gdn_norm,
              w_branch_fox, w_branch_gdn, w_out, norm_ffn, w_up, ffn_conv_w, w_down, norm_final):
    B, S, D = x.shape
    h = x
    for l in range(DEPTH):
        hn = rmsnorm_2(h, norm_mix[l])
        proj = jnp.einsum('bsd,de->bse', hn, w_in[l])
        (fq, fk, fv, ff, gq, gk, gv, ga, gb, gz, gate_fox, gate_gdn) = split_in(proj)

        log_f = jax.nn.log_sigmoid(ff.astype(jnp.float32) + fox_f_bias[l].astype(jnp.float32))
        y_fox = fox_attention(fq.reshape(B, S, FOX_HEADS, FOX_HEAD_DIM),
                              fk.reshape(B, S, FOX_HEADS, FOX_HEAD_DIM),
                              fv.reshape(B, S, FOX_HEADS, FOX_HEAD_DIM), log_f)

        qkv = jax.nn.silu(causal_dwconv(jnp.concatenate([gq, gk, gv], axis=-1), gdn_conv_w[l]))
        cq, ck, cv = jnp.split(qkv, [GDN_K_WIDTH, 2 * GDN_K_WIDTH], axis=-1)
        q = l2norm(cq.reshape(B, S, GDN_HEADS, GDN_HEAD_K))
        k = l2norm(ck.reshape(B, S, GDN_HEADS, GDN_HEAD_K))
        v = cv.reshape(B, S, GDN_HEADS, GDN_HEAD_V)
        g = -jnp.exp(gdn_a_log[l].astype(jnp.float32)) * jax.nn.softplus(
            ga.astype(jnp.float32) + gdn_dt_bias[l].astype(jnp.float32))
        beta = jax.nn.sigmoid(gb.astype(jnp.float32))
        o = gated_delta_rule(q, k, v, g, beta)
        o = rmsnorm_2(o, gdn_norm[l]) * jax.nn.silu(gz.reshape(B, S, GDN_HEADS, GDN_HEAD_V))
        y_gdn = o.reshape(B, S, GDN_V_WIDTH)

        y = (jax.nn.sigmoid(gate_fox) * jnp.einsum('bse,ed->bsd', y_fox, w_branch_fox[l])
             + jax.nn.sigmoid(gate_gdn) * jnp.einsum('bse,ed->bsd', y_gdn, w_branch_gdn[l]))
        h = h + jnp.einsum('bsd,de->bse', y, w_out[l])

        hn = rmsnorm_2(h, norm_ffn[l])
        up = causal_dwconv(jnp.einsum('bsd,df->bsf', hn, w_up[l]), ffn_conv_w[l])
        u_gate, u_val = jnp.split(up, 2, axis=-1)
        h = h + jnp.einsum('bsf,fd->bsd', jax.nn.silu(u_gate) * u_val, w_down[l])
    return rmsnorm_2(h, norm_final)


def setup_inputs(seed=0):
    out = dict(first_inputs(seed))
    for name, value in second_inputs(seed + 1).items():
        if name != "x":
            out[name + "_2"] = value
    return out


def reference(
    x, norm1_g, w_in, ig_b, fg_b, conv_w, head_norm_g, pool_w, pool_scale, w_out, norm2_g,
    w_router, b_router, w_gate, b_gate, w_up, b_up, w_down, b_down, normf_g, norm_mix_2, w_in_2,
    fox_f_bias_2, gdn_conv_w_2, gdn_a_log_2, gdn_dt_bias_2, gdn_norm_2, w_branch_fox_2,
    w_branch_gdn_2, w_out_2, norm_ffn_2, w_up_2, ffn_conv_w_2, w_down_2, norm_final_2,
):
    x = first_block(
        x, norm1_g, w_in, ig_b, fg_b, conv_w, head_norm_g, pool_w, pool_scale, w_out, norm2_g,
        w_router, b_router, w_gate, b_gate, w_up, b_up, w_down, b_down, normf_g,
    )
    return second_block(
        x, norm_mix_2, w_in_2, fox_f_bias_2, gdn_conv_w_2, gdn_a_log_2, gdn_dt_bias_2,
        gdn_norm_2, w_branch_fox_2, w_branch_gdn_2, w_out_2, norm_ffn_2, w_up_2, ffn_conv_w_2,
        w_down_2, norm_final_2,
    )


_drawn_inputs = setup_inputs


def setup_inputs(seed=0):
    import zlib

    import numpy as np

    out = dict(_drawn_inputs(seed))
    spreads = {}
    factors = {'ig_b': 64.0, 'b_gate': 8.0, 'b_up': 8.0, 'b_down': 8.0, 'gdn_norm_2': 3.723}
    for name, (base, spread) in spreads.items():
        noise = np.random.default_rng([zlib.crc32(name.encode()), seed]).standard_normal(out[name].shape)
        drawn = base * np.exp(spread * noise) if base else spread * noise
        out[name] = __import__('jax').numpy.asarray(drawn.astype(out[name].dtype))
    for name, factor in factors.items():
        out[name] = (out[name] * factor).astype(out[name].dtype)
    return out
```

```python
from contextlib import ExitStack

import numpy as np
import concourse.bass as bass
from concourse import mybir

F32 = mybir.dt.float32
I32 = mybir.dt.int32
U32 = mybir.dt.uint32
ALU = mybir.AluOpType
ACT = mybir.ActivationFunctionType
AX = mybir.AxisListType

P = 128
D = 1024
S = 256
NT = S // P
KC = D // P
SLOTS = 6
PIECE = 4096
NH = 4
NE = 32
TOPK = 4
CAP = 64
EPS1 = 1e-5
EPS2 = 1e-6


class Ring:

    def __init__(self, sem, tag, buf, first=0, slots=SLOTS):
        self.buf, self.slots = buf, slots
        self.loaded = [sem(f"{tag}_loaded{s}") for s in range(slots)]
        self.first = first

    def nth(self, g):
        s = g % self.slots
        return (g - (s if s >= self.first else s + self.slots)) // self.slots

    def slot(self, g):
        return self.buf[:, g % self.slots, :]

    def load(self, eng, g, dst, src):
        eng.dma_start(dst, src).then_inc(self.loaded[g % self.slots], 16)

    def landed(self, pe, g):
        pe.wait_ge(self.loaded[g % self.slots], 16 * (self.nth(g) + 1))


class Banks:

    def __init__(self, sem, tag, ps):
        self.ps = ps
        self.full = [sem(f"{tag}_full{b}") for b in range(8)]
        self.free = [sem(f"{tag}_free{b}") for b in range(8)]
        self.uses = [0] * 8
        self.at = {}
        self.turn = 0

    def plan(self, *keys):
        for key in keys:
            b = self.turn % 8
            self.turn += 1
            self.at[key] = (b, self.uses[b])
            self.uses[b] += 1

    def claim(self, pe, key):
        b, n = self.at[key]
        if n > 0:
            pe.wait_ge(self.free[b], n)
        return self.ps[:, b, :]

    def filled(self, last, key):
        last.then_inc(self.full[self.at[key][0]], 1)

    def take(self, eng, key):
        b, n = self.at[key]
        eng.wait_ge(self.full[b], n + 1)
        return self.ps[:, b, :]

    def release(self, last, key):
        last.then_inc(self.free[self.at[key][0]], 1)

    def moved(self, eng, key):
        b, n = self.at[key]
        eng.wait_ge(self.free[b], n + 1)

    def done(self, eng, key):
        self.take(eng, key)


class Chain:

    def __init__(self, eng, sem, n=0):
        self.eng, self.sem, self.n, self.base = eng, sem, n, None

    def __call__(self, ins):
        self.n += 1
        ins.then_inc(self.sem, 1)
        self.wait()

    def mark(self, ins):
        self.n += 1
        ins.then_inc(self.sem, 1)

    def wait(self):
        self.eng.wait_ge(self.sem, self.n if self.base is None else self.base + self.n)


def bcast(ap, n):
    return ap.unsqueeze(2).to_broadcast([ap.shape[0], ap.shape[1], n])


def build(nc, A, out, dbg=None):
    top = ExitStack()
    sems = {}

    def sem(name):
        if name not in sems:
            sems[name] = top.enter_context(nc.semaphore(name))
        return sems[name]

    def sb(name, shape, dt=F32, stack=None):
        return (stack or top).enter_context(nc.sbuf_tensor(name, shape, dt))

    with top:
        ps = top.enter_context(nc.psum_tensor("ps", [P, 8, 512], F32))
        ring_buf = sb("ring_buf", [P, SLOTS, PIECE])
        x = sb("x", [P, NT, D])
        xn = sb("xn", [P, NT, D])
        hT = sb("hT", [P, KC, S])
        ident = sb("ident", [P, P])
        tri = sb("tri", [P, P])
        ustrict = sb("ustrict", [P, P])
        ones = sb("ones", [P, 2 * P])
        sel = sb("sel", [8, 8, P])
        stat = sb("stat", [P, 16])
        prow1 = sb("prow1", [P, P])
        prow2 = sb("prow2", [P, P])
        prm1 = sb("prm1", [P, P])
        prm2 = sb("prm2", [P, P])
        slot = sb("slot", [P, NT, NE])
        gate = sb("gate", [P, NT, NE])
        iota_cap = sb("iota_cap", [P, 2, CAP])
        passes = sb("passes", [1, 1], I32)
        ab = top.enter_context(ExitStack())
        brow = sb("brow", [1, 2, D], stack=ab)
        ring = Ring(sem, "ringA", ring_buf, first=5)
        banks = Banks(sem, "bankA", ps)
        k = Kit(nc, sem, ident, stat, x, xn, hT)
        with ExitStack() as a:
            phase_a(nc, A, sem, lambda n, s, dt=F32: sb(n, s, dt, a), ring, banks, k, locals())
        if dbg:
            dump(nc, sem, dbg.get("A"), locals(), "A")
        gain = sb("gain", [P, D])
        ringC = Ring(sem, "ringC", ring_buf, slots=5)
        spare = ring_buf[:, 5, :]
        banksC = Banks(sem, "bankC", ps)
        with ExitStack() as b:
            phase_b(nc, A, sem, lambda n, s, dt=F32: sb(n, s, dt, b), ring, banks, locals())
        if dbg:
            dump(nc, sem, dbg.get("B"), locals(), "B")
        with ExitStack() as c:
            phase_c(nc, A, sem, lambda n, s, dt=F32: sb(n, s, dt, c), ringC, banksC, k, locals())
        if dbg:
            dump(nc, sem, dbg.get("C"), locals(), "C")
        with ExitStack() as d:
            phase_d(nc, A, out, sem, lambda n, s, dt=F32: sb(n, s, dt, d), ringC, banksC, k, locals())


def dump(nc, sem, what, env, ph):
    if not what:
        return
    with nc.Block() as block:
        @block.sync
        def _(sp):
            for name, ap in what.items():
                sp.dma_start(ap, env[name][:]).then_inc(sem("dumped" + ph), 16)

            n = 16 * len(what)
            sp.wait_ge(sem("dumped" + ph), n)


P1 = dict(norm1_g=0, norm2_g=8, head_norm_g=16, pool_scale=20, conv_w=24)
P2 = dict(norm_mix_2=0, norm_ffn_2=8, gdn_norm_2=16, gdn_conv_w_2=17)


class Kit:

    def __init__(self, nc, sem, ident, stat, x, xn, hT):
        self.nc, self.sem, self.ident, self.stat, self.x, self.xn, self.hT = nc, sem, ident, stat, x, xn, hT

    def squares(self, act, tag, n, junk):
        for t in range(NT):
            act.activation(junk[:, t, :], self.x[:, t, :], ACT.Square,
                           accum_out=self.stat[:, 4 * n + t:4 * n + t + 1]).then_inc(self.sem(tag + "_squares"), 1)

    def root(self, act, tag, n):
        c = self.stat[:, 4 * n:4 * n + 2]
        act.wait_ge(self.sem(tag + "_mean"), 1)
        act.activation(c, c, ACT.Sqrt).then_inc(self.sem(tag + "_root"), 1)

    def scale(self, v, chain, tag, n, eps):
        c = self.stat[:, 4 * n:4 * n + 2]
        r = self.stat[:, 4 * n + 2:4 * n + 4]
        v.wait_ge(self.sem(tag + "_squares"), NT)
        v.tensor_scalar(c, c, 1.0 / D, eps, ALU.mult, ALU.add).then_inc(self.sem(tag + "_mean"), 1)
        v.wait_ge(self.sem(tag + "_root"), 1)
        chain(v.reciprocal(r, c))
        for t in range(NT):
            v.tensor_scalar(self.xn[:, t, :], self.x[:, t, :], r[:, t:t + 1], None, ALU.mult)\
                .then_inc(self.sem(tag + "_xn"), 1)

    def gained(self, v, chain, tag, n, eps, gain, out=None):
        c = self.stat[:, 4 * n:4 * n + 2]
        r = self.stat[:, 4 * n + 2:4 * n + 4]
        v.wait_ge(self.sem(tag + "_squares"), NT)
        v.tensor_scalar(c, c, 1.0 / D, eps, ALU.mult, ALU.add).then_inc(self.sem(tag + "_mean"), 1)
        v.wait_ge(self.sem(tag + "_root"), 1)
        chain(v.reciprocal(r, c))
        for t in range(NT):
            v.scalar_tensor_tensor((self.x if out is None else out)[:, t, :], self.x[:, t, :], r[:, t:t + 1],
                                   gain, ALU.mult, ALU.mult).then_inc(self.sem(tag + "_x"), 1)

    def transposes(self, pe, banks, tag):
        pe.wait_ge(self.sem(tag + "_xn"), NT)
        for j in range(KC // 2):
            bank = banks.claim(pe, (tag, j))
            for c in (2 * j, 2 * j + 1):
                for t in range(NT):
                    o = (c % 2) * S + t * P
                    last = pe.transpose(bank[:, o:o + P], self.xn[:, t, c * P:(c + 1) * P], self.ident[:, :])
            banks.filled(last, (tag, j))

    def evacuate(self, v, banks, tag, g):
        for j in range(KC // 2):
            bank = banks.take(v, (tag, j))
            last = v.tensor_tensor(self.hT[:, 2 * j:2 * j + 2, :], bank.rearrange("p (c t) -> p c t", c=2),
                                   bcast(g[:, 2 * j:2 * j + 2], S), ALU.mult)
            banks.release(last, (tag, j))


EXPERT = 12


def load_biases(sp, A, brow, sem, e):
    for m, name in enumerate(("b_gate", "b_up")):
        sp.dma_start(brow[0:1, m, :], A[name][0][bass.ds(e, 1), :]).then_inc(sem("brow_in"), 16)


def load_half(sp, A, ring, m, h, e):
    g = EXPERT + 2 * m + h
    w = A[("w_gate", "w_up", "w_down")[m]][0]
    ring.load(sp, g, ring.slot(g).rearrange("p (c n) -> p c n", c=4),
              w[bass.ds(e, 1), h * 512:(h + 1) * 512, :].rearrange("a (c p) n -> p (a c) n", p=P))


def phase_a(nc, A, sem, sb, ring, banks, k, env):
    x, xn, hT, ident, tri, ustrict, ones, sel = (env[n] for n in "x xn hT ident tri ustrict ones sel".split())
    prow1, prow2, prm1, prm2, slot, gate, iota_cap, passes, brow = (
        env[n] for n in "prow1 prow2 prm1 prm2 slot gate iota_cap passes brow".split())
    W = NH * P

    wg = sb("wg", [P, KC, 8])
    qkT = sb("qkT", [P, 8, S])
    vext = sb("vext", [P, NT, NH, P + 1])
    og = sb("og", [P, NT, W])
    pa = sb("pa", [P, 4, S])
    pb = sb("pb", [P, 4, S])
    inv = sb("inv", [P, 4, S])
    tcount = sb("tcount", [P, S])
    yT = sb("yT", [P, KC, S])
    uT = yT[:, 0:4, :]
    DT = sb("DT", [P, NT, NH, S])
    hm = qkT[:, 0:4, :].rearrange("p (t a) (b d) -> p t (a b) d", t=NT, b=2)
    den = sb("den", [P, NT, NH])
    bst = sb("bst", [P, NT * NH, 6])
    mv = sb("mv", [P, NT * NH, 2])
    rs = sb("rs", [P, NT * NH])
    rows = sb("rows", [4, 10, S])
    FX, AB, E, L, LF, B, C, M, NM, EM = range(10)
    gb = sb("gb", [4, 2])
    ccol = sb("ccol", [P, 16])
    pool_w = sb("pool_w", [P, 4, P])
    wr = sb("wr", [P, KC, NE])
    brt = sb("brt", [P, NE])
    bdn = sb("bdn", [NE, D])
    lg = sb("lg", [P, NT, NE])
    v8 = sb("v8", [P, NT, 8])
    i8 = sb("i8", [P, NT, 8], U32)
    f8 = sb("f8", [P, NT, 8])
    e4 = sb("e4", [P, NT, 4])
    es = sb("es", [P, NT])
    mask = sb("mask", [P, NT, NE])
    tmp = sb("tmp", [P, NT, NE])
    iota_e = sb("iota_e", [P, NE])
    gT = sb("gT", [NE, NT, P])
    cnt = sb("cnt", [1, NE])
    cm = sb("cm", [1, 4])

    w_in, w_out = A["w_in"][0], A["w_out"][0]
    IN_COLS = [0, W, 2 * W, 3 * W, 4 * W + 2 * NH]
    Q_, K_, V_, O_, U_, OUT0, OUT1 = range(5, 12)

    banks.plan("prm1", *[("n1", j) for j in range(4)], "gates", *[("qk", j) for j in range(4)],
               "cols", ("mb", 0), ("mb", 1), ("v", 0), ("v", 1), *[("sc", h) for h in range(NH)],
               ("o", 0), ("o", 1), ("u", 0), ("u", 1),
               *[("num", j, hp) for j in range(NT) for hp in range(2)],
               "prm2", ("pool", 0), ("pool", 1), ("ym", 0), ("ym", 1),
               *[("out", n, t) for n in range(2) for t in range(NT)],
               *[("n2", j) for j in range(4)], "lg", "rk", "gt",
               *[("bd", t, n) for t in range(NT) for n in range(2)])

    def piece(g):
        return ring.slot(g).rearrange("p (c n) -> p c n", c=KC)

    with nc.Block() as block:
        @block.sync
        def _(sp):
            for j, c0 in enumerate(IN_COLS):
                ring.load(sp, Q_ + j, piece(Q_ + j), w_in[:, c0:c0 + 512].rearrange("(c p) n -> p c n", p=P))
            for n in range(2):
                if n == 1:
                    banks.done(sp, ("qk", 1))
                ring.load(sp, OUT0 + n, piece(OUT0 + n),
                          w_out[:, n * 512:(n + 1) * 512].rearrange("(c p) n -> p c n", p=P))
            load_biases(sp, A, brow, sem, 0)
            for m in range(3):
                for h in range(2):
                    g = 12 + 2 * m + h
                    banks.done(sp, [("qk", 3), ("v", 1), ("o", 1), ("u", 1), ("out", 0, 1), ("out", 1, 1)][2 * m + h])
                    load_half(sp, A, ring, m, h, 0)

        @block.scalar
        def _(act):
            act.dma_start(x[:, :, :], A["x"][0].rearrange("(t p) d -> p t d", p=P)).then_inc(sem("x_in"), 16)
            for name, n in (("norm1_g", 8), ("norm2_g", 8), ("head_norm_g", 4), ("pool_scale", 4)):
                act.dma_start(prow1[P1[name]:P1[name] + n, :],
                              A[name][0].rearrange("(c p) -> c p", p=P)).then_inc(sem("prow1_in"), 16)
            for i in range(4):
                act.dma_start(prow1[24 + 8 * i:32 + 8 * i, :],
                              A["conv_w"][0, i].rearrange("(c p) -> c p", p=P)).then_inc(sem("prow1_in"), 16)
            act.dma_start(wg[:, :, :], w_in[:, 4 * W:4 * W + 8].rearrange("(c p) n -> p c n", p=P))\
                .then_inc(sem("wg_in"), 16)
            act.dma_start(gb[:, 0:1], A["ig_b"].rearrange("a h -> h a")).then_inc(sem("gb_in"), 16)
            act.dma_start(gb[:, 1:2], A["fg_b"].rearrange("a h -> h a")).then_inc(sem("gb_in"), 16)
            act.wait_ge(sem("x_in"), 16)
            k.squares(act, "n1", 0, hT[:, :, :].rearrange("p (t c) n -> p t (c n)", t=NT))
            k.root(act, "n1", 0)
            act.dma_start(pool_w[:, :, :], A["pool_w"][0].rearrange("g c d -> c g d")).then_inc(sem("pool_w_in"), 16)
            act.dma_start(wr[:, :, :], A["w_router"][0].rearrange("(c p) n -> p c n", p=P)).then_inc(sem("wr_in"), 16)
            act.dma_start(brt[:, :], A["b_router"].to_broadcast([P, NE])).then_inc(sem("wr_in"), 16)
            act.dma_start(bdn[:, :], A["b_down"][0]).then_inc(sem("bdn_in"), 16)
            for name, n in (("norm_mix_2", 8), ("norm_ffn_2", 8), ("gdn_norm_2", 1)):
                act.dma_start(prow2[P2[name]:P2[name] + n, :],
                              A[name][0].rearrange("(c p) -> c p", p=P)).then_inc(sem("prow2_in"), 16)
            for i in range(4):
                act.dma_start(prow2[17 + 24 * i:41 + 24 * i, :],
                              A["gdn_conv_w_2"][0, i].rearrange("(c p) -> c p", p=P)).then_inc(sem("prow2_in"), 16)
            chain = Chain(act, sem("actA"))
            act.wait_ge(sem("fx"), 1)
            chain(act.activation(rows[:, AB, :], rows[:, FX, :], ACT.Abs))
            chain(act.activation(rows[:, E, :], rows[:, AB, :], ACT.Exp, scale=-1.0))
            act.activation(rows[:, L, :], rows[:, E, :], ACT.Ln, bias=1.0).then_inc(sem("ln1p"), 1)
            act.wait_ge(sem("nm"), 1)
            act.activation(rows[:, EM, :], rows[:, NM, :], ACT.Exp).then_inc(sem("em"), 1)
            for j in range(4):
                banks.moved(act, ("qk", j))
                act.activation(qkT[:, 2 * j:2 * j + 2, :], qkT[:, 2 * j:2 * j + 2, :], ACT.Silu)\
                    .then_inc(sem("qk_silu"), 1)
            banks.moved(act, ("mb", 0))
            banks.moved(act, ("mb", 1))
            for t in range(NT):
                act.activation(DT[:, t, :, t * P:], DT[:, t, :, t * P:], ACT.Exp).then_inc(sem("decay"), 1)
            for t in range(NT):
                bank = banks.take(act, ("o", t))
                last = act.activation(og[:, t, :], bank, ACT.Sigmoid)
                banks.release(last, ("o", t))
            for j in range(2):
                bank = banks.take(act, ("u", j))
                last = act.copy(uT[:, 2 * j:2 * j + 2, :], bank.rearrange("p (c t) -> p c t", c=2))
                banks.release(last, ("u", j))
            act.wait_ge(sem("hvar"), 1)
            act.activation(rs[:, :], rs[:, :], ACT.Sqrt).then_inc(sem("hroot"), 1)
            for g in range(4):
                if g % 2 == 0:
                    bank = banks.take(act, ("pool", g // 2))
                last = act.activation(yT[:, 4 + g, :], bank[:, (g % 2) * S:(g % 2 + 1) * S], ACT.Copy,
                                      scale=prm1[:, P1["pool_scale"] + g:P1["pool_scale"] + g + 1])
                if g % 2:
                    banks.release(last, ("pool", g // 2))
            for n in range(2):
                for t in range(NT):
                    banks.moved(act, ("out", n, t))
            k.squares(act, "n2", 1, yT[:, :, :].rearrange("p (t c) n -> p t (c n)", t=NT))
            k.root(act, "n2", 1)
            act.wait_ge(sem("v8neg"), 1)
            for t in range(NT):
                act.activation(e4[:, t, :], v8[:, t, 0:4], ACT.Exp, bias=f8[:, t, 7:8],
                               accum_out=es[:, t:t + 1]).then_inc(sem("e4"), 1)

        @block.gpsimd
        def _(g):
            chain = Chain(g, sem("poolA"))
            chain.mark(g.memset(ones[:, :], 1.0))
            chain.mark(g.memset(vext[:, :, :, P:P + 1], 1.0))
            chain(g.memset(sel[:, :, :], 1.0))
            g.affine_select(out=ident[:, :], in_=ones[:, 0:P], compare_op=ALU.is_equal, fill=0.0, base=0,
                            pattern=[[-1, P]], channel_multiplier=1).then_inc(sem("consts"), 1)
            g.affine_select(out=tri[:, :], in_=ones[:, 0:P], compare_op=ALU.is_ge, fill=0.0, base=0,
                            pattern=[[1, P]], channel_multiplier=-1).then_inc(sem("consts"), 1)
            g.affine_select(out=ustrict[:, :], in_=ones[:, 0:P], compare_op=ALU.is_gt, fill=0.0, base=0,
                            pattern=[[1, P]], channel_multiplier=-1).then_inc(sem("consts"), 1)
            g.affine_select(out=sel[:, :, :], in_=sel[:, :, :], compare_op=ALU.is_equal, fill=0.0, base=0,
                            pattern=[[-1, 8], [0, P]], channel_multiplier=1).then_inc(sem("consts"), 1)
            g.iota(iota_cap[:, :, :], pattern=[[0, 2], [1, CAP]], base=0, channel_multiplier=0,
                   allow_small_or_imprecise_dtypes=True).then_inc(sem("consts"), 1)
            g.iota(iota_e[:, :], pattern=[[1, NE]], base=0, channel_multiplier=0,
                   allow_small_or_imprecise_dtypes=True).then_inc(sem("consts"), 1)
            g.iota(tcount[:, :], pattern=[[1, S]], base=1, channel_multiplier=0,
                   allow_small_or_imprecise_dtypes=True).then_inc(sem("tcount"), 1)
            for t in range(NT):
                g.wait_ge(sem("decay"), t + 1)
                g.tensor_tensor(DT[:, t, :, t * P:t * P + P], DT[:, t, :, t * P:t * P + P],
                                tri[:, :].unsqueeze(1).to_broadcast([P, NH, P]), ALU.mult)\
                    .then_inc(sem("decay_masked"), 1)
            for j in range(2):
                banks.moved(g, ("u", j))
            g.wait_ge(sem("inv"), 4)
            src = uT
            for n in range(4):
                dst = (pa, pb)[n % 2]
                w = 1 << n
                chain.mark(g.tensor_tensor(dst[:, n:, w:], src[:, n:, w:], src[:, n:, :S - w], ALU.add))
                chain(g.tensor_copy(dst[:, n:, 0:w], src[:, n:, 0:w]))
                src = dst
                chain(g.tensor_tensor(inv[:, n, :], inv[:, n, :], dst[:, n, :], ALU.mult))
            g.tensor_tensor(inv[:, :, :], inv[:, :, :], uT[:, :, :], ALU.subtract).then_inc(sem("pooled"), 1)

        @block.vector
        def _(v):
            chain = Chain(v, sem("dveA"))
            k.scale(v, chain, "n1", 0, EPS1)
            bank = banks.take(v, "prm1")
            last = v.tensor_copy(prm1[:, 0:56], bank[:, 0:56])
            banks.release(last, "prm1")
            banks.moved(v, "prm1")
            k.evacuate(v, banks, "n1", prm1[:, 0:8])
            v.wait_ge(sem("gb_in"), 32)
            bank = banks.take(v, "gates")
            v.tensor_scalar(rows[:, FX, :], bank[0:4, S:2 * S], gb[:, 1:2], None, ALU.add).then_inc(sem("fx"), 1)
            v.wait_ge(sem("tcount"), 1)
            chain(v.reciprocal(tcount[:, :], tcount[:, :]))
            for n in range(4):
                v.tensor_scalar(inv[:, n, :], tcount[:, :], 1.0 / (2 << n), None, ALU.max).then_inc(sem("inv"), 1)
            v.wait_ge(sem("ln1p"), 1)
            chain(v.scalar_tensor_tensor(rows[:, LF, :], rows[:, FX, :], 0.0, rows[:, L, :], ALU.min, ALU.subtract))
            v.wait_ge(sem("consts"), 6)
            chain(v.tensor_tensor_scan(rows[:, B, :], ones[0:4, :], rows[:, LF, :], 0.0, ALU.mult, ALU.add))
            last = v.scalar_tensor_tensor(rows[:, C, :], bank[0:4, 0:S], gb[:, 0:1], rows[:, B, :],
                                          ALU.add, ALU.subtract)
            banks.release(last, "gates")
            banks.moved(v, "gates")
            chain(v.tensor_tensor_scan(rows[:, M, :], rows[:, C, :], rows[:, C, :], 0.0, ALU.max, ALU.max))
            v.scalar_tensor_tensor(rows[:, NM, :], rows[:, M, :], -1.0, rows[:, B, :], ALU.mult, ALU.subtract)\
                .then_inc(sem("nm"), 1)
            v.tensor_scalar(rows[:, M, :], rows[:, M, :], -1.0, None, ALU.mult).then_inc(sem("negm"), 1)
            for j in range(4):
                bank = banks.take(v, ("qk", j))
                for i in range(4):
                    for c in (2 * j, 2 * j + 1):
                        o = (c % 2) * S
                        w = prm1[:, 24 + 8 * (3 - i) + c:25 + 8 * (3 - i) + c]
                        if i == 0:
                            last = v.tensor_scalar(qkT[:, c, :], bank[:, o:o + S], w, None, ALU.mult)
                        else:
                            last = v.scalar_tensor_tensor(qkT[:, c, i:], bank[:, o:o + S - i], w, qkT[:, c, i:],
                                                          ALU.mult, ALU.add)
                        if i < 3:
                            chain.mark(last)
                    if i < 3:
                        chain.wait()
                banks.release(last, ("qk", j))
            bank = banks.take(v, "cols")
            last = v.tensor_copy(ccol[:, :], bank[:, 0:16])
            banks.release(last, "cols")
            banks.moved(v, "cols")
            for h in range(NH):
                if h % 2 == 0:
                    bank = banks.take(v, ("mb", h // 2))
                for t in range(NT):
                    o = (h % 2) * S
                    last = v.tensor_scalar(DT[:, t, h, t * P:], bank[:, o + t * P:o + S],
                                           ccol[:, 4 * t + h:4 * t + h + 1], 0.0, ALU.add, ALU.min)
                if h % 2:
                    banks.release(last, ("mb", h // 2))
            for j in (2, 3):
                v.wait_ge(sem("qk_silu"), j + 1)
                v.tensor_scalar(qkT[:, 2 * j:2 * j + 2, :], qkT[:, 2 * j:2 * j + 2, :], float(P) ** -0.5, None,
                                ALU.mult).then_inc(sem("k_scaled"), 1)
            for t in range(NT):
                bank = banks.take(v, ("v", t))
                last = v.tensor_copy(vext[:, t, :, 0:P], bank.rearrange("p (h d) -> p h d", h=NH))
                banks.release(last, ("v", t))
            v.wait_ge(sem("decay_masked"), NT)
            for h in range(NH):
                bank = banks.take(v, ("sc", h))
                v.tensor_tensor(DT[:, 0, h, :], bank[:, 0:S], DT[:, 0, h, :], ALU.mult)
                last = v.tensor_tensor(DT[:, 1, h, P:], bank[:, S:S + P], DT[:, 1, h, P:], ALU.mult)
                banks.release(last, ("sc", h))
            for j in range(NT):
                for hp in range(2):
                    bank = banks.take(v, ("num", j, hp))
                    pair = bank[:, 0:2 * (P + 1)].rearrange("p (h d) -> p h d", h=2)
                    dd = den[:, j, 2 * hp:2 * hp + 2]
                    em = ccol[:, 8 + 4 * j + 2 * hp:8 + 4 * j + 2 * hp + 2].unsqueeze(2)
                    chain(v.scalar_tensor_tensor(dd.unsqueeze(2), pair[:, :, P:P + 1], -1.0, em, ALU.mult, ALU.max))
                    chain(v.tensor_tensor(dd.unsqueeze(2), pair[:, :, P:P + 1], dd.unsqueeze(2), ALU.max))
                    chain(v.reciprocal(dd, dd))
                    for h in range(2):
                        last = v.tensor_scalar(hm[:, j, 2 * hp + h, :], pair[:, h, 0:P],
                                               den[:, j, 2 * hp + h:2 * hp + h + 1], None, ALU.mult)
                    banks.release(last, ("num", j, hp))
                    banks.moved(v, ("num", j, hp))
                    for h in range(2):
                        n = j * NH + 2 * hp + h
                        chain.mark(v.bn_stats(bst[:, n, :], hm[:, j, 2 * hp + h, :]))
            chain.wait()
            for n in range(NT * NH):
                chain.mark(v.bn_aggr(mv[:, n, :], bst[:, n, :]))
            chain.wait()
            v.tensor_scalar(rs[:, :].unsqueeze(2), mv[:, :, 1:2], EPS1, None, ALU.add).then_inc(sem("hvar"), 1)
            v.wait_ge(sem("hroot"), 1)
            chain(v.reciprocal(rs[:, :], rs[:, :]))
            for n in range(NT * NH):
                v1 = hm[:, n // NH, n % NH, :]
                chain.mark(v.tensor_scalar(v1, v1, mv[:, n, 0:1], rs[:, n:n + 1], ALU.subtract, ALU.mult))
            chain.wait()
            for t in range(NT):
                banks.moved(v, ("o", t))
                v.tensor_tensor(og[:, t, :], og[:, t, :], hm[:, t, :, :].rearrange("p h d -> p (h d)"), ALU.mult)\
                    .then_inc(sem("ym"), 1)
            bank = banks.take(v, "prm2")
            last = v.tensor_copy(prm2[:, 0:113], bank[:, 0:113])
            banks.release(last, "prm2")
            for j in range(2):
                bank = banks.take(v, ("ym", j))
                last = v.tensor_tensor(yT[:, 2 * j:2 * j + 2, :], bank.rearrange("p (c t) -> p c t", c=2),
                                       bcast(prm1[:, 16 + 2 * j:18 + 2 * j], S), ALU.mult)
                banks.release(last, ("ym", j))
            for n in range(2):
                for t in range(NT):
                    bank = banks.take(v, ("out", n, t))
                    xs = x[:, t, n * 512:(n + 1) * 512]
                    last = v.tensor_tensor(xs, xs, bank, ALU.add)
                    banks.release(last, ("out", n, t))
            k.scale(v, chain, "n2", 1, EPS1)
            k.evacuate(v, banks, "n2", prm1[:, 8:16])
            v.wait_ge(sem("wr_in"), 32)
            bank = banks.take(v, "lg")
            last = v.tensor_tensor(lg[:, :, :], bank[:, 0:NT * NE].rearrange("p (t e) -> p t e", t=NT),
                                   brt[:, :].unsqueeze(1).to_broadcast([P, NT, NE]), ALU.add)
            banks.release(last, "lg")
            banks.moved(v, "lg")
            for t in range(NT):
                chain.mark(v.max(v8[:, t, :], lg[:, t, :]))
            chain.wait()
            for t in range(NT):
                chain.mark(v.max_index(i8[:, t, :], v8[:, t, :], lg[:, t, :]))
            chain.wait()
            chain(v.tensor_copy(f8[:, :, :], i8[:, :, :]))
            v.tensor_scalar(f8[:, :, 7:8], v8[:, :, 0:1], -1.0, None, ALU.mult).then_inc(sem("v8neg"), 1)
            v.wait_ge(sem("e4"), NT)
            chain(v.reciprocal(es[:, :], es[:, :]))
            chain(v.tensor_tensor(e4[:, :, :], e4[:, :, :], bcast(es[:, :], TOPK), ALU.mult))
            for q in range(TOPK):
                for t in range(NT):
                    i = f8[:, t, q:q + 1]
                    if q == 0:
                        chain.mark(v.tensor_scalar(mask[:, t, :], iota_e[:, :], i, None, ALU.is_equal))
                        chain.mark(v.tensor_scalar(gate[:, t, :], iota_e[:, :], i, e4[:, t, q:q + 1],
                                                   ALU.is_equal, ALU.mult))
                    else:
                        chain.mark(v.scalar_tensor_tensor(mask[:, t, :], iota_e[:, :], i, mask[:, t, :],
                                                          ALU.is_equal, ALU.add))
                        chain(v.tensor_scalar(tmp[:, t, :], iota_e[:, :], i, e4[:, t, q:q + 1],
                                              ALU.is_equal, ALU.mult))
                        chain.mark(v.tensor_tensor(gate[:, t, :], gate[:, t, :], tmp[:, t, :], ALU.add))
                chain.wait()
            v.tensor_copy(tmp[:, :, :], mask[:, :, :]).then_inc(sem("mask"), 1)
            bank = banks.take(v, "rk")
            rk = bank[:, 0:NT * NE].rearrange("p (t e) -> p t e", t=NT)
            chain.mark(v.scalar_tensor_tensor(slot[:, :, :], rk, 1.0, mask[:, :, :], ALU.add, ALU.mult))
            last = v.tensor_copy(cnt[:, :], bank[0:1, 256:256 + NE])
            banks.release(last, "rk")
            banks.moved(v, "rk")
            chain.mark(v.tensor_scalar(slot[:, :, :], slot[:, :, :], -1.0, None, ALU.add))
            chain(v.reduce_max(cm[:, 0:1], cnt[:, :], AX.X))
            chain.mark(v.tensor_scalar(cm[:, 2:3], cm[:, 0:1], 2.0 * CAP, 1.0, ALU.is_gt, ALU.add))
            chain(v.tensor_scalar(cm[:, 1:2], cm[:, 0:1], 1.0 * CAP, None, ALU.is_gt))
            chain(v.tensor_tensor(cm[:, 1:2], cm[:, 1:2], cm[:, 2:3], ALU.add))
            chain(v.tensor_scalar(cm[:, 3:4], cm[:, 0:1], 3.0 * CAP, None, ALU.is_gt))
            v.tensor_tensor(passes[:, :], cm[:, 1:2], cm[:, 3:4], ALU.add).then_inc(sem("passes"), 1)
            bank = banks.take(v, "gt")
            last = v.tensor_copy(gT[:, :, :], bank[0:NE, 0:S].rearrange("p (t n) -> p t n", t=NT))
            banks.release(last, "gt")
            for t in range(NT):
                for n in range(2):
                    bank = banks.take(v, ("bd", t, n))
                    xs = x[:, t, n * 512:(n + 1) * 512]
                    last = v.tensor_tensor(xs, xs, bank, ALU.add)
                    banks.release(last, ("bd", t, n))

        @block.tensor
        def _(pe):
            pe.wait_ge(sem("consts"), 4)
            pe.wait_ge(sem("prow1_in"), 16 * 8)
            bank = banks.claim(pe, "prm1")
            banks.filled(pe.transpose(bank[:, 0:56], prow1[0:56, :], ident[0:56, 0:56]), "prm1")
            k.transposes(pe, banks, "n1")
            pe.wait_ge(sem("wg_in"), 16)
            for j in range(4):
                banks.moved(pe, ("n1", j))
            bank = banks.claim(pe, "gates")
            for n in range(2):
                for c in range(KC):
                    last = pe.matmul(bank[0:4, n * S:(n + 1) * S], wg[:, c, 4 * n:4 * n + 4], hT[:, c, :],
                                     start=c == 0, stop=c == KC - 1)
            banks.filled(last, "gates")

            def feature_major(g, key, m):
                bank = banks.claim(pe, key)
                for i in range(2):
                    for c in range(KC):
                        last = pe.matmul(bank[:, i * S:(i + 1) * S], piece(g)[:, c, (m + i) * P:(m + i + 1) * P],
                                         hT[:, c, :], start=c == 0, stop=c == KC - 1)
                banks.filled(last, key)
                return last

            def token_major(g, key, t):
                bank = banks.claim(pe, key)
                for c in range(KC):
                    last = pe.matmul(bank, hT[:, c, t * P:(t + 1) * P], piece(g)[:, c, :],
                                     start=c == 0, stop=c == KC - 1)
                banks.filled(last, key)
                return last

            for g in (Q_, K_):
                ring.landed(pe, g)
                for m in (0, 2):
                    last = feature_major(g, ("qk", 2 * (g - Q_) + m // 2), m)
            pe.wait_ge(sem("em"), 1)
            pe.wait_ge(sem("negm"), 1)
            bank = banks.claim(pe, "cols")
            for n, r in enumerate((C, EM)):
                for t in range(NT):
                    o = 8 * n + 4 * t
                    last = pe.transpose(bank[:, o:o + 4], rows[:, r, t * P:(t + 1) * P], ident[0:4, 0:4])
            banks.filled(last, "cols")
            for h in range(NH):
                if h % 2 == 0:
                    bank = banks.claim(pe, ("mb", h // 2))
                last = pe.matmul(bank[:, (h % 2) * S:(h % 2 + 1) * S], sel[0:4, h, :], rows[:, M, :],
                                 start=True, stop=True)
                if h % 2:
                    banks.filled(last, ("mb", h // 2))
            ring.landed(pe, V_)
            for t in range(NT):
                last = token_major(V_, ("v", t), t)
            pe.wait_ge(sem("qk_silu"), 4)
            pe.wait_ge(sem("k_scaled"), 2)
            for h in range(NH):
                bank = banks.claim(pe, ("sc", h))
                pe.matmul(bank[:, 0:S], qkT[:, 4 + h, 0:P], qkT[:, h, :], start=True, stop=True)
                last = pe.matmul(bank[:, S:S + P], qkT[:, 4 + h, P:S], qkT[:, h, P:S], start=True, stop=True)
                banks.filled(last, ("sc", h))
            ring.landed(pe, O_)
            for t in range(NT):
                last = token_major(O_, ("o", t), t)
            ring.landed(pe, U_)
            for m in (0, 2):
                last = feature_major(U_, ("u", m // 2), m)
            for t in range(NT):
                banks.moved(pe, ("v", t))
            for h in range(NH):
                banks.moved(pe, ("sc", h))
            for j in range(NT):
                for hp in range(2):
                    bank = banks.claim(pe, ("num", j, hp))
                    for h in (2 * hp, 2 * hp + 1):
                        for i in range(j + 1):
                            o = (h % 2) * (P + 1)
                            last = pe.matmul(bank[:, o:o + P + 1], DT[:, i, h, j * P:(j + 1) * P], vext[:, i, h, :],
                                             start=i == 0, stop=i == j)
                    banks.filled(last, ("num", j, hp))
            pe.wait_ge(sem("prow2_in"), 16 * 7)
            bank = banks.claim(pe, "prm2")
            banks.filled(pe.transpose(bank[:, 0:113], prow2[0:113, :], ident[0:113, 0:113]), "prm2")
            pe.wait_ge(sem("pool_w_in"), 16)
            pe.wait_ge(sem("pooled"), 1)
            for g in range(4):
                if g % 2 == 0:
                    bank = banks.claim(pe, ("pool", g // 2))
                last = pe.matmul(bank[:, (g % 2) * S:(g % 2 + 1) * S], pool_w[:, g, :], inv[:, g, :],
                                 start=True, stop=True)
                if g % 2:
                    banks.filled(last, ("pool", g // 2))
            pe.wait_ge(sem("ym"), NT)
            for j in range(2):
                bank = banks.claim(pe, ("ym", j))
                for i in range(2):
                    for t in range(NT):
                        c = 2 * j + i
                        last = pe.transpose(bank[:, i * S + t * P:i * S + (t + 1) * P], og[:, t, c * P:(c + 1) * P],
                                            ident[:, :])
                banks.filled(last, ("ym", j))
            for j in range(2):
                banks.moved(pe, ("ym", j))
                banks.moved(pe, ("pool", j))
            for n in range(2):
                ring.landed(pe, OUT0 + n)
                for t in range(NT):
                    bank = banks.claim(pe, ("out", n, t))
                    for c in range(KC):
                        last = pe.matmul(bank, yT[:, c, t * P:(t + 1) * P], piece(OUT0 + n)[:, c, :],
                                         start=c == 0, stop=c == KC - 1)
                    banks.filled(last, ("out", n, t))
            k.transposes(pe, banks, "n2")
            for j in range(4):
                banks.moved(pe, ("n2", j))
            pe.wait_ge(sem("wr_in"), 32)
            bank = banks.claim(pe, "lg")
            for t in range(NT):
                for c in range(KC):
                    last = pe.matmul(bank[:, t * NE:(t + 1) * NE], hT[:, c, t * P:(t + 1) * P], wr[:, c, :],
                                     start=c == 0, stop=c == KC - 1)
            banks.filled(last, "lg")
            pe.wait_ge(sem("mask"), 1)
            bank = banks.claim(pe, "rk")
            pe.matmul(bank[:, 0:NE], ustrict[:, :], tmp[:, 0, :], start=True, stop=True)
            pe.matmul(bank[:, NE:2 * NE], ones[:, 0:P], tmp[:, 0, :], start=True, stop=False)
            pe.matmul(bank[:, NE:2 * NE], ustrict[:, :], tmp[:, 1, :], start=False, stop=True)
            pe.matmul(bank[0:1, 256:256 + NE], ones[:, 0:1], tmp[:, 0, :], start=True, stop=False)
            last = pe.matmul(bank[0:1, 256:256 + NE], ones[:, 0:1], tmp[:, 1, :], start=False, stop=True)
            banks.filled(last, "rk")
            bank = banks.claim(pe, "gt")
            for t in range(NT):
                last = pe.transpose(bank[0:NE, t * P:(t + 1) * P], gate[:, t, :], ident[:, :])
            banks.filled(last, "gt")
            pe.wait_ge(sem("bdn_in"), 16)
            banks.moved(pe, "gt")
            for t in range(NT):
                for n in range(2):
                    bank = banks.claim(pe, ("bd", t, n))
                    last = pe.matmul(bank, gT[:, t, :], bdn[:, n * 512:(n + 1) * 512], start=True, stop=True)
                    banks.filled(last, ("bd", t, n))


def phase_b(nc, A, sem, sb, ring, banks, env):
    x, xn, ident, prm1, slot, gate, iota_cap, passes, brow = (
        env[n] for n in "x xn ident prm1 slot gate iota_cap passes brow".split())
    ones_row = sb("ones_row", [1, CAP])
    pass0 = sb("pass0", [P, S // CAP + 1])
    pick = sb("pick", [P, NT, CAP])
    gpick = sb("gpick", [P, NT, 2, CAP])
    gpickT = sb("gpickT", [P, NT, P])
    xg = sb("xg", [P, KC, CAP])
    gt = sb("gt", [P, 512])
    sg = sb("sg", [P, 512])
    up = sb("up", [P, 512])
    aT = sb("aT", [P, 4, 2, CAP])
    y = sb("y", [P, 512])
    G_, T_, GATE, UP, AT, DN, SC0, SC1 = range(8)
    uses = [1, 1, 1, 1, 1, 1, 2, 2]
    first = list(banks.uses)

    def bank_claim(pe, b, i, nth=0):
        pe.wait_ge(banks.free[b], first[b] + uses[b] * i + nth)
        return banks.ps[:, b, :]

    def bank_take(eng, b, i, nth=0):
        eng.wait_ge(banks.full[b], first[b] + uses[b] * i + nth + 1)
        return banks.ps[:, b, :]

    def bank_moved(eng, b, i):
        eng.wait_ge(banks.free[b], first[b] + uses[b] * (i + 1))

    def bank_done(eng, b, i):
        eng.wait_ge(banks.full[b], first[b] + uses[b] * i)

    def passes_of(eng):
        eng.wait_ge(sem("passes"), 1)
        return eng.value_load(passes[0:1, 0:1], min_val=1, max_val=S // CAP)

    with nc.Block() as block:
        @block.sync
        def _(sp):
            steps = sp.snap(passes_of(sp) * NE)
            with sp.Fori(1, steps) as i:
                e = sp.snap(i % NE)
                sp.wait_ge(sem("bias_used"), i)
                load_biases(sp, A, brow, sem, e)
                for m, b in enumerate((GATE, UP, DN)):
                    sp.wait_ge(sem(f"first_half_used{m}"), i)
                    load_half(sp, A, ring, m, 0, e)
                    bank_done(sp, b, i)
                    load_half(sp, A, ring, m, 1, e)
            for g in range(5):
                m, h = divmod(g, 2)
                if h == 0:
                    sp.wait_ge(sem(f"first_half_used{m}"), steps)
                else:
                    bank_done(sp, (GATE, UP)[m], steps)
                load_c(sp, A, env["ringC"], g)

        @block.vector
        def _(v):
            for p in range(S // CAP + 1):
                v.memset(pass0[:, p:p + 1], -float(p * CAP)).then_inc(sem("pass0"), 1)
            v.memset(ones_row[:, :], 1.0).then_inc(sem("ones_row"), 1)
            v.memset(y[:, :], 0.0).then_inc(sem("zeroed"), 1)
            v.memset(gpickT[:, :, :], 0.0).then_inc(sem("zeroed"), 1)
            v.wait_ge(sem("pass0"), S // CAP + 1)
            steps = v.snap(passes_of(v) * NE)

            def picks(e, p):
                for t in range(NT):
                    v.tensor_scalar(pick[:, t, :], iota_cap[:, 0, :], slot[:, t, bass.ds(e, 1)],
                                    pass0[:, bass.ds(p, 1)], ALU.subtract, ALU.is_equal).then_inc(sem("picks"), 1)

            def gathered(i):
                bank = bank_take(v, G_, i)
                v.tensor_tensor(xg[:, :, :], bank.rearrange("p (c j) -> p c j", c=KC), bcast(prm1[:, 8:16], CAP),
                                ALU.mult).then_inc(banks.free[G_], 1)

            def summed(i):
                for t in range(NT):
                    for h in range(2):
                        bank = bank_take(v, SC0 + h, i, t)
                        xs = x[:, t, h * 512:(h + 1) * 512]
                        v.tensor_tensor(xs, xs, bank, ALU.add).then_inc(banks.free[SC0 + h], 1)

            for t in range(NT):
                v.tensor_scalar(pick[:, t, :], iota_cap[:, 0, :], slot[:, t, 0:1], None, ALU.is_equal)\
                    .then_inc(sem("picks"), 1)
            gathered(0)
            with v.Fori(0, steps) as i:
                e = v.snap(i % NE)
                bank_done(v, T_, i)
                v.wait_ge(sem("picks"), NT * i + NT)
                for t in range(NT):
                    v.tensor_scalar(gpick[:, t, :, :], pick[:, t, :].unsqueeze(1).to_broadcast([P, 2, CAP]),
                                    gate[:, t, bass.ds(e, 1)], None, ALU.mult).then_inc(sem("gpicks"), 1)
                bank_done(v, G_, i + 1)
                v.wait_ge(sem("gpicks"), NT * i + NT)
                nxt = v.snap(i + 1)
                picks(v.snap(nxt % NE), v.snap(nxt // NE))
                bank = bank_take(v, GATE, i)
                v.tensor_scalar(gt[:, :], bank, 7.0, None, ALU.min).then_inc(banks.free[GATE], 1)
                v.wait_ge(sem("sig"), i + 1)
                v.tensor_tensor(gt[:, :], gt[:, :], sg[:, :], ALU.mult).then_inc(sem("glu"), 1)
                bank = bank_take(v, UP, i)
                v.tensor_scalar(up[:, :], bank, 7.0, -7.0, ALU.min, ALU.max).then_inc(banks.free[UP], 1)
                v.wait_ge(sem("glu"), i + 1)
                bank_moved(v, UP, i)
                v.scalar_tensor_tensor(gt[:, :], up[:, :], 1.0, gt[:, :], ALU.add, ALU.mult).then_inc(sem("acted"), 1)
                summed(i)
                bank = bank_take(v, AT, i)
                v.tensor_copy(aT[:, :, :, :], bank.rearrange("p (c h j) -> p c h j", c=4, h=2))\
                    .then_inc(banks.free[AT], 1)
                gathered(nxt)
            summed(steps)

        @block.scalar
        def _(act):
            act.dma_start(env["gain"][:, :], A["normf_g"].unsqueeze(0).to_broadcast([P, D]))\
                .then_inc(sem("normf_in"), 16)
            steps = act.snap(passes_of(act) * NE)
            with act.Fori(0, steps) as i:
                bank_moved(act, GATE, i)
                act.activation(sg[:, :], gt[:, :], ACT.Sigmoid, scale=1.702).then_inc(sem("sig"), 1)
                bank_done(act, SC1, i + 1)
                bank = bank_take(act, T_, i)
                act.copy(gpickT[:, :, :], bank[:, 0:NT * P].rearrange("p (t n) -> p t n", t=NT))\
                    .then_inc(banks.free[T_], 1)
                bank = bank_take(act, DN, i)
                act.copy(y[:, :], bank).then_inc(banks.free[DN], 1)

        @block.tensor
        def _(pe):
            steps = pe.snap(passes_of(pe) * NE)

            def gather(i):
                pe.wait_ge(sem("picks"), NT * i + NT)
                bank = bank_claim(pe, G_, i)
                for c in range(KC):
                    for t in range(NT):
                        last = pe.matmul(bank[:, c * CAP:(c + 1) * CAP], xn[:, t, c * P:(c + 1) * P],
                                         pick[:, t, :], start=t == 0, stop=t == NT - 1)
                last.then_inc(banks.full[G_], 1)

            def scatter_before(i):
                pe.wait_ge(banks.free[T_], first[T_] + i)
                pe.wait_ge(banks.free[DN], first[DN] + i)
                for t in range(NT):
                    for h in range(2):
                        bank = bank_claim(pe, SC0 + h, i, t)
                        pe.matmul(bank, gpickT[h * CAP:(h + 1) * CAP, t, :], y[h * CAP:(h + 1) * CAP, :],
                                  start=True, stop=True).then_inc(banks.full[SC0 + h], 1)

            pe.wait_ge(sem("ones_row"), 1)
            pe.wait_ge(sem("zeroed"), 2)
            gather(0)
            with pe.Fori(0, steps) as i:
                bank_moved(pe, G_, i)
                pe.wait_ge(sem("brow_in"), 32 * i + 32)
                for m, b in ((0, GATE), (1, UP)):
                    bank = bank_claim(pe, b, i)
                    for h in range(2):
                        last = pe.matmul(bank[h * CAP:(h + 1) * CAP, :], ones_row[:, :],
                                         brow[0:1, m, h * 512:(h + 1) * 512], start=True, stop=False)
                    if m == 1:
                        last.then_inc(sem("bias_used"), 1)
                    for kh in range(2):
                        g = EXPERT + 2 * m + kh
                        pe.wait_ge(ring.loaded[g % SLOTS], 16 * ring.nth(g) + 16 + 16 * i)
                        w = ring.slot(g).rearrange("p (c n) -> p c n", c=4)
                        for c in range(4):
                            for h in range(2):
                                last = pe.matmul(bank[h * CAP:(h + 1) * CAP, :], xg[:, 4 * kh + c, :],
                                                 w[:, c, h * 512:(h + 1) * 512], start=False,
                                                 stop=kh == 1 and c == 3)
                        if kh == 0:
                            last.then_inc(sem(f"first_half_used{m}"), 1)
                    last.then_inc(banks.full[b], 1)
                scatter_before(i)
                pe.wait_ge(sem("gpicks"), NT * i + NT)
                bank = bank_claim(pe, T_, i)
                for t in range(NT):
                    last = pe.transpose(bank[:, t * P:(t + 1) * P], gpick[:, t, :, :].rearrange("p a j -> p (a j)"),
                                        ident[:, :])
                last.then_inc(banks.full[T_], 1)
                pe.wait_ge(sem("acted"), i + 1)
                bank = bank_claim(pe, AT, i)
                for c in range(4):
                    last = pe.transpose(bank[:, c * P:(c + 1) * P], gt[:, c * P:(c + 1) * P], ident[:, :])
                last.then_inc(banks.full[AT], 1)
                gather(pe.snap(i + 1))
                bank_moved(pe, AT, i)
                bank = bank_claim(pe, DN, i)
                for kh in range(2):
                    g = EXPERT + 4 + kh
                    pe.wait_ge(ring.loaded[g % SLOTS], 16 * ring.nth(g) + 16 + 16 * i)
                    w = ring.slot(g).rearrange("p (c n) -> p c n", c=4)
                    for c in range(4):
                        for h in range(2):
                            last = pe.matmul(bank[h * CAP:(h + 1) * CAP, :], aT[:, c, kh, :],
                                             w[:, c, h * 512:(h + 1) * 512], start=kh == 0 and c == 0,
                                             stop=kh == 1 and c == 3)
                    if kh == 0:
                        last.then_inc(sem("first_half_used2"), 1)
                last.then_inc(banks.full[DN], 1)
            scatter_before(steps)


HG = 4
LEVELS = 7
FQ, FK, FV, FF, GQ, GK, GV, GA, GZ, GATE_F, GATE_G = (
    0, 1024, 2048, 3072, 3080, 4104, 5128, 6152, 6168, 7192, 8216)
PIECES_C = [("w_in_2", c + 512 * hg) for hg in range(2)
            for c in (GQ, GK, GV, FQ, FK, FV, GZ)]
PIECES_C += [p for n in range(2) for p in (
    ("w_in_2", GATE_F + 512 * n), ("w_branch_fox_2", 512 * n), ("w_in_2", GATE_G + 512 * n),
    ("w_branch_gdn_2", 512 * n))]
PIECES_C += [("w_out_2", 512 * n) for n in range(2)]
LAST_C = [(w, hg, 1) for hg in range(2) for w in ("gq", "gk", "gv", "fq", "fk", "fv", "gz")]
LAST_C += [(w, n, 1) for n in range(2) for w in ("gf", "bf", "gg", "bg")]
LAST_C += [("out", n, 1) for n in range(2)]


def load_c(sp, A, ring, g):
    name, c0 = PIECES_C[g]
    ring.load(sp, g, ring.slot(g).rearrange("p (c n) -> p c n", c=KC),
              A[name][0][:, c0:c0 + 512].rearrange("(c p) n -> p c n", p=P))


FF_CHUNKS = 22
NUP = FF_CHUNKS // 2
NDOWN = (FF_CHUNKS + 3) // 4
UP0 = len(PIECES_C)
DOWN0 = UP0 + NUP


def load_up(sp, A, ring, j):
    w = A["w_up_2"][0].rearrange("(c p) (h n) -> p c h n", p=P, h=2)
    dst = ring.slot(UP0 + j).rearrange("p (c h n) -> p c h n", c=KC, h=2)
    for h in range(2):
        ring.load(sp, UP0 + j, dst[:, :, h, :], w[:, :, h, j * 2 * P:(j + 1) * 2 * P])


def load_down(sp, A, ring, j):
    n = min(4, FF_CHUNKS - 4 * j)
    ring.load(sp, DOWN0 + j, ring.slot(DOWN0 + j).rearrange("p (c n) -> p c n", c=4)[:, 0:n, :],
              A["w_down_2"][0][4 * j * P:(4 * j + n) * P, :].rearrange("(c p) n -> p c n", p=P))


def phase_c(nc, A, sem, sb, ring, banks, k, env):
    x, xn, hT, ident, tri, ustrict, ones, sel, prm2, gain, spare = (
        env[n] for n in "x xn hT ident tri ustrict ones sel prm2 gain spare".split())
    wg2 = sb("wg2", [P, KC, 24])
    rb = sb("rb", [8, 3])
    rowp = sb("rowp", [8, 3, S])
    NEGC, GC, BETA = range(3)
    temp = xn[0:8, :, :].rearrange("p t (a s) -> p (t a) s", s=S)
    TA, TB, TC, TD, TE, BEG, KD, TF = range(8)
    cols = sb("cols", [P, 6, 8])
    lm = sb("lm", [P, LEVELS, P])
    gT = sb("gT2", [P, 3, HG, S])
    fqk = spare[:, 0:2 * HG * S].rearrange("p (a h s) -> p a h s", a=2, h=HG)
    fv = spare[:, 2048:3072].rearrange("p (t n) -> p t n", t=NT)
    gz = spare[:, 3072:4096].rearrange("p (t n) -> p t n", t=NT)
    X = sb("X", [P, NT, HG, P])
    XT = sb("XT", [P, NT, HG, P])
    work = sb("work", [P, 2, NT, HG * P])
    ATm, T1 = work[:, 0], work[:, 1]
    AT = xn[:, 0, :].rearrange("p (t h n) -> p t h n", t=NT, h=HG)
    attnT = xn[:, 1, :].rearrange("p (t h n) -> p t h n", t=NT, h=HG)
    sq = X[:, :, :, :].rearrange("p t h n -> p (t h n)").rearrange("p (b n) -> p b n", b=2)
    vb = sb("vb", [P, NT, HG, P])
    kbg = sb("kbg", [P, HG, P])
    kdec = sb("kdec", [P, HG, P])
    egb = sb("egb", [P, HG, P])
    u = gT[:, 2].rearrange("p h (t n) -> p t h n", t=NT)
    wTn = sb("wTn", [P, HG, P])
    state = sb("state", [P, HG, P])
    o = gT[:, 1].rearrange("p h (t n) -> p t h n", t=NT)
    osum = sb("osum", [P, NT, HG])
    prob = work[:, :, :, :].rearrange("p a t n -> p (a t n)")[:, 0:HG * 384].rearrange("p (h n) -> p h n", h=HG)
    probT = spare[:, 0:HG * 384].rearrange("p (h n) -> p h n", h=HG)
    negmask = sb("negmask", [P, P])
    fmax = sb("fmax", [P, HG, NT])
    fsum = sb("fsum", [P, HG, NT])
    yfT = sb("yfT", [P, KC, S])
    ygT = sb("ygT", [P, KC, S])
    mixT = gT[:, 0:2].rearrange("p a h s -> p (a h) s")
    sgf = work[:, 0].rearrange("p t n -> p t n")
    sgg = work[:, 1].rearrange("p t n -> p t n")

    banks.plan(*[("nm", j) for j in range(4)], ("rw", 0), ("rw", 1))
    for hg in range(2):
        banks.plan(("gq", hg, 0), ("gq", hg, 1), ("gk", hg, 0), ("gk", hg, 1), *([] if hg else ["cols"]),
                   ("gv", hg, 0), ("gv", hg, 1), *[("ss", hg, j) for j in range(4)],
                   ("fq", hg, 0), ("fq", hg, 1), *[("rb", hg, h) for h in range(HG)],
                   ("fk", hg, 0), ("fk", hg, 1), *[("kq", hg, h) for h in range(HG)],
                   *[(w, hg, t) for w in ("kt", "vt") for t in range(NT)],
                   *[("x1", hg, t) for t in range(NT)], ("fv", hg, 0), ("fv", hg, 1),
                   ("gz", hg, 0), ("gz", hg, 1))
        for l in range(1, LEVELS):
            banks.plan(*[("t1", hg, l, t) for t in range(NT)])
            for t in range(NT):
                banks.plan(*([("xx", hg, l, t)] if l < LEVELS - 1 else []), ("xt", hg, l, t))
        banks.plan(*[("lo", hg, h) for h in range(HG)], ("u0", hg), ("wT", hg), ("st", hg), ("o0", hg), ("u1", hg),
                   *[("pt", hg, h) for h in range(HG)], ("o1", hg), ("pv", hg, 0), ("pv", hg, 1),
                   ("oT", hg, 0), ("oT", hg, 1))
    for n in range(2):
        banks.plan(*[(w, n, j) for w in ("gf", "bf", "gg", "bg") for j in range(2)])
    banks.plan(*[("out", n, t) for n in range(2) for t in range(NT)])

    def piece(g):
        return ring.slot(g).rearrange("p (c n) -> p c n", c=KC)

    def heads(bank):
        return bank.rearrange("p (h n) -> p h n", h=HG)

    flat = hT[:, :, :].rearrange("p (t c) n -> p t (c n)", t=NT)

    with nc.Block() as block:
        @block.sync
        def _(sp):
            sp.dma_start(wg2[:, :, 0:8], A["w_in_2"][0][:, FF:FF + 8].rearrange("(c p) n -> p c n", p=P))\
                .then_inc(sem("wg2_in"), 16)
            sp.dma_start(wg2[:, :, 8:24], A["w_in_2"][0][:, GA:GA + 16].rearrange("(c p) n -> p c n", p=P))\
                .then_inc(sem("wg2_in"), 16)
            for i, name in enumerate(("fox_f_bias_2", "gdn_a_log_2", "gdn_dt_bias_2")):
                sp.dma_start(rb[:, i:i + 1], A[name].rearrange("a h -> h a")).then_inc(sem("rb_in"), 16)
            for g in range(5, UP0 + 5):
                banks.done(sp, LAST_C[g - 5])
                if g < UP0:
                    load_c(sp, A, ring, g)
                else:
                    load_up(sp, A, ring, g - UP0)

        @block.scalar
        def _(act):
            chain = Chain(act, sem("actC"))
            k.squares(act, "nf", 2, flat)
            k.root(act, "nf", 2)
            act.wait_ge(sem("nf_x"), NT)
            k.squares(act, "nm", 3, flat)
            k.root(act, "nm", 3)
            act.wait_ge(sem("rb_in"), 48)
            chain(act.activation(rb[:, 1:2], rb[:, 1:2], ACT.Exp))
            banks.moved(act, ("rw", 0))
            for a, b in ((TA, TC), (TB, TD)):
                chain(act.activation(temp[:, b, :], temp[:, a, :], ACT.Abs))
                chain(act.activation(temp[:, b, :], temp[:, b, :], ACT.Exp, scale=-1.0))
            for b in (TC, TD):
                act.activation(temp[:, b, :], temp[:, b, :], ACT.Ln, bias=1.0).then_inc(sem("rows_ln"), 1)
            bank = banks.take(act, ("rw", 1))
            banks.release(act.activation(rowp[:, BETA, :], bank[0:8, 0:S], ACT.Sigmoid), ("rw", 1))
            act.wait_ge(sem("gc_rows"), 2)
            act.activation(temp[:, BEG, P:S], rowp[:, GC, P:S], ACT.Exp).then_inc(sem("eg_rows"), 1)
            act.activation(temp[:, KD, 0:P], temp[:, KD, 0:P], ACT.Exp).then_inc(sem("eg_rows"), 1)

            for hg in range(2):
                for w in range(3):
                    for j in range(2):
                        banks.moved(act, (("gq", "gk", "gv")[w], hg, j))
                        part = gT[:, w, 2 * j:2 * j + 2, :]
                        act.activation(part, part, ACT.Silu).then_inc(sem("g_silu"), 1)
                for j in range(4):
                    act.wait_ge(sem("g_silu"), 6 * hg + 4)
                    if j >= 2:
                        banks.done(act, ("ss", hg, j - 2))
                    act.activation(sq[:, j % 2, :], gT[:, j // 2, 2 * (j % 2):2 * (j % 2) + 2, :].rearrange("p h s -> p (h s)"),
                                   ACT.Square).then_inc(sem("g_sq"), 1)
                for j in range(4):
                    act.wait_ge(sem("ss_eps"), 4 * hg + j + 1)
                    act.activation(work[:, j // 2, j % 2, :], work[:, j // 2, j % 2, :], ACT.Sqrt)\
                        .then_inc(sem("ss_root"), 1)
                for j in range(2):
                    bank = banks.take(act, ("fq", hg, j))
                    last = act.activation(fqk[:, 0, 2 * j:2 * j + 2, :], bank.rearrange("p (h s) -> p h s", h=2),
                                          ACT.Copy, scale=float(P) ** -0.5)
                    banks.release(last, ("fq", hg, j))
                for h in range(HG):
                    act.wait_ge(sem("dlog"), 4 * hg + h + 1)
                    act.activation(attnT[:, :, h, :], attnT[:, :, h, :], ACT.Exp).then_inc(sem("dexp"), 1)
                    bank = banks.take(act, ("rb", hg, h))
                    act.activation(egb[:, h, :], bank[:, P:S], ACT.Exp).then_inc(sem("egb"), 1)
                for j in range(2):
                    bank = banks.take(act, ("fk", hg, j))
                    last = act.copy(fqk[:, 1, 2 * j:2 * j + 2, :], bank.rearrange("p (h s) -> p h s", h=2))
                    banks.release(last, ("fk", hg, j))
                for t in range(NT):
                    bank = banks.take(act, ("x1", hg, t))
                    banks.release(act.copy(X[:, t], heads(bank)), ("x1", hg, t))
                for t in range(NT):
                    bank = banks.take(act, ("fv", hg, t))
                    banks.release(act.copy(fv[:, t, :], bank), ("fv", hg, t))
                for t in range(NT):
                    bank = banks.take(act, ("gz", hg, t))
                    banks.release(act.activation(gz[:, t, :], bank, ACT.Silu), ("gz", hg, t))
                for l in range(1, LEVELS):
                    for t in range(NT):
                        bank = banks.take(act, ("t1", hg, l, t))
                        banks.release(act.copy(T1[:, t, :], bank), ("t1", hg, l, t))
                for h in range(HG):
                    act.wait_ge(sem("fmax"), 4 * hg + h + 1)
                    bank = banks.take(act, ("lo", hg, h))
                    act.activation(prob[:, h, 0:P], bank[:, 0:P], ACT.Exp, bias=fmax[:, h, 0:1],
                                   accum_out=fsum[:, h, 0:1])
                    last = act.activation(prob[:, h, P:384], bank[:, P:384], ACT.Exp, bias=fmax[:, h, 1:2],
                                          accum_out=fsum[:, h, 1:2])
                    banks.release(last, ("lo", hg, h))
                bank = banks.take(act, ("u0", hg))
                banks.release(act.copy(u[:, 0], heads(bank)), ("u0", hg))
                bank = banks.take(act, ("wT", hg))
                banks.release(act.activation(wTn[:, :, :], heads(bank), ACT.Copy, scale=-1.0), ("wT", hg))
                bank = banks.take(act, ("st", hg))
                banks.release(act.copy(state[:, :, :], heads(bank)), ("st", hg))
                bank = banks.take(act, ("u1", hg))
                banks.release(act.copy(u[:, 1], heads(bank)), ("u1", hg))
                for h in range(HG):
                    bank = banks.take(act, ("pt", hg, h))
                    banks.release(act.copy(probT[:, h, :], bank[:, 0:384]), ("pt", hg, h))
                for j in range(2):
                    bank = banks.take(act, ("pv", hg, j))
                    last = act.copy(yfT[:, HG * hg + 2 * j:HG * hg + 2 * j + 2, :], bank.rearrange("p (h s) -> p h s", h=2))
                    banks.release(last, ("pv", hg, j))
                act.wait_ge(sem("o_mean"), hg + 1)
                act.activation(osum[:, :, :], osum[:, :, :], ACT.Sqrt).then_inc(sem("o_root"), 1)
            for n in range(2):
                for w, buf in (("gf", sgf), ("gg", sgg)):
                    for j in range(2):
                        bank = banks.take(act, (w, n, j))
                        if n and w == "gf":
                            banks.moved(act, ("bf", 0, j))
                        if n and w == "gg":
                            act.wait_ge(sem("mixed"), j + 1)
                        banks.release(act.activation(buf[:, j, :], bank, ACT.Sigmoid), (w, n, j))

        @block.gpsimd
        def _(g):
            chain = Chain(g, sem("poolC"))
            chain(g.memset(lm[:, :, :], 0.0))
            for l in range(LEVELS):
                b = 1 << l
                odd = lm[:, l, :].rearrange("p (m o r) -> p m o r", o=2, r=b)[:, :, 1, :]
                m = P // (2 * b)
                chain(g.memset(odd, -1.0))
                chain(g.affine_select(out=odd, in_=odd, compare_op=ALU.is_ge, fill=0.0, base=0,
                                      pattern=[[-2 * b, m], [0, b]], channel_multiplier=1))
                chain(g.affine_select(out=odd, in_=odd, compare_op=ALU.is_ge, fill=0.0, base=b - 1,
                                      pattern=[[2 * b, m], [0, b]], channel_multiplier=-1))
            chain(g.memset(negmask[:, :], 0.0))
            g.affine_select(out=negmask[:, :], in_=negmask[:, :], compare_op=ALU.is_ge, fill=-1e30, base=0,
                            pattern=[[-1, P]], channel_multiplier=1).then_inc(sem("consts2"), 1)
            for hg in range(2):
                for h in range(HG):
                    g.wait_ge(sem("dexp"), 4 * hg + h + 1)
                    g.tensor_tensor(AT[:, :, h, :], attnT[:, :, h, :],
                                    ustrict[:, :].unsqueeze(1).to_broadcast([P, NT, P]), ALU.mult)\
                        .then_inc(sem("dstrict"), 1)
                    g.tensor_tensor(attnT[:, :, h, :], attnT[:, :, h, :],
                                    tri[:, :].unsqueeze(1).to_broadcast([P, NT, P]), ALU.mult)\
                        .then_inc(sem("dincl"), 1)
                g.wait_ge(sem("kk"), 4 * hg + 4)
                for l in range(LEVELS):
                    for t in range(NT):
                        if l > 1:
                            banks.done(g, ("t1", hg, l - 1, t))
                        if l == 1:
                            g.wait_ge(sem("x1T"), NT * hg + t + 1)
                        g.tensor_tensor(heads(ATm[:, t, :]), AT[:, t], lm[:, l, :].unsqueeze(1).to_broadcast([P, HG, P]),
                                        ALU.mult).then_inc(sem("ATm"), 1)

        @block.vector
        def _(v):
            chain = Chain(v, sem("dveC"))
            v.wait_ge(sem("normf_in"), 16)
            k.gained(v, chain, "nf", 2, EPS1, gain[:, :])
            k.scale(v, chain, "nm", 3, EPS2)
            k.evacuate(v, banks, "nm", prm2[:, 0:8])
            v.wait_ge(sem("rb_in"), 48)
            bank = banks.take(v, ("rw", 0))
            v.tensor_scalar(temp[:, TA, :], bank[0:8, 0:S], rb[:, 0:1], None, ALU.add)
            last = v.tensor_scalar(temp[:, TB, :], bank[0:8, S:2 * S], rb[:, 2:3], None, ALU.add)
            banks.release(last, ("rw", 0))
            v.wait_ge(sem("rows_ln"), 2)
            chain.mark(v.scalar_tensor_tensor(temp[:, TE, :], temp[:, TA, :], 0.0, temp[:, TC, :], ALU.min, ALU.subtract))
            chain(v.scalar_tensor_tensor(temp[:, TF, :], temp[:, TB, :], 0.0, temp[:, TD, :], ALU.max, ALU.add))
            chain(v.tensor_scalar(temp[:, TF, :], temp[:, TF, :], rb[:, 1:2], -1.0, ALU.mult, ALU.mult))
            chain(v.tensor_tensor_scan(temp[:, TA, :], ones[0:8, :], temp[:, TE, :], 0.0, ALU.mult, ALU.add))
            v.tensor_scalar(rowp[:, NEGC, :], temp[:, TA, :], -1.0, None, ALU.mult).then_inc(sem("negc"), 1)
            for t in range(NT):
                chain(v.tensor_tensor_scan(rowp[:, GC, t * P:(t + 1) * P], ones[0:8, 0:P],
                                           temp[:, TF, t * P:(t + 1) * P], 0.0, ALU.mult, ALU.add))
            v.tensor_scalar(temp[:, KD, 0:P], rowp[:, GC, 0:P], -1.0, rowp[:, GC, P - 1:P], ALU.mult, ALU.add)\
                .then_inc(sem("gc_rows"), 1)
            v.tensor_copy(temp[:, TC, 0:P], rowp[:, GC, 0:P]).then_inc(sem("gc_rows"), 1)
            v.wait_ge(sem("eg_rows"), 2)
            banks.moved(v, ("rw", 1))
            v.tensor_tensor(temp[:, BEG, P:S], temp[:, BEG, P:S], rowp[:, BETA, P:S], ALU.mult).then_inc(sem("beg"), 1)

            def conv(w, name, hg):
                for j in range(2):
                    bank = banks.take(v, (name, hg, j))
                    for i in range(4):
                        for a in range(2):
                            ch = 8 * w + HG * hg + 2 * j + a
                            c = gT[:, w, 2 * j + a, :]
                            tap = prm2[:, 17 + 24 * (3 - i) + ch:18 + 24 * (3 - i) + ch]
                            if i == 0:
                                last = v.tensor_scalar(c, bank[:, a * S:(a + 1) * S], tap, None, ALU.mult)
                            else:
                                last = v.scalar_tensor_tensor(c[:, i:], bank[:, a * S:(a + 1) * S - i], tap, c[:, i:],
                                                              ALU.mult, ALU.add)
                            if i < 3:
                                chain.mark(last)
                        if i < 3:
                            chain.wait()
                    banks.release(last, (name, hg, j))

            for hg in range(2):
                if hg:
                    for j in range(2):
                        banks.done(v, ("oT", 0, j))
                conv(0, "gq", hg)
                conv(1, "gk", hg)
                if hg == 0:
                    bank = banks.take(v, "cols")
                    last = v.tensor_copy(cols[:, :, :], bank[:, 0:48].rearrange("p (a h) -> p a h", a=6))
                    banks.release(last, "cols")
                conv(2, "gv", hg)
                for j in range(4):
                    bank = banks.take(v, ("ss", hg, j))
                    wv = work[:, j // 2, j % 2, :]
                    v.tensor_scalar(wv, bank, EPS2, None, ALU.add).then_inc(sem("ss_eps"), 1)
                    v.wait_ge(sem("ss_root"), 4 * hg + j + 1)
                    chain(v.reciprocal(wv, wv))
                    part = gT[:, j // 2, 2 * (j % 2):2 * (j % 2) + 2, :]
                    last = v.scalar_tensor_tensor(part.rearrange("p h s -> p (h s)"), part.rearrange("p h s -> p (h s)"),
                                                  float(P) ** -0.5 if j < 2 else 1.0, wv, ALU.mult, ALU.mult)
                    banks.release(last, ("ss", hg, j))
                if hg == 0:
                    banks.moved(v, "cols")
                for h in range(HG):
                    bank = banks.take(v, ("rb", hg, h))
                    hh = HG * hg + h
                    for t in range(NT):
                        last = v.tensor_scalar(attnT[:, t, h, :], bank[:, t * P:(t + 1) * P], cols[:, t, hh:hh + 1], 0.0,
                                               ALU.subtract, ALU.min)
                    last.then_inc(sem("dlog"), 1)
                for h in range(HG):
                    v.wait_ge(sem("dstrict"), 4 * hg + h + 1)
                    v.wait_ge(sem("egb"), 4 * hg + h + 1)
                    rbk = banks.take(v, ("rb", hg, h))
                    last = v.tensor_tensor(AT[:, :, h, :], AT[:, :, h, :],
                                           rbk[:, S:2 * S].rearrange("p (t n) -> p t n", t=NT), ALU.mult)
                    banks.release(last, ("rb", hg, h))
                    banks.moved(v, ("rb", hg, h))
                    v.wait_ge(sem("dincl"), 4 * hg + h + 1)
                    bank = banks.take(v, ("kq", hg, h))
                    v.tensor_tensor(AT[:, :, h, :], AT[:, :, h, :],
                                    bank[:, 0:S].rearrange("p (t n) -> p t n", t=NT), ALU.mult).then_inc(sem("kk"), 1)
                    last = v.tensor_tensor(attnT[:, :, h, :], attnT[:, :, h, :],
                                           bank[:, S:2 * S].rearrange("p (t n) -> p t n", t=NT), ALU.mult)
                    banks.release(last, ("kq", hg, h))
                    v.tensor_tensor(egb[:, h, :], egb[:, h, :], gT[:, 0, h, P:S], ALU.mult).then_inc(sem("qdec"), 1)
                for t in range(NT):
                    bank = banks.take(v, ("kt", hg, t))
                    col = cols[:, 5 - t, HG * hg:HG * hg + HG]
                    last = v.tensor_tensor((kdec, kbg)[t][:, :, :], heads(bank), bcast(col, P), ALU.mult)
                    banks.release(last, ("kt", hg, t))
                for t in range(NT):
                    bank = banks.take(v, ("vt", hg, t))
                    last = v.tensor_tensor(vb[:, t], heads(bank), bcast(cols[:, 2 + t, HG * hg:HG * hg + HG], P), ALU.mult)
                    banks.release(last, ("vt", hg, t))
                for t in range(NT):
                    v.wait_ge(sem("ATm"), 2 * LEVELS * hg + t + 1)
                    v.tensor_tensor(XT[:, t], heads(ATm[:, t, :]), ident[:, :].unsqueeze(1).to_broadcast([P, HG, P]),
                                    ALU.add).then_inc(sem("x1T"), 1)
                for l in range(1, LEVELS):
                    for t in range(NT):
                        for w, buf in (("xx", X), ("xt", XT)):
                            if w == "xx" and l == LEVELS - 1:
                                continue
                            bank = banks.take(v, (w, hg, l, t))
                            if w == "xx":
                                banks.done(v, ("xt", hg, l, t))
                            banks.release(v.tensor_tensor(buf[:, t], buf[:, t], heads(bank), ALU.add), (w, hg, l, t))
                for h in range(HG):
                    bank = banks.take(v, ("lo", hg, h))
                    chain.mark(v.reduce_max(fmax[:, h, 0:1], bank[:, 0:P], AX.X))
                    chain(v.reduce_max(fmax[:, h, 1:2], bank[:, P:384], AX.X))
                    v.tensor_scalar(fmax[:, h, :], fmax[:, h, :], -1.0, None, ALU.mult).then_inc(sem("fmax"), 1)
                for h in range(HG):
                    banks.moved(v, ("lo", hg, h))
                    chain(v.reciprocal(fsum[:, h, :], fsum[:, h, :]))
                    v.tensor_scalar(prob[:, h, 0:P], prob[:, h, 0:P], fsum[:, h, 0:1], None, ALU.mult)
                    v.tensor_scalar(prob[:, h, P:384], prob[:, h, P:384], fsum[:, h, 1:2], None, ALU.mult)\
                        .then_inc(sem("prob"), 1)
                for t in range(NT):
                    bank = banks.take(v, ("o%d" % t, hg))
                    banks.release(v.tensor_copy(o[:, t], heads(bank)), ("o%d" % t, hg))
                    banks.moved(v, ("o%d" % t, hg))
                    chain(v.tensor_tensor(vb[:, t], o[:, t], o[:, t], ALU.mult))
                    chain(v.tensor_reduce(osum[:, t, :], vb[:, t], AX.X, ALU.add))
                v.tensor_scalar(osum[:, :, :], osum[:, :, :], 1.0 / P, EPS2, ALU.mult, ALU.add).then_inc(sem("o_mean"), 1)
                v.wait_ge(sem("o_root"), hg + 1)
                chain(v.reciprocal(osum[:, :, :], osum[:, :, :]))
                for t in range(NT):
                    chain.mark(v.tensor_tensor(o[:, t], o[:, t], bcast(osum[:, t, :], P), ALU.mult))
                chain.wait()
                for t in range(NT):
                    banks.moved(v, ("gz", hg, t))
                    v.tensor_tensor(o[:, t], o[:, t], heads(gz[:, t, :]), ALU.mult).then_inc(sem("o_done"), 1)
                for j in range(2):
                    bank = banks.take(v, ("oT", hg, j))
                    last = v.tensor_scalar(ygT[:, HG * hg + 2 * j:HG * hg + 2 * j + 2, :],
                                           bank.rearrange("p (h s) -> p h s", h=2), prm2[:, 16:17], None, ALU.mult)
                    banks.release(last, ("oT", hg, j))
            for n in range(2):
                for j in range(2):
                    bank = banks.take(v, ("bf", n, j))
                    banks.moved(v, ("gf", n, j))
                    part = mixT[:, 4 * n + 2 * j:4 * n + 2 * j + 2, :].rearrange("p h s -> p (h s)")
                    banks.release(v.tensor_tensor(part, sgf[:, j, :], bank, ALU.mult), ("bf", n, j))
                for j in range(2):
                    bank = banks.take(v, ("bg", n, j))
                    banks.moved(v, ("gg", n, j))
                    part = mixT[:, 4 * n + 2 * j:4 * n + 2 * j + 2, :].rearrange("p h s -> p (h s)")
                    last = v.tensor_tensor(sgg[:, j, :], sgg[:, j, :], bank, ALU.mult)
                    banks.release(last, ("bg", n, j))
                    banks.moved(v, ("bg", n, j))
                    v.tensor_tensor(part, part, sgg[:, j, :], ALU.add).then_inc(sem("mixed"), 1)
            for n in range(2):
                for t in range(NT):
                    bank = banks.take(v, ("out", n, t))
                    xs = x[:, t, n * 512:(n + 1) * 512]
                    banks.release(v.tensor_tensor(xs, xs, bank, ALU.add), ("out", n, t))

        @block.tensor
        def _(pe):
            def feature_major(g, key, m, rhs=hT):
                bank = banks.claim(pe, key)
                for i in range(2):
                    for c in range(KC):
                        last = pe.matmul(bank[:, i * S:(i + 1) * S], piece(g)[:, c, (m + i) * P:(m + i + 1) * P],
                                         rhs[:, c, :], start=c == 0, stop=c == KC - 1)
                banks.filled(last, key)

            def token_major(g, key, t, lhs=hT):
                bank = banks.claim(pe, key)
                for c in range(KC):
                    last = pe.matmul(bank, lhs[:, c, t * P:(t + 1) * P], piece(g)[:, c, :],
                                     start=c == 0, stop=c == KC - 1)
                banks.filled(last, key)

            def both_f(g, name, n, rhs=hT):
                ring.landed(pe, g)
                for j in range(2):
                    feature_major(g, (name, n, j), 2 * j, rhs)

            def both_t(g, name, n, lhs=hT):
                ring.landed(pe, g)
                for t in range(NT):
                    token_major(g, (name, n, t), t, lhs)

            k.transposes(pe, banks, "nm")
            pe.wait_ge(sem("wg2_in"), 32)
            for j in range(4):
                banks.moved(pe, ("nm", j))
            for b, parts in ((0, (0, 8)), (1, (16,))):
                bank = banks.claim(pe, ("rw", b))
                for i, w0 in enumerate(parts):
                    for c in range(KC):
                        last = pe.matmul(bank[0:8, i * S:(i + 1) * S], wg2[:, c, w0:w0 + 8], hT[:, c, :],
                                         start=c == 0, stop=c == KC - 1)
                banks.filled(last, ("rw", b))
            for hg in range(2):
                g0 = 7 * hg
                both_f(g0, "gq", hg)
                both_f(g0 + 1, "gk", hg)
                if hg == 0:
                    pe.wait_ge(sem("beg"), 1)
                    bank = banks.claim(pe, "cols")
                    for i, r in enumerate((rowp[:, GC, 0:P], rowp[:, GC, P:S], rowp[:, BETA, 0:P], rowp[:, BETA, P:S],
                                           temp[:, BEG, P:S], temp[:, KD, 0:P])):
                        last = pe.transpose(bank[:, 8 * i:8 * i + 8], r, ident[0:8, 0:8])
                    banks.filled(last, "cols")
                both_f(g0 + 2, "gv", hg)
                for j in range(4):
                    pe.wait_ge(sem("g_sq"), 4 * hg + j + 1)
                    bank = banks.claim(pe, ("ss", hg, j))
                    banks.filled(pe.matmul(bank, ones[:, 0:P], sq[:, j % 2, :], start=True, stop=True), ("ss", hg, j))
                both_f(g0 + 3, "fq", hg)
                pe.wait_ge(sem("negc"), 1)
                for h in range(HG):
                    bank = banks.claim(pe, ("rb", hg, h))
                    pe.matmul(bank[:, 0:S], sel[:, HG * hg + h, :], rowp[:, GC, :], start=True, stop=True)
                    last = pe.matmul(bank[:, S:2 * S], sel[:, HG * hg + h, :], rowp[:, BETA, :], start=True, stop=True)
                    banks.filled(last, ("rb", hg, h))
                both_f(g0 + 4, "fk", hg)
                for j in range(4):
                    banks.moved(pe, ("ss", hg, j))
                for h in range(HG):
                    bank = banks.claim(pe, ("kq", hg, h))
                    for i in (0, 1):
                        for t in range(NT):
                            c = slice(t * P, (t + 1) * P)
                            last = pe.matmul(bank[:, i * S + t * P:i * S + (t + 1) * P], gT[:, 1, h, c],
                                             gT[:, 1 - i, h, c], start=True, stop=True)
                    banks.filled(last, ("kq", hg, h))
                for w, name in ((1, "kt"), (2, "vt")):
                    if w == 2:
                        pe.wait_ge(sem("g_silu"), 6 * hg + 6)
                    for t in range(NT):
                        bank = banks.claim(pe, (name, hg, t))
                        for h in range(HG):
                            last = pe.transpose(bank[:, h * P:(h + 1) * P], gT[:, w, h, t * P:(t + 1) * P], ident[:, :])
                        banks.filled(last, (name, hg, t))
                for t in range(NT):
                    pe.wait_ge(sem("x1T"), NT * hg + t + 1)
                    bank = banks.claim(pe, ("x1", hg, t))
                    for h in range(HG):
                        last = pe.transpose(bank[:, h * P:(h + 1) * P], XT[:, t, h, :], ident[:, :])
                    banks.filled(last, ("x1", hg, t))
                both_t(g0 + 5, "fv", hg)
                both_t(g0 + 6, "gz", hg)
                for l in range(1, LEVELS):
                    for t in range(NT):
                        pe.wait_ge(sem("ATm"), 2 * LEVELS * hg + 2 * l + t + 1)
                        if l == 1:
                            banks.moved(pe, ("x1", hg, t))
                        else:
                            banks.moved(pe, ("xx", hg, l - 1, t))
                        bank = banks.claim(pe, ("t1", hg, l, t))
                        for h in range(HG):
                            last = pe.matmul(bank[:, h * P:(h + 1) * P], ATm[:, t, h * P:(h + 1) * P], X[:, t, h, :],
                                             start=True, stop=True)
                        banks.filled(last, ("t1", hg, l, t))
                    for t in range(NT):
                        banks.moved(pe, ("t1", hg, l, t))
                        if l > 1:
                            banks.moved(pe, ("xt", hg, l - 1, t))
                        if l < LEVELS - 1:
                            bank = banks.claim(pe, ("xx", hg, l, t))
                            for h in range(HG):
                                last = pe.matmul(bank[:, h * P:(h + 1) * P], XT[:, t, h, :], T1[:, t, h * P:(h + 1) * P],
                                                 start=True, stop=True)
                            banks.filled(last, ("xx", hg, l, t))
                        bank = banks.claim(pe, ("xt", hg, l, t))
                        for h in range(HG):
                            last = pe.matmul(bank[:, h * P:(h + 1) * P], T1[:, t, h * P:(h + 1) * P], XT[:, t, h, :],
                                             start=True, stop=True)
                        banks.filled(last, ("xt", hg, l, t))
                for j in range(2):
                    banks.moved(pe, ("fq", hg, j))
                    banks.moved(pe, ("fk", hg, j))
                pe.wait_ge(sem("consts2"), 1)
                for h in range(HG):
                    bank = banks.claim(pe, ("lo", hg, h))
                    for t in range(NT):
                        c = bank[:, 0:P] if t == 0 else bank[:, P:384]
                        pe.matmul(c, fqk[:, 0, h, t * P:(t + 1) * P], fqk[:, 1, h, 0:(t + 1) * P], start=True, stop=False)
                        pe.matmul(c, sel[:, HG * hg + h, :], rowp[:, NEGC, 0:(t + 1) * P], start=False, stop=False)
                        last = pe.matmul(c[:, t * P:(t + 1) * P], ident[:, :], negmask[:, :], start=False, stop=True)
                    banks.filled(last, ("lo", hg, h))
                for t in range(NT):
                    banks.moved(pe, ("kt", hg, t))
                    banks.moved(pe, ("vt", hg, t))
                    banks.moved(pe, ("xt", hg, LEVELS - 1, t))

                def per_head(key, *terms):
                    bank = banks.claim(pe, key)
                    for h in range(HG):
                        for i, (a, b) in enumerate(terms):
                            last = pe.matmul(bank[:, h * P:(h + 1) * P], a[:, h, :], b[:, h, :], start=i == 0,
                                             stop=i == len(terms) - 1)
                    banks.filled(last, key)

                per_head(("u0", hg), (XT[:, 0], vb[:, 0]))
                per_head(("wT", hg), (kbg, XT[:, 1]))
                banks.moved(pe, ("u0", hg))
                per_head(("st", hg), (kdec, u[:, 0]))
                for h in range(HG):
                    banks.moved(pe, ("kq", hg, h))
                per_head(("o0", hg), (attnT[:, 0], u[:, 0]))
                banks.moved(pe, ("wT", hg))
                banks.moved(pe, ("st", hg))
                per_head(("u1", hg), (XT[:, 1], vb[:, 1]), (wTn, state))
                for h in range(HG):
                    pe.wait_ge(sem("prob"), 4 * hg + h + 1)
                    bank = banks.claim(pe, ("pt", hg, h))
                    pe.transpose(bank[:, 0:P], prob[:, h, 0:P], ident[:, :])
                    pe.transpose(bank[:, P:S], prob[:, h, P:S], ident[:, :])
                    last = pe.transpose(bank[:, S:384], prob[:, h, S:384], ident[:, :])
                    banks.filled(last, ("pt", hg, h))
                banks.moved(pe, ("u1", hg))
                pe.wait_ge(sem("qdec"), 4 * hg + 4)
                per_head(("o1", hg), (egb, state), (attnT[:, 1], u[:, 1]))
                for t in range(NT):
                    banks.moved(pe, ("fv", hg, t))
                for j in range(2):
                    bank = banks.claim(pe, ("pv", hg, j))
                    for h in (2 * j, 2 * j + 1):
                        banks.moved(pe, ("pt", hg, h))
                        c = bank[:, (h % 2) * S:(h % 2 + 1) * S]
                        pe.matmul(c, fv[:, 0, h * P:(h + 1) * P], probT[:, h, 0:S], start=True, stop=False)
                        last = pe.matmul(c[:, P:S], fv[:, 1, h * P:(h + 1) * P], probT[:, h, S:384], start=False, stop=True)
                    banks.filled(last, ("pv", hg, j))
                pe.wait_ge(sem("o_done"), NT * hg + NT)
                for j in range(2):
                    bank = banks.claim(pe, ("oT", hg, j))
                    for i in range(2):
                        for t in range(NT):
                            last = pe.transpose(bank[:, i * S + t * P:i * S + (t + 1) * P], o[:, t, 2 * j + i, :], ident[:, :])
                    banks.filled(last, ("oT", hg, j))
            for hg in range(2):
                for j in range(2):
                    banks.moved(pe, ("pv", hg, j))
                    banks.moved(pe, ("oT", hg, j))
            for n in range(2):
                g0 = 14 + 4 * n
                both_f(g0, "gf", n)
                both_f(g0 + 1, "bf", n, yfT)
                both_f(g0 + 2, "gg", n)
                both_f(g0 + 3, "bg", n, ygT)
            pe.wait_ge(sem("mixed"), 4)
            for n in range(2):
                both_t(22 + n, "out", n, mixT)


def phase_d(nc, A, out, sem, sb, ring, banks, k, env):
    x, xn, hT, ident, prm2, gain, spare, prow1, prow2 = (
        env[n] for n in "x xn hT ident prm2 gain spare prow1 prow2".split())
    aT = sb("aT2", [P, FF_CHUNKS, S])
    taps = sb("taps", [P, 2, 3 * FF_CHUNKS])
    cv = sb("cv", [P, 2, 2, 2, S])
    res = spare[:, 0:NT * D].rearrange("p (t d) -> p t d", t=NT)
    prow = (prow1, prow2)

    banks.plan("taps", *[("nn", j) for j in range(4)])
    for j in range(NUP):
        banks.plan(("up", j, 0), ("up", j, 1))
    banks.plan(*[("dn", t, n) for t in range(NT) for n in range(2)])

    with nc.Block() as block:
        @block.sync
        def _(sp):
            sp.dma_start(gain[:, :], A["norm_final_2"].unsqueeze(0).to_broadcast([P, D])).then_inc(sem("norm_final_in"), 16)
            for g in range(UP0 + 5, DOWN0 + NDOWN):
                if g - 5 < DOWN0:
                    banks.done(sp, ("up", g - 5 - UP0, 1))
                else:
                    sp.wait_ge(sem("down_piece_used"), g - 5 - DOWN0 + 1)
                if g < DOWN0:
                    load_up(sp, A, ring, g - UP0)
                else:
                    load_down(sp, A, ring, g - DOWN0)
            for t in range(NT):
                sp.wait_ge(sem("fin_x"), t + 1)
                sp.dma_start(out[0, t * P:(t + 1) * P, :], res[:, t, :]).then_inc(sem("out_stored"), 16)
            sp.wait_ge(sem("out_stored"), 16 * NT)

        @block.scalar
        def _(act):
            for h in range(2):
                for i in range(3):
                    act.dma_start(prow[h][FF_CHUNKS * i:FF_CHUNKS * (i + 1), :],
                                  A["ffn_conv_w_2"][0, i, h * FF_CHUNKS * P:(h + 1) * FF_CHUNKS * P]
                                  .rearrange("(c p) -> c p", p=P)).then_inc(sem("taps_in"), 16)
            flat = hT[:, :, :].rearrange("p (t c) n -> p t (c n)", t=NT)
            k.squares(act, "nn", 0, flat)
            k.root(act, "nn", 0)
            for j in range(NUP):
                act.wait_ge(sem("up_conv"), 2 * j + 1)
                act.activation(cv[:, j % 2, 0], cv[:, j % 2, 0], ACT.Silu).then_inc(sem("up_silu"), 1)
            act.wait_ge(sem("down_added"), 4)
            k.squares(act, "fin", 1, flat)
            k.root(act, "fin", 1)

        @block.vector
        def _(v):
            chain = Chain(v, sem("dveD"))
            k.scale(v, chain, "nn", 0, EPS2)
            bank = banks.take(v, "taps")
            last = v.tensor_copy(taps[:, :, :], bank[:, 0:6 * FF_CHUNKS].rearrange("p (h n) -> p h n", h=2))
            banks.release(last, "taps")
            k.evacuate(v, banks, "nn", prm2[:, 8:16])
            banks.moved(v, "taps")
            for j in range(NUP):
                for h in range(2):
                    bank = banks.take(v, ("up", j, h))
                    for i in range(3):
                        for a in range(2):
                            c = cv[:, j % 2, h, a, :]
                            w = taps[:, h, FF_CHUNKS * (2 - i) + 2 * j + a:FF_CHUNKS * (2 - i) + 2 * j + a + 1]
                            if i == 0:
                                last = v.tensor_scalar(c, bank[:, a * S:(a + 1) * S], w, None, ALU.mult)
                            else:
                                last = v.scalar_tensor_tensor(c[:, i:], bank[:, a * S:(a + 1) * S - i], w, c[:, i:],
                                                              ALU.mult, ALU.add)
                            if i < 2:
                                chain.mark(last)
                            elif a == 0:
                                last.then_inc(sem("up_conv_first"), 1)
                        if i < 2:
                            chain.wait()
                    banks.release(last, ("up", j, h))
                    banks.moved(v, ("up", j, h))
                    v.sem_inc(sem("up_conv"), 1)
                v.wait_ge(sem("up_silu"), j + 1)
                v.tensor_tensor(aT[:, 2 * j:2 * j + 2, :], cv[:, j % 2, 0], cv[:, j % 2, 1], ALU.mult)\
                    .then_inc(sem("up_act"), 1)
            for t in range(NT):
                for n in range(2):
                    bank = banks.take(v, ("dn", t, n))
                    xs = x[:, t, n * 512:(n + 1) * 512]
                    v.tensor_tensor(xs, xs, bank, ALU.add).then_inc(sem("down_added"), 1)
            v.wait_ge(sem("norm_final_in"), 16)
            k.gained(v, chain, "fin", 1, EPS2, gain[:, :], res)

        @block.tensor
        def _(pe):
            pe.wait_ge(sem("taps_in"), 16 * 6)
            bank = banks.claim(pe, "taps")
            for h in range(2):
                n = 3 * FF_CHUNKS
                last = pe.transpose(bank[:, h * n:(h + 1) * n], prow[h][0:n, :], ident[0:n, 0:n])
            banks.filled(last, "taps")
            k.transposes(pe, banks, "nn")
            for j in range(4):
                banks.moved(pe, ("nn", j))
            for j in range(NUP):
                s = (UP0 + j) % 5
                pe.wait_ge(ring.loaded[s], env_loaded(UP0 + j))
                w = ring.slot(UP0 + j).rearrange("p (c h n) -> p c h n", c=KC, h=2)
                for h in range(2):
                    bank = banks.claim(pe, ("up", j, h))
                    for a in range(2):
                        for c in range(KC):
                            last = pe.matmul(bank[:, a * S:(a + 1) * S], w[:, c, h, a * P:(a + 1) * P], hT[:, c, :],
                                             start=c == 0, stop=c == KC - 1)
                    banks.filled(last, ("up", j, h))
            pe.wait_ge(sem("up_act"), NUP)
            dn = {(t, n): banks.claim(pe, ("dn", t, n)) for t in range(NT) for n in range(2)}
            for j in range(NDOWN):
                g = DOWN0 + j
                pe.wait_ge(ring.loaded[g % 5], env_loaded(g))
                w = ring.slot(g).rearrange("p (c n) -> p c n", c=4)
                for c in range(min(4, FF_CHUNKS - 4 * j)):
                    kk = 4 * j + c
                    for t in range(NT):
                        for n in range(2):
                            last = pe.matmul(dn[t, n], aT[:, kk, t * P:(t + 1) * P], w[:, c, n * 512:(n + 1) * 512],
                                             start=kk == 0, stop=kk == FF_CHUNKS - 1)
                            if kk == FF_CHUNKS - 1:
                                banks.filled(last, ("dn", t, n))
                if j < NDOWN - 1:
                    last.then_inc(sem("down_piece_used"), 1)


def env_loaded(g):
    return 16 * sum(2 if UP0 <= q < DOWN0 else 1 for q in range(g % 5, g + 1, 5))


INS = ("x norm1_g w_in ig_b fg_b conv_w head_norm_g pool_w pool_scale w_out norm2_g w_router b_router w_gate "
       "b_gate w_up b_up w_down b_down normf_g norm_mix_2 w_in_2 fox_f_bias_2 gdn_conv_w_2 gdn_a_log_2 "
       "gdn_dt_bias_2 gdn_norm_2 w_branch_fox_2 w_branch_gdn_2 w_out_2 norm_ffn_2 w_up_2 ffn_conv_w_2 w_down_2 "
       "norm_final_2").split()


def kernel(**inputs):
    import concourse.bacc as bacc
    from concourse.bass_utils import run_bass_kernel_spmd

    nc = bacc.Bacc("TRN2", target_bir_lowering=False, num_devices=1)
    arrays, A = {}, {}
    for name in INS:
        a = np.ascontiguousarray(inputs[name])
        arrays[f"in_{name}"] = a
        A[name] = nc.dram_tensor(f"in_{name}", a.shape, mybir.dt.from_np(a.dtype), kind="ExternalInput").ap()
    out = nc.dram_tensor("out", (1, S, D), F32, kind="ExternalOutput").ap()
    build(nc, A, out)
    r = run_bass_kernel_spmd(nc, [arrays], core_ids=[0])
    return r.results[0]["out"]
```

```python
from contextlib import ExitStack

import numpy as np
import concourse.bass as bass
from concourse import mybir

F32 = mybir.dt.float32
F32R = mybir.dt.float32r
I32 = mybir.dt.int32
U32 = mybir.dt.uint32
ALU = mybir.AluOpType
ACT = mybir.ActivationFunctionType
AX = mybir.AxisListType

P = 128
D = 1024
S = 256
NT = S // P
KC = D // P
SLOTS = 6
PIECE = 4096
NH = 4
NE = 32
TOPK = 4
CAP = 64
EPS1 = 1e-5
EPS2 = 1e-6


class Ring:

    def __init__(self, sem, tag, buf, first=0, slots=SLOTS):
        self.buf, self.slots = buf, slots
        self.loaded = [sem(f"{tag}_loaded{s}") for s in range(slots)]
        self.first = first

    def nth(self, g):
        s = g % self.slots
        return (g - (s if s >= self.first else s + self.slots)) // self.slots

    def slot(self, g):
        s = g % self.slots
        return self.buf[0][:, s, :] if s < 2 else self.buf[1][:, s - 2, :]

    def load(self, eng, g, dst, src):
        eng.dma_start(dst, src).then_inc(self.loaded[g % self.slots], 16)

    def landed(self, pe, g):
        pe.wait_ge(self.loaded[g % self.slots], 16 * (self.nth(g) + 1))


class Banks:

    def __init__(self, sem, tag, ps):
        self.ps = ps
        self.full = [sem(f"{tag}_full{b}") for b in range(8)]
        self.free = [sem(f"{tag}_free{b}") for b in range(8)]
        self.uses = [0] * 8
        self.at = {}
        self.turn = 0

    def plan(self, *keys):
        for key in keys:
            b = self.turn % 8
            self.turn += 1
            self.at[key] = (b, self.uses[b])
            self.uses[b] += 1

    def claim(self, pe, key):
        b, n = self.at[key]
        if n > 0:
            pe.wait_ge(self.free[b], n)
        return self.ps[:, b, :]

    def filled(self, last, key):
        last.then_inc(self.full[self.at[key][0]], 1)

    def take(self, eng, key):
        b, n = self.at[key]
        eng.wait_ge(self.full[b], n + 1)
        return self.ps[:, b, :]

    def release(self, last, key):
        last.then_inc(self.free[self.at[key][0]], 1)

    def moved(self, eng, key):
        b, n = self.at[key]
        eng.wait_ge(self.free[b], n + 1)

    def done(self, eng, key):
        self.take(eng, key)


class Units:

    BUFS = 4

    def __init__(self, sem, ring, banks, high, low):
        self.sem, self.ring, self.banks, self.high, self.low = sem, ring, banks, high, low
        self.units = []
        self.emitted = {}

    def plan(self, g, kind, keys):
        for q, key in enumerate(keys):
            self.units.append((g, kind, q, key))

    def raw(self, u):
        g, kind, q, _ = self.units[u]
        p = self.ring.slot(g)
        if kind == "columns":
            return p.rearrange("p (c n) -> p c n", c=KC)[:, :, q * P:(q + 1) * P]
        if kind == "up":
            return p.rearrange("p (c h n) -> p c h n", c=KC, h=2)[:, :, q // 2, (q % 2) * P:(q % 2 + 1) * P]
        return p[:, q * D:(q + 1) * D].rearrange("p (c n) -> p c n", c=KC)

    def buf(self, which, u):
        return which[:, u % self.BUFS, :]

    def unnamed(self, u):
        return sum(self.units[w][3] is None for w in range(u + 1))

    def used(self, eng, u):
        key = self.units[u][3]
        if key is None:
            eng.wait_ge(self.sem("unit_used"), self.unnamed(u))
        else:
            self.banks.done(eng, key)

    def finish(self, last, u):
        key = self.units[u][3]
        if key is None:
            last.then_inc(self.sem("unit_used"), 1)
        else:
            self.banks.filled(last, key)

    def ahead(self, eng, who, n):
        for u in range(self.emitted.get(who, 0), min(n + self.BUFS, len(self.units))):
            self.emitted[who] = u + 1
            g, _, q, _ = self.units[u]
            hi = self.buf(self.high, u).rearrange("p (c n) -> p c n", c=KC)
            lo = self.buf(self.low, u).rearrange("p (c n) -> p c n", c=KC)
            if who == "high":
                if u >= self.BUFS:
                    self.used(eng, u - self.BUFS)
                eng.wait_ge(self.ring.loaded[g % self.ring.slots], landed_c(g))
                eng.copy(hi, self.raw(u)).then_inc(self.sem("high_split"), 1)
            elif who == ("low0", "low1")[u % 2]:
                eng.wait_ge(self.sem("high_split"), u + 1)
                eng.tensor_tensor(lo, self.raw(u), hi.bitcast(F32), ALU.subtract).then_inc(self.sem(who + "_split"), 1)

    def ready(self, pe, u):
        pe.wait_ge(self.sem("low%d_split" % (u % 2)), u // 2 + 1)

    def freed(self, sp, g):
        for who in (0, 1):
            n = sum(w[0] <= g for w in self.units[who::2])
            sp.wait_ge(self.sem("low%d_split" % who), n)


class Chain:

    def __init__(self, eng, sem, n=0):
        self.eng, self.sem, self.n, self.base = eng, sem, n, None

    def __call__(self, ins):
        self.n += 1
        ins.then_inc(self.sem, 1)
        self.wait()

    def mark(self, ins):
        self.n += 1
        ins.then_inc(self.sem, 1)

    def wait(self):
        self.eng.wait_ge(self.sem, self.n if self.base is None else self.base + self.n)


def bcast(ap, n):
    return ap.unsqueeze(2).to_broadcast([ap.shape[0], ap.shape[1], n])


def build(nc, A, out, dbg=None):
    top = ExitStack()
    sems = {}

    def sem(name):
        if name not in sems:
            sems[name] = top.enter_context(nc.semaphore(name))
        return sems[name]

    def sb(name, shape, dt=F32, stack=None):
        return (stack or top).enter_context(nc.sbuf_tensor(name, shape, dt))

    with top:
        ps = top.enter_context(nc.psum_tensor("ps", [P, 8, 512], F32))
        ring01 = sb("ring01", [P, 2, PIECE])
        x = sb("x", [P, NT, D])
        xn = sb("xn", [P, NT, D])
        hT = sb("hT", [P, KC, S])
        ident = sb("ident", [P, P])
        tri = sb("tri", [P, P])
        ustrict = sb("ustrict", [P, P])
        ones = sb("ones", [P, 2 * P])
        sel = sb("sel", [8, 8, P])
        stat = sb("stat", [P, 16])
        prow1 = sb("prow1", [P, P])
        prow2 = sb("prow2", [P, P])
        prm1 = sb("prm1", [P, P])
        prm2 = sb("prm2", [P, P])
        slot = sb("slot", [P, NT, NE])
        gate = sb("gate", [P, NT, NE])
        iota_cap = sb("iota_cap", [P, 2, CAP])
        passes = sb("passes", [1, 1], I32)
        gain = sb("gain", [P, D])
        ab = top.enter_context(ExitStack())
        ring25 = sb("ring25", [P, 4, PIECE], stack=ab)
        brow = sb("brow", [1, 2, D], stack=ab)
        ring = Ring(sem, "ringA", (ring01, ring25), first=5)
        banks = Banks(sem, "bankA", ps)
        k = Kit(nc, sem, ident, stat, x, xn, hT)
        with ExitStack() as a:
            phase_a(nc, A, sem, lambda n, s, dt=F32: sb(n, s, dt, a), ring, banks, k, locals())
        if dbg:
            dump(nc, sem, dbg.get("A"), locals(), "A")
        ringC = Ring(sem, "ringC", (ring01,), slots=2)
        banksC = Banks(sem, "bankC", ps)
        with ExitStack() as b:
            phase_b(nc, A, sem, lambda n, s, dt=F32: sb(n, s, dt, b), ring, banks, locals())
        if dbg:
            dump(nc, sem, dbg.get("B"), locals(), "B")
        ab.close()
        high = sb("high", [P, Units.BUFS, D], F32R)
        low = sb("low", [P, Units.BUFS, D], F32R)
        hTh = sb("hTh", [P, KC, S], F32R)
        hTl = sb("hTl", [P, KC, S], F32R)
        units = Units(sem, ringC, banksC, high, low)
        plan_units(units)
        with ExitStack() as ce:
            yfT = sb("yfT", [P, KC, S], stack=ce)
            ygT = sb("ygT", [P, KC, S], stack=ce)
            with ExitStack() as c:
                phase_c(nc, A, sem, lambda n, s, dt=F32: sb(n, s, dt, c), ringC, banksC, k, locals())
            with ExitStack() as e:
                phase_e(nc, A, sem, lambda n, s, dt=F32: sb(n, s, dt, e), ringC, banksC, k, locals())
        if dbg:
            dump(nc, sem, dbg.get("C"), locals(), "C")
        with ExitStack() as d:
            phase_d(nc, A, out, sem, lambda n, s, dt=F32: sb(n, s, dt, d), ringC, banksC, k, locals())


def dump(nc, sem, what, env, ph):
    if not what:
        return
    with nc.Block() as block:
        @block.sync
        def _(sp):
            for name, ap in what.items():
                sp.dma_start(ap, env[name][:]).then_inc(sem("dumped" + ph), 16)

            n = 16 * len(what)
            sp.wait_ge(sem("dumped" + ph), n)


P1 = dict(norm1_g=0, norm2_g=8, head_norm_g=16, pool_scale=20, conv_w=24)
P2 = dict(norm_mix_2=0, norm_ffn_2=8, gdn_norm_2=16, gdn_conv_w_2=17)


class Kit:

    def __init__(self, nc, sem, ident, stat, x, xn, hT):
        self.nc, self.sem, self.ident, self.stat, self.x, self.xn, self.hT = nc, sem, ident, stat, x, xn, hT

    @staticmethod
    def nth(tag):
        return ("n1", "n2", "nf", "nm", "nn", "fin").index(tag) + 1

    def squares(self, act, tag, n, junk):
        for t in range(NT):
            act.activation(junk[:, t, :], self.x[:, t, :], ACT.Square,
                           accum_out=self.stat[:, 4 * n + t:4 * n + t + 1]).then_inc(self.sem("norm_squares"), 1)

    def root(self, act, tag, n):
        c = self.stat[:, 4 * n:4 * n + 2]
        act.wait_ge(self.sem("norm_mean"), self.nth(tag))
        act.activation(c, c, ACT.Sqrt).then_inc(self.sem("norm_root"), 1)

    def scale(self, v, chain, tag, n, eps):
        c = self.stat[:, 4 * n:4 * n + 2]
        r = self.stat[:, 4 * n + 2:4 * n + 4]
        v.wait_ge(self.sem("norm_squares"), NT * self.nth(tag))
        v.tensor_scalar(c, c, 1.0 / D, eps, ALU.mult, ALU.add).then_inc(self.sem("norm_mean"), 1)
        v.wait_ge(self.sem("norm_root"), self.nth(tag))
        chain(v.reciprocal(r, c))
        for t in range(NT):
            v.tensor_scalar(self.xn[:, t, :], self.x[:, t, :], r[:, t:t + 1], None, ALU.mult)\
                .then_inc(self.sem("norm_scaled"), 1)

    def gained(self, v, chain, tag, n, eps, gain, out=None):
        c = self.stat[:, 4 * n:4 * n + 2]
        r = self.stat[:, 4 * n + 2:4 * n + 4]
        v.wait_ge(self.sem("norm_squares"), NT * self.nth(tag))
        v.tensor_scalar(c, c, 1.0 / D, eps, ALU.mult, ALU.add).then_inc(self.sem("norm_mean"), 1)
        v.wait_ge(self.sem("norm_root"), self.nth(tag))
        chain(v.reciprocal(r, c))
        for t in range(NT):
            v.scalar_tensor_tensor((self.x if out is None else out)[:, t, :], self.x[:, t, :], r[:, t:t + 1],
                                   gain, ALU.mult, ALU.mult).then_inc(self.sem("norm_scaled"), 1)

    def transposes(self, pe, banks, tag):
        pe.wait_ge(self.sem("norm_scaled"), NT * self.nth(tag))
        for j in range(KC // 2):
            bank = banks.claim(pe, (tag, j))
            for c in (2 * j, 2 * j + 1):
                for t in range(NT):
                    o = (c % 2) * S + t * P
                    last = pe.transpose(bank[:, o:o + P], self.xn[:, t, c * P:(c + 1) * P], self.ident[:, :])
            banks.filled(last, (tag, j))

    def evacuate(self, v, banks, tag, g):
        for j in range(KC // 2):
            bank = banks.take(v, (tag, j))
            last = v.tensor_tensor(self.hT[:, 2 * j:2 * j + 2, :], bank.rearrange("p (c t) -> p c t", c=2),
                                   bcast(g[:, 2 * j:2 * j + 2], S), ALU.mult)
            banks.release(last, (tag, j))


EXPERT = 12


def load_biases(sp, A, brow, sem, e):
    for m, name in enumerate(("b_gate", "b_up")):
        sp.dma_start(brow[0:1, m, :], A[name][0][bass.ds(e, 1), :]).then_inc(sem("brow_in"), 16)


def load_half(sp, A, ring, m, h, e):
    g = EXPERT + 2 * m + h
    w = A[("w_gate", "w_up", "w_down")[m]][0]
    ring.load(sp, g, ring.slot(g).rearrange("p (c n) -> p c n", c=4),
              w[bass.ds(e, 1), h * 512:(h + 1) * 512, :].rearrange("a (c p) n -> p (a c) n", p=P))


def evacuate_split(k, v, banks, tag, g, high, low):
    def low_part(j):
        v.wait_ge(k.sem(tag + "_high"), j + 1)
        c = slice(2 * j, 2 * j + 2)
        v.tensor_tensor(low[:, c, :], k.hT[:, c, :], high[:, c, :].bitcast(F32), ALU.subtract)\
            .then_inc(k.sem(tag + "_low"), 1)

    for j in range(KC // 2):
        bank = banks.take(v, (tag, j))
        last = v.tensor_tensor(k.hT[:, 2 * j:2 * j + 2, :], bank.rearrange("p (c t) -> p c t", c=2),
                               bcast(g[:, 2 * j:2 * j + 2], S), ALU.mult)
        banks.release(last, (tag, j))
        if j:
            low_part(j - 1)
    low_part(KC // 2 - 1)


def high_parts(k, act, banks, tag, high):
    for j in range(KC // 2):
        banks.moved(act, (tag, j))
        act.copy(high[:, 2 * j:2 * j + 2, :], k.hT[:, 2 * j:2 * j + 2, :]).then_inc(k.sem(tag + "_high"), 1)


def phase_a(nc, A, sem, sb, ring, banks, k, env):
    x, xn, hT, ident, tri, ustrict, ones, sel = (env[n] for n in "x xn hT ident tri ustrict ones sel".split())
    prow1, prow2, prm1, prm2, slot, gate, iota_cap, passes, brow = (
        env[n] for n in "prow1 prow2 prm1 prm2 slot gate iota_cap passes brow".split())
    W = NH * P

    wg = sb("wg", [P, KC, 8])
    qkT = sb("qkT", [P, 8, S])
    vext = sb("vext", [P, NT, NH, P + 1])
    og = sb("og", [P, NT, W])
    pa = sb("pa", [P, 4, S])
    pb = sb("pb", [P, 4, S])
    inv = sb("inv", [P, 4, S])
    tcount = sb("tcount", [P, S])
    yT = sb("yT", [P, KC, S])
    uT = yT[:, 0:4, :]
    DT = sb("DT", [P, NT, NH, S])
    hm = qkT[:, 0:4, :].rearrange("p (t a) (b d) -> p t (a b) d", t=NT, b=2)
    den = sb("den", [P, NT, NH])
    bst = sb("bst", [P, NT * NH, 6])
    mv = sb("mv", [P, NT * NH, 2])
    rs = sb("rs", [P, NT * NH])
    rows = sb("rows", [4, 10, S])
    FX, AB, E, L, LF, B, C, M, NM, EM = range(10)
    gb = sb("gb", [4, 2])
    ccol = sb("ccol", [P, 16])
    pool_w = sb("pool_w", [P, 4, P])
    wr = sb("wr", [P, KC, NE])
    brt = sb("brt", [P, NE])
    bdn = sb("bdn", [NE, D])
    lg = sb("lg", [P, NT, NE])
    v8 = sb("v8", [P, NT, 8])
    i8 = sb("i8", [P, NT, 8], U32)
    f8 = sb("f8", [P, NT, 8])
    e4 = sb("e4", [P, NT, 4])
    es = sb("es", [P, NT])
    mask = sb("mask", [P, NT, NE])
    tmp = sb("tmp", [P, NT, NE])
    iota_e = sb("iota_e", [P, NE])
    gT = sb("gT", [NE, NT, P])
    cnt = sb("cnt", [1, NE])
    cm = sb("cm", [1, 4])

    w_in, w_out = A["w_in"][0], A["w_out"][0]
    IN_COLS = [0, W, 2 * W, 3 * W, 4 * W + 2 * NH]
    Q_, K_, V_, O_, U_, OUT0, OUT1 = range(5, 12)

    banks.plan("prm1", *[("n1", j) for j in range(4)], "gates", *[("qk", j) for j in range(4)],
               "cols", ("mb", 0), ("mb", 1), ("v", 0), ("v", 1), *[("sc", h) for h in range(NH)],
               ("o", 0), ("o", 1), ("u", 0), ("u", 1),
               *[("num", j, hp) for j in range(NT) for hp in range(2)],
               "prm2", ("pool", 0), ("pool", 1), ("ym", 0), ("ym", 1),
               *[("out", n, t) for n in range(2) for t in range(NT)],
               *[("n2", j) for j in range(4)], "lg", "rk", "gt",
               *[("bd", t, n) for t in range(NT) for n in range(2)])

    def piece(g):
        return ring.slot(g).rearrange("p (c n) -> p c n", c=KC)

    with nc.Block() as block:
        @block.sync
        def _(sp):
            for j, c0 in enumerate(IN_COLS):
                ring.load(sp, Q_ + j, piece(Q_ + j), w_in[:, c0:c0 + 512].rearrange("(c p) n -> p c n", p=P))
            for n in range(2):
                if n == 1:
                    banks.done(sp, ("qk", 1))
                ring.load(sp, OUT0 + n, piece(OUT0 + n),
                          w_out[:, n * 512:(n + 1) * 512].rearrange("(c p) n -> p c n", p=P))
            load_biases(sp, A, brow, sem, 0)
            for m in range(3):
                for h in range(2):
                    g = 12 + 2 * m + h
                    banks.done(sp, [("qk", 3), ("v", 1), ("o", 1), ("u", 1), ("out", 0, 1), ("out", 1, 1)][2 * m + h])
                    load_half(sp, A, ring, m, h, 0)

        @block.scalar
        def _(act):
            act.dma_start(x[:, :, :], A["x"][0].rearrange("(t p) d -> p t d", p=P)).then_inc(sem("x_in"), 16)
            for name, n in (("norm1_g", 8), ("norm2_g", 8), ("head_norm_g", 4), ("pool_scale", 4)):
                act.dma_start(prow1[P1[name]:P1[name] + n, :],
                              A[name][0].rearrange("(c p) -> c p", p=P)).then_inc(sem("prow1_in"), 16)
            for i in range(4):
                act.dma_start(prow1[24 + 8 * i:32 + 8 * i, :],
                              A["conv_w"][0, i].rearrange("(c p) -> c p", p=P)).then_inc(sem("prow1_in"), 16)
            act.dma_start(wg[:, :, :], w_in[:, 4 * W:4 * W + 8].rearrange("(c p) n -> p c n", p=P))\
                .then_inc(sem("wg_in"), 16)
            act.dma_start(gb[:, 0:1], A["ig_b"].rearrange("a h -> h a")).then_inc(sem("gb_in"), 16)
            act.dma_start(gb[:, 1:2], A["fg_b"].rearrange("a h -> h a")).then_inc(sem("gb_in"), 16)
            act.wait_ge(sem("x_in"), 16)
            k.squares(act, "n1", 0, hT[:, :, :].rearrange("p (t c) n -> p t (c n)", t=NT))
            k.root(act, "n1", 0)
            act.dma_start(pool_w[:, :, :], A["pool_w"][0].rearrange("g c d -> c g d")).then_inc(sem("pool_w_in"), 16)
            act.dma_start(wr[:, :, :], A["w_router"][0].rearrange("(c p) n -> p c n", p=P)).then_inc(sem("wr_in"), 16)
            act.dma_start(brt[:, :], A["b_router"].to_broadcast([P, NE])).then_inc(sem("wr_in"), 16)
            act.dma_start(bdn[:, :], A["b_down"][0]).then_inc(sem("bdn_in"), 16)
            for name, n in (("norm_mix_2", 8), ("norm_ffn_2", 8), ("gdn_norm_2", 1)):
                act.dma_start(prow2[P2[name]:P2[name] + n, :],
                              A[name][0].rearrange("(c p) -> c p", p=P)).then_inc(sem("prow2_in"), 16)
            for i in range(4):
                act.dma_start(prow2[17 + 24 * i:41 + 24 * i, :],
                              A["gdn_conv_w_2"][0, i].rearrange("(c p) -> c p", p=P)).then_inc(sem("prow2_in"), 16)
            chain = Chain(act, sem("actA"))
            act.wait_ge(sem("fx"), 1)
            chain(act.activation(rows[:, AB, :], rows[:, FX, :], ACT.Abs))
            chain(act.activation(rows[:, E, :], rows[:, AB, :], ACT.Exp, scale=-1.0))
            act.activation(rows[:, L, :], rows[:, E, :], ACT.Ln, bias=1.0).then_inc(sem("ln1p"), 1)
            act.wait_ge(sem("nm"), 1)
            act.activation(rows[:, EM, :], rows[:, NM, :], ACT.Exp).then_inc(sem("em"), 1)
            for j in range(4):
                banks.moved(act, ("qk", j))
                act.activation(qkT[:, 2 * j:2 * j + 2, :], qkT[:, 2 * j:2 * j + 2, :], ACT.Silu)\
                    .then_inc(sem("qk_silu"), 1)
            banks.moved(act, ("mb", 0))
            banks.moved(act, ("mb", 1))
            for t in range(NT):
                act.activation(DT[:, t, :, t * P:], DT[:, t, :, t * P:], ACT.Exp).then_inc(sem("decay"), 1)
            for t in range(NT):
                bank = banks.take(act, ("o", t))
                last = act.activation(og[:, t, :], bank, ACT.Sigmoid)
                banks.release(last, ("o", t))
            for j in range(2):
                bank = banks.take(act, ("u", j))
                last = act.copy(uT[:, 2 * j:2 * j + 2, :], bank.rearrange("p (c t) -> p c t", c=2))
                banks.release(last, ("u", j))
            act.wait_ge(sem("hvar"), 1)
            act.activation(rs[:, :], rs[:, :], ACT.Sqrt).then_inc(sem("hroot"), 1)
            for g in range(4):
                if g % 2 == 0:
                    bank = banks.take(act, ("pool", g // 2))
                last = act.activation(yT[:, 4 + g, :], bank[:, (g % 2) * S:(g % 2 + 1) * S], ACT.Copy,
                                      scale=prm1[:, P1["pool_scale"] + g:P1["pool_scale"] + g + 1])
                if g % 2:
                    banks.release(last, ("pool", g // 2))
            for n in range(2):
                for t in range(NT):
                    banks.moved(act, ("out", n, t))
            k.squares(act, "n2", 1, yT[:, :, :].rearrange("p (t c) n -> p t (c n)", t=NT))
            k.root(act, "n2", 1)
            act.wait_ge(sem("v8neg"), 1)
            for t in range(NT):
                act.activation(e4[:, t, :], v8[:, t, 0:4], ACT.Exp, bias=f8[:, t, 7:8],
                               accum_out=es[:, t:t + 1]).then_inc(sem("e4"), 1)

        @block.gpsimd
        def _(g):
            chain = Chain(g, sem("poolA"))
            chain.mark(g.memset(ones[:, :], 1.0))
            chain.mark(g.memset(vext[:, :, :, P:P + 1], 1.0))
            chain(g.memset(sel[:, :, :], 1.0))
            g.affine_select(out=ident[:, :], in_=ones[:, 0:P], compare_op=ALU.is_equal, fill=0.0, base=0,
                            pattern=[[-1, P]], channel_multiplier=1).then_inc(sem("consts"), 1)
            g.affine_select(out=tri[:, :], in_=ones[:, 0:P], compare_op=ALU.is_ge, fill=0.0, base=0,
                            pattern=[[1, P]], channel_multiplier=-1).then_inc(sem("consts"), 1)
            g.affine_select(out=ustrict[:, :], in_=ones[:, 0:P], compare_op=ALU.is_gt, fill=0.0, base=0,
                            pattern=[[1, P]], channel_multiplier=-1).then_inc(sem("consts"), 1)
            g.affine_select(out=sel[:, :, :], in_=sel[:, :, :], compare_op=ALU.is_equal, fill=0.0, base=0,
                            pattern=[[-1, 8], [0, P]], channel_multiplier=1).then_inc(sem("consts"), 1)
            g.iota(iota_cap[:, :, :], pattern=[[0, 2], [1, CAP]], base=0, channel_multiplier=0,
                   allow_small_or_imprecise_dtypes=True).then_inc(sem("consts"), 1)
            g.iota(iota_e[:, :], pattern=[[1, NE]], base=0, channel_multiplier=0,
                   allow_small_or_imprecise_dtypes=True).then_inc(sem("consts"), 1)
            g.iota(tcount[:, :], pattern=[[1, S]], base=1, channel_multiplier=0,
                   allow_small_or_imprecise_dtypes=True).then_inc(sem("tcount"), 1)
            for t in range(NT):
                g.wait_ge(sem("decay"), t + 1)
                g.tensor_tensor(DT[:, t, :, t * P:t * P + P], DT[:, t, :, t * P:t * P + P],
                                tri[:, :].unsqueeze(1).to_broadcast([P, NH, P]), ALU.mult)\
                    .then_inc(sem("decay_masked"), 1)
            for j in range(2):
                banks.moved(g, ("u", j))
            g.wait_ge(sem("inv"), 4)
            src = uT
            for n in range(4):
                dst = (pa, pb)[n % 2]
                w = 1 << n
                chain.mark(g.tensor_tensor(dst[:, n:, w:], src[:, n:, w:], src[:, n:, :S - w], ALU.add))
                chain(g.tensor_copy(dst[:, n:, 0:w], src[:, n:, 0:w]))
                src = dst
                chain(g.tensor_tensor(inv[:, n, :], inv[:, n, :], dst[:, n, :], ALU.mult))
            g.tensor_tensor(inv[:, :, :], inv[:, :, :], uT[:, :, :], ALU.subtract).then_inc(sem("pooled"), 1)

        @block.vector
        def _(v):
            chain = Chain(v, sem("dveA"))
            k.scale(v, chain, "n1", 0, EPS1)
            bank = banks.take(v, "prm1")
            last = v.tensor_copy(prm1[:, 0:56], bank[:, 0:56])
            banks.release(last, "prm1")
            banks.moved(v, "prm1")
            k.evacuate(v, banks, "n1", prm1[:, 0:8])
            v.wait_ge(sem("gb_in"), 32)
            bank = banks.take(v, "gates")
            v.tensor_scalar(rows[:, FX, :], bank[0:4, S:2 * S], gb[:, 1:2], None, ALU.add).then_inc(sem("fx"), 1)
            v.wait_ge(sem("tcount"), 1)
            chain(v.reciprocal(tcount[:, :], tcount[:, :]))
            for n in range(4):
                v.tensor_scalar(inv[:, n, :], tcount[:, :], 1.0 / (2 << n), None, ALU.max).then_inc(sem("inv"), 1)
            v.wait_ge(sem("ln1p"), 1)
            chain(v.scalar_tensor_tensor(rows[:, LF, :], rows[:, FX, :], 0.0, rows[:, L, :], ALU.min, ALU.subtract))
            v.wait_ge(sem("consts"), 6)
            chain(v.tensor_tensor_scan(rows[:, B, :], ones[0:4, :], rows[:, LF, :], 0.0, ALU.mult, ALU.add))
            last = v.scalar_tensor_tensor(rows[:, C, :], bank[0:4, 0:S], gb[:, 0:1], rows[:, B, :],
                                          ALU.add, ALU.subtract)
            banks.release(last, "gates")
            banks.moved(v, "gates")
            chain(v.tensor_tensor_scan(rows[:, M, :], rows[:, C, :], rows[:, C, :], 0.0, ALU.max, ALU.max))
            v.scalar_tensor_tensor(rows[:, NM, :], rows[:, M, :], -1.0, rows[:, B, :], ALU.mult, ALU.subtract)\
                .then_inc(sem("nm"), 1)
            v.tensor_scalar(rows[:, M, :], rows[:, M, :], -1.0, None, ALU.mult).then_inc(sem("negm"), 1)
            for j in range(4):
                bank = banks.take(v, ("qk", j))
                for i in range(4):
                    for c in (2 * j, 2 * j + 1):
                        o = (c % 2) * S
                        w = prm1[:, 24 + 8 * (3 - i) + c:25 + 8 * (3 - i) + c]
                        if i == 0:
                            last = v.tensor_scalar(qkT[:, c, :], bank[:, o:o + S], w, None, ALU.mult)
                        else:
                            last = v.scalar_tensor_tensor(qkT[:, c, i:], bank[:, o:o + S - i], w, qkT[:, c, i:],
                                                          ALU.mult, ALU.add)
                        if i < 3:
                            chain.mark(last)
                    if i < 3:
                        chain.wait()
                banks.release(last, ("qk", j))
            bank = banks.take(v, "cols")
            last = v.tensor_copy(ccol[:, :], bank[:, 0:16])
            banks.release(last, "cols")
            banks.moved(v, "cols")
            for h in range(NH):
                if h % 2 == 0:
                    bank = banks.take(v, ("mb", h // 2))
                for t in range(NT):
                    o = (h % 2) * S
                    last = v.tensor_scalar(DT[:, t, h, t * P:], bank[:, o + t * P:o + S],
                                           ccol[:, 4 * t + h:4 * t + h + 1], 0.0, ALU.add, ALU.min)
                if h % 2:
                    banks.release(last, ("mb", h // 2))
            for j in (2, 3):
                v.wait_ge(sem("qk_silu"), j + 1)
                v.tensor_scalar(qkT[:, 2 * j:2 * j + 2, :], qkT[:, 2 * j:2 * j + 2, :], float(P) ** -0.5, None,
                                ALU.mult).then_inc(sem("k_scaled"), 1)
            for t in range(NT):
                bank = banks.take(v, ("v", t))
                last = v.tensor_copy(vext[:, t, :, 0:P], bank.rearrange("p (h d) -> p h d", h=NH))
                banks.release(last, ("v", t))
            v.wait_ge(sem("decay_masked"), NT)
            for h in range(NH):
                bank = banks.take(v, ("sc", h))
                v.tensor_tensor(DT[:, 0, h, :], bank[:, 0:S], DT[:, 0, h, :], ALU.mult)
                last = v.tensor_tensor(DT[:, 1, h, P:], bank[:, S:S + P], DT[:, 1, h, P:], ALU.mult)
                banks.release(last, ("sc", h))
            for j in range(NT):
                for hp in range(2):
                    bank = banks.take(v, ("num", j, hp))
                    pair = bank[:, 0:2 * (P + 1)].rearrange("p (h d) -> p h d", h=2)
                    dd = den[:, j, 2 * hp:2 * hp + 2]
                    em = ccol[:, 8 + 4 * j + 2 * hp:8 + 4 * j + 2 * hp + 2].unsqueeze(2)
                    chain(v.scalar_tensor_tensor(dd.unsqueeze(2), pair[:, :, P:P + 1], -1.0, em, ALU.mult, ALU.max))
                    chain(v.tensor_tensor(dd.unsqueeze(2), pair[:, :, P:P + 1], dd.unsqueeze(2), ALU.max))
                    chain(v.reciprocal(dd, dd))
                    for h in range(2):
                        last = v.tensor_scalar(hm[:, j, 2 * hp + h, :], pair[:, h, 0:P],
                                               den[:, j, 2 * hp + h:2 * hp + h + 1], None, ALU.mult)
                    banks.release(last, ("num", j, hp))
                    banks.moved(v, ("num", j, hp))
                    for h in range(2):
                        n = j * NH + 2 * hp + h
                        chain.mark(v.bn_stats(bst[:, n, :], hm[:, j, 2 * hp + h, :]))
            chain.wait()
            for n in range(NT * NH):
                chain.mark(v.bn_aggr(mv[:, n, :], bst[:, n, :]))
            chain.wait()
            v.tensor_scalar(rs[:, :].unsqueeze(2), mv[:, :, 1:2], EPS1, None, ALU.add).then_inc(sem("hvar"), 1)
            v.wait_ge(sem("hroot"), 1)
            chain(v.reciprocal(rs[:, :], rs[:, :]))
            for n in range(NT * NH):
                v1 = hm[:, n // NH, n % NH, :]
                chain.mark(v.tensor_scalar(v1, v1, mv[:, n, 0:1], rs[:, n:n + 1], ALU.subtract, ALU.mult))
            chain.wait()
            for t in range(NT):
                banks.moved(v, ("o", t))
                v.tensor_tensor(og[:, t, :], og[:, t, :], hm[:, t, :, :].rearrange("p h d -> p (h d)"), ALU.mult)\
                    .then_inc(sem("ym"), 1)
            bank = banks.take(v, "prm2")
            last = v.tensor_copy(prm2[:, 0:113], bank[:, 0:113])
            banks.release(last, "prm2")
            for j in range(2):
                bank = banks.take(v, ("ym", j))
                last = v.tensor_tensor(yT[:, 2 * j:2 * j + 2, :], bank.rearrange("p (c t) -> p c t", c=2),
                                       bcast(prm1[:, 16 + 2 * j:18 + 2 * j], S), ALU.mult)
                banks.release(last, ("ym", j))
            for n in range(2):
                for t in range(NT):
                    bank = banks.take(v, ("out", n, t))
                    xs = x[:, t, n * 512:(n + 1) * 512]
                    last = v.tensor_tensor(xs, xs, bank, ALU.add)
                    banks.release(last, ("out", n, t))
            k.scale(v, chain, "n2", 1, EPS1)
            k.evacuate(v, banks, "n2", prm1[:, 8:16])
            v.wait_ge(sem("wr_in"), 32)
            bank = banks.take(v, "lg")
            last = v.tensor_tensor(lg[:, :, :], bank[:, 0:NT * NE].rearrange("p (t e) -> p t e", t=NT),
                                   brt[:, :].unsqueeze(1).to_broadcast([P, NT, NE]), ALU.add)
            banks.release(last, "lg")
            banks.moved(v, "lg")
            for t in range(NT):
                chain.mark(v.max(v8[:, t, :], lg[:, t, :]))
            chain.wait()
            for t in range(NT):
                chain.mark(v.max_index(i8[:, t, :], v8[:, t, :], lg[:, t, :]))
            chain.wait()
            chain(v.tensor_copy(f8[:, :, :], i8[:, :, :]))
            v.tensor_scalar(f8[:, :, 7:8], v8[:, :, 0:1], -1.0, None, ALU.mult).then_inc(sem("v8neg"), 1)
            v.wait_ge(sem("e4"), NT)
            chain(v.reciprocal(es[:, :], es[:, :]))
            chain(v.tensor_tensor(e4[:, :, :], e4[:, :, :], bcast(es[:, :], TOPK), ALU.mult))
            for q in range(TOPK):
                for t in range(NT):
                    i = f8[:, t, q:q + 1]
                    if q == 0:
                        chain.mark(v.tensor_scalar(mask[:, t, :], iota_e[:, :], i, None, ALU.is_equal))
                        chain.mark(v.tensor_scalar(gate[:, t, :], iota_e[:, :], i, e4[:, t, q:q + 1],
                                                   ALU.is_equal, ALU.mult))
                    else:
                        chain.mark(v.scalar_tensor_tensor(mask[:, t, :], iota_e[:, :], i, mask[:, t, :],
                                                          ALU.is_equal, ALU.add))
                        chain(v.tensor_scalar(tmp[:, t, :], iota_e[:, :], i, e4[:, t, q:q + 1],
                                              ALU.is_equal, ALU.mult))
                        chain.mark(v.tensor_tensor(gate[:, t, :], gate[:, t, :], tmp[:, t, :], ALU.add))
                chain.wait()
            v.tensor_copy(tmp[:, :, :], mask[:, :, :]).then_inc(sem("mask"), 1)
            bank = banks.take(v, "rk")
            rk = bank[:, 0:NT * NE].rearrange("p (t e) -> p t e", t=NT)
            chain.mark(v.scalar_tensor_tensor(slot[:, :, :], rk, 1.0, mask[:, :, :], ALU.add, ALU.mult))
            last = v.tensor_copy(cnt[:, :], bank[0:1, 256:256 + NE])
            banks.release(last, "rk")
            banks.moved(v, "rk")
            chain.mark(v.tensor_scalar(slot[:, :, :], slot[:, :, :], -1.0, None, ALU.add))
            chain(v.reduce_max(cm[:, 0:1], cnt[:, :], AX.X))
            chain.mark(v.tensor_scalar(cm[:, 2:3], cm[:, 0:1], 2.0 * CAP, 1.0, ALU.is_gt, ALU.add))
            chain(v.tensor_scalar(cm[:, 1:2], cm[:, 0:1], 1.0 * CAP, None, ALU.is_gt))
            chain(v.tensor_tensor(cm[:, 1:2], cm[:, 1:2], cm[:, 2:3], ALU.add))
            chain(v.tensor_scalar(cm[:, 3:4], cm[:, 0:1], 3.0 * CAP, None, ALU.is_gt))
            v.tensor_tensor(passes[:, :], cm[:, 1:2], cm[:, 3:4], ALU.add).then_inc(sem("passes"), 1)
            bank = banks.take(v, "gt")
            last = v.tensor_copy(gT[:, :, :], bank[0:NE, 0:S].rearrange("p (t n) -> p t n", t=NT))
            banks.release(last, "gt")
            for t in range(NT):
                for n in range(2):
                    bank = banks.take(v, ("bd", t, n))
                    xs = x[:, t, n * 512:(n + 1) * 512]
                    last = v.tensor_tensor(xs, xs, bank, ALU.add)
                    banks.release(last, ("bd", t, n))

        @block.tensor
        def _(pe):
            pe.wait_ge(sem("consts"), 4)
            pe.wait_ge(sem("prow1_in"), 16 * 8)
            bank = banks.claim(pe, "prm1")
            banks.filled(pe.transpose(bank[:, 0:56], prow1[0:56, :], ident[0:56, 0:56]), "prm1")
            k.transposes(pe, banks, "n1")
            pe.wait_ge(sem("wg_in"), 16)
            for j in range(4):
                banks.moved(pe, ("n1", j))
            bank = banks.claim(pe, "gates")
            for n in range(2):
                for c in range(KC):
                    last = pe.matmul(bank[0:4, n * S:(n + 1) * S], wg[:, c, 4 * n:4 * n + 4], hT[:, c, :],
                                     start=c == 0, stop=c == KC - 1)
            banks.filled(last, "gates")

            def feature_major(g, key, m):
                bank = banks.claim(pe, key)
                for i in range(2):
                    for c in range(KC):
                        last = pe.matmul(bank[:, i * S:(i + 1) * S], piece(g)[:, c, (m + i) * P:(m + i + 1) * P],
                                         hT[:, c, :], start=c == 0, stop=c == KC - 1)
                banks.filled(last, key)
                return last

            def token_major(g, key, t):
                bank = banks.claim(pe, key)
                for c in range(KC):
                    last = pe.matmul(bank, hT[:, c, t * P:(t + 1) * P], piece(g)[:, c, :],
                                     start=c == 0, stop=c == KC - 1)
                banks.filled(last, key)
                return last

            for g in (Q_, K_):
                ring.landed(pe, g)
                for m in (0, 2):
                    last = feature_major(g, ("qk", 2 * (g - Q_) + m // 2), m)
            pe.wait_ge(sem("em"), 1)
            pe.wait_ge(sem("negm"), 1)
            bank = banks.claim(pe, "cols")
            for n, r in enumerate((C, EM)):
                for t in range(NT):
                    o = 8 * n + 4 * t
                    last = pe.transpose(bank[:, o:o + 4], rows[:, r, t * P:(t + 1) * P], ident[0:4, 0:4])
            banks.filled(last, "cols")
            for h in range(NH):
                if h % 2 == 0:
                    bank = banks.claim(pe, ("mb", h // 2))
                last = pe.matmul(bank[:, (h % 2) * S:(h % 2 + 1) * S], sel[0:4, h, :], rows[:, M, :],
                                 start=True, stop=True)
                if h % 2:
                    banks.filled(last, ("mb", h // 2))
            ring.landed(pe, V_)
            for t in range(NT):
                last = token_major(V_, ("v", t), t)
            pe.wait_ge(sem("qk_silu"), 4)
            pe.wait_ge(sem("k_scaled"), 2)
            for h in range(NH):
                bank = banks.claim(pe, ("sc", h))
                pe.matmul(bank[:, 0:S], qkT[:, 4 + h, 0:P], qkT[:, h, :], start=True, stop=True)
                last = pe.matmul(bank[:, S:S + P], qkT[:, 4 + h, P:S], qkT[:, h, P:S], start=True, stop=True)
                banks.filled(last, ("sc", h))
            ring.landed(pe, O_)
            for t in range(NT):
                last = token_major(O_, ("o", t), t)
            ring.landed(pe, U_)
            for m in (0, 2):
                last = feature_major(U_, ("u", m // 2), m)
            for t in range(NT):
                banks.moved(pe, ("v", t))
            for h in range(NH):
                banks.moved(pe, ("sc", h))
            for j in range(NT):
                for hp in range(2):
                    bank = banks.claim(pe, ("num", j, hp))
                    for h in (2 * hp, 2 * hp + 1):
                        for i in range(j + 1):
                            o = (h % 2) * (P + 1)
                            last = pe.matmul(bank[:, o:o + P + 1], DT[:, i, h, j * P:(j + 1) * P], vext[:, i, h, :],
                                             start=i == 0, stop=i == j)
                    banks.filled(last, ("num", j, hp))
            pe.wait_ge(sem("prow2_in"), 16 * 7)
            bank = banks.claim(pe, "prm2")
            banks.filled(pe.transpose(bank[:, 0:113], prow2[0:113, :], ident[0:113, 0:113]), "prm2")
            pe.wait_ge(sem("pool_w_in"), 16)
            pe.wait_ge(sem("pooled"), 1)
            for g in range(4):
                if g % 2 == 0:
                    bank = banks.claim(pe, ("pool", g // 2))
                last = pe.matmul(bank[:, (g % 2) * S:(g % 2 + 1) * S], pool_w[:, g, :], inv[:, g, :],
                                 start=True, stop=True)
                if g % 2:
                    banks.filled(last, ("pool", g // 2))
            pe.wait_ge(sem("ym"), NT)
            for j in range(2):
                bank = banks.claim(pe, ("ym", j))
                for i in range(2):
                    for t in range(NT):
                        c = 2 * j + i
                        last = pe.transpose(bank[:, i * S + t * P:i * S + (t + 1) * P], og[:, t, c * P:(c + 1) * P],
                                            ident[:, :])
                banks.filled(last, ("ym", j))
            for j in range(2):
                banks.moved(pe, ("ym", j))
                banks.moved(pe, ("pool", j))
            for n in range(2):
                ring.landed(pe, OUT0 + n)
                for t in range(NT):
                    bank = banks.claim(pe, ("out", n, t))
                    for c in range(KC):
                        last = pe.matmul(bank, yT[:, c, t * P:(t + 1) * P], piece(OUT0 + n)[:, c, :],
                                         start=c == 0, stop=c == KC - 1)
                    banks.filled(last, ("out", n, t))
            k.transposes(pe, banks, "n2")
            for j in range(4):
                banks.moved(pe, ("n2", j))
            pe.wait_ge(sem("wr_in"), 32)
            bank = banks.claim(pe, "lg")
            for t in range(NT):
                for c in range(KC):
                    last = pe.matmul(bank[:, t * NE:(t + 1) * NE], hT[:, c, t * P:(t + 1) * P], wr[:, c, :],
                                     start=c == 0, stop=c == KC - 1)
            banks.filled(last, "lg")
            pe.wait_ge(sem("mask"), 1)
            bank = banks.claim(pe, "rk")
            pe.matmul(bank[:, 0:NE], ustrict[:, :], tmp[:, 0, :], start=True, stop=True)
            pe.matmul(bank[:, NE:2 * NE], ones[:, 0:P], tmp[:, 0, :], start=True, stop=False)
            pe.matmul(bank[:, NE:2 * NE], ustrict[:, :], tmp[:, 1, :], start=False, stop=True)
            pe.matmul(bank[0:1, 256:256 + NE], ones[:, 0:1], tmp[:, 0, :], start=True, stop=False)
            last = pe.matmul(bank[0:1, 256:256 + NE], ones[:, 0:1], tmp[:, 1, :], start=False, stop=True)
            banks.filled(last, "rk")
            bank = banks.claim(pe, "gt")
            for t in range(NT):
                last = pe.transpose(bank[0:NE, t * P:(t + 1) * P], gate[:, t, :], ident[:, :])
            banks.filled(last, "gt")
            pe.wait_ge(sem("bdn_in"), 16)
            banks.moved(pe, "gt")
            for t in range(NT):
                for n in range(2):
                    bank = banks.claim(pe, ("bd", t, n))
                    last = pe.matmul(bank, gT[:, t, :], bdn[:, n * 512:(n + 1) * 512], start=True, stop=True)
                    banks.filled(last, ("bd", t, n))


def phase_b(nc, A, sem, sb, ring, banks, env):
    x, xn, ident, prm1, slot, gate, iota_cap, passes, brow = (
        env[n] for n in "x xn ident prm1 slot gate iota_cap passes brow".split())
    ones_row = sb("ones_row", [1, CAP])
    pass0 = sb("pass0", [P, S // CAP + 1])
    pick = sb("pick", [P, NT, CAP])
    gpick = sb("gpick", [P, NT, 2, CAP])
    gpickT = sb("gpickT", [P, NT, P])
    xg = sb("xg", [P, KC, CAP])
    gt = sb("gt", [P, 512])
    sg = sb("sg", [P, 512])
    up = sb("up", [P, 512])
    aT = sb("aT", [P, 4, 2, CAP])
    y = sb("y", [P, 512])
    G_, T_, GATE, UP, AT, DN, SC0, SC1 = range(8)
    uses = [1, 1, 1, 1, 1, 1, 2, 2]
    first = list(banks.uses)

    def bank_claim(pe, b, i, nth=0):
        pe.wait_ge(banks.free[b], first[b] + uses[b] * i + nth)
        return banks.ps[:, b, :]

    def bank_take(eng, b, i, nth=0):
        eng.wait_ge(banks.full[b], first[b] + uses[b] * i + nth + 1)
        return banks.ps[:, b, :]

    def bank_moved(eng, b, i):
        eng.wait_ge(banks.free[b], first[b] + uses[b] * (i + 1))

    def bank_done(eng, b, i):
        eng.wait_ge(banks.full[b], first[b] + uses[b] * i)

    def passes_of(eng):
        eng.wait_ge(sem("passes"), 1)
        return eng.value_load(passes[0:1, 0:1], min_val=1, max_val=S // CAP)

    with nc.Block() as block:
        @block.sync
        def _(sp):
            steps = sp.snap(passes_of(sp) * NE)
            with sp.Fori(1, steps) as i:
                e = sp.snap(i % NE)
                sp.wait_ge(sem("bias_used"), i)
                load_biases(sp, A, brow, sem, e)
                for m, b in enumerate((GATE, UP, DN)):
                    sp.wait_ge(sem(f"first_half_used{m}"), i)
                    load_half(sp, A, ring, m, 0, e)
                    bank_done(sp, b, i)
                    load_half(sp, A, ring, m, 1, e)
            sp.wait_ge(sem("first_half_used0"), steps)
            load_c(sp, A, env["ringC"], 0)
            bank_done(sp, GATE, steps)
            load_c(sp, A, env["ringC"], 1)

        @block.vector
        def _(v):
            for p in range(S // CAP + 1):
                v.memset(pass0[:, p:p + 1], -float(p * CAP)).then_inc(sem("pass0"), 1)
            v.memset(ones_row[:, :], 1.0).then_inc(sem("ones_row"), 1)
            v.memset(y[:, :], 0.0).then_inc(sem("zeroed"), 1)
            v.memset(gpickT[:, :, :], 0.0).then_inc(sem("zeroed"), 1)
            v.wait_ge(sem("pass0"), S // CAP + 1)
            steps = v.snap(passes_of(v) * NE)

            def picks(e, p):
                for t in range(NT):
                    v.tensor_scalar(pick[:, t, :], iota_cap[:, 0, :], slot[:, t, bass.ds(e, 1)],
                                    pass0[:, bass.ds(p, 1)], ALU.subtract, ALU.is_equal).then_inc(sem("picks"), 1)

            def gathered(i):
                bank = bank_take(v, G_, i)
                v.tensor_tensor(xg[:, :, :], bank.rearrange("p (c j) -> p c j", c=KC), bcast(prm1[:, 8:16], CAP),
                                ALU.mult).then_inc(banks.free[G_], 1)

            def summed(i):
                for t in range(NT):
                    for h in range(2):
                        bank = bank_take(v, SC0 + h, i, t)
                        xs = x[:, t, h * 512:(h + 1) * 512]
                        v.tensor_tensor(xs, xs, bank, ALU.add).then_inc(banks.free[SC0 + h], 1)

            for t in range(NT):
                v.tensor_scalar(pick[:, t, :], iota_cap[:, 0, :], slot[:, t, 0:1], None, ALU.is_equal)\
                    .then_inc(sem("picks"), 1)
            gathered(0)
            with v.Fori(0, steps) as i:
                e = v.snap(i % NE)
                bank_done(v, T_, i)
                v.wait_ge(sem("picks"), NT * i + NT)
                for t in range(NT):
                    v.tensor_scalar(gpick[:, t, :, :], pick[:, t, :].unsqueeze(1).to_broadcast([P, 2, CAP]),
                                    gate[:, t, bass.ds(e, 1)], None, ALU.mult).then_inc(sem("gpicks"), 1)
                bank_done(v, G_, i + 1)
                v.wait_ge(sem("gpicks"), NT * i + NT)
                nxt = v.snap(i + 1)
                picks(v.snap(nxt % NE), v.snap(nxt // NE))
                bank = bank_take(v, GATE, i)
                v.tensor_scalar(gt[:, :], bank, 7.0, None, ALU.min).then_inc(banks.free[GATE], 1)
                v.wait_ge(sem("sig"), i + 1)
                v.tensor_tensor(gt[:, :], gt[:, :], sg[:, :], ALU.mult).then_inc(sem("glu"), 1)
                bank = bank_take(v, UP, i)
                v.tensor_scalar(up[:, :], bank, 7.0, -7.0, ALU.min, ALU.max).then_inc(banks.free[UP], 1)
                v.wait_ge(sem("glu"), i + 1)
                bank_moved(v, UP, i)
                v.scalar_tensor_tensor(gt[:, :], up[:, :], 1.0, gt[:, :], ALU.add, ALU.mult).then_inc(sem("acted"), 1)
                summed(i)
                bank = bank_take(v, AT, i)
                v.tensor_copy(aT[:, :, :, :], bank.rearrange("p (c h j) -> p c h j", c=4, h=2))\
                    .then_inc(banks.free[AT], 1)
                gathered(nxt)
            summed(steps)

        @block.scalar
        def _(act):
            act.dma_start(env["gain"][:, :], A["normf_g"].unsqueeze(0).to_broadcast([P, D]))\
                .then_inc(sem("normf_in"), 16)
            steps = act.snap(passes_of(act) * NE)
            with act.Fori(0, steps) as i:
                bank_moved(act, GATE, i)
                act.activation(sg[:, :], gt[:, :], ACT.Sigmoid, scale=1.702).then_inc(sem("sig"), 1)
                bank_done(act, SC1, i + 1)
                bank = bank_take(act, T_, i)
                act.copy(gpickT[:, :, :], bank[:, 0:NT * P].rearrange("p (t n) -> p t n", t=NT))\
                    .then_inc(banks.free[T_], 1)
                bank = bank_take(act, DN, i)
                act.copy(y[:, :], bank).then_inc(banks.free[DN], 1)

        @block.tensor
        def _(pe):
            steps = pe.snap(passes_of(pe) * NE)

            def gather(i):
                pe.wait_ge(sem("picks"), NT * i + NT)
                bank = bank_claim(pe, G_, i)
                for c in range(KC):
                    for t in range(NT):
                        last = pe.matmul(bank[:, c * CAP:(c + 1) * CAP], xn[:, t, c * P:(c + 1) * P],
                                         pick[:, t, :], start=t == 0, stop=t == NT - 1)
                last.then_inc(banks.full[G_], 1)

            def scatter_before(i):
                pe.wait_ge(banks.free[T_], first[T_] + i)
                pe.wait_ge(banks.free[DN], first[DN] + i)
                for t in range(NT):
                    for h in range(2):
                        bank = bank_claim(pe, SC0 + h, i, t)
                        pe.matmul(bank, gpickT[h * CAP:(h + 1) * CAP, t, :], y[h * CAP:(h + 1) * CAP, :],
                                  start=True, stop=True).then_inc(banks.full[SC0 + h], 1)

            pe.wait_ge(sem("ones_row"), 1)
            pe.wait_ge(sem("zeroed"), 2)
            gather(0)
            with pe.Fori(0, steps) as i:
                bank_moved(pe, G_, i)
                pe.wait_ge(sem("brow_in"), 32 * i + 32)
                for m, b in ((0, GATE), (1, UP)):
                    bank = bank_claim(pe, b, i)
                    for h in range(2):
                        last = pe.matmul(bank[h * CAP:(h + 1) * CAP, :], ones_row[:, :],
                                         brow[0:1, m, h * 512:(h + 1) * 512], start=True, stop=False)
                    if m == 1:
                        last.then_inc(sem("bias_used"), 1)
                    for kh in range(2):
                        g = EXPERT + 2 * m + kh
                        pe.wait_ge(ring.loaded[g % SLOTS], 16 * ring.nth(g) + 16 + 16 * i)
                        w = ring.slot(g).rearrange("p (c n) -> p c n", c=4)
                        for c in range(4):
                            for h in range(2):
                                last = pe.matmul(bank[h * CAP:(h + 1) * CAP, :], xg[:, 4 * kh + c, :],
                                                 w[:, c, h * 512:(h + 1) * 512], start=False,
                                                 stop=kh == 1 and c == 3)
                        if kh == 0:
                            last.then_inc(sem(f"first_half_used{m}"), 1)
                    last.then_inc(banks.full[b], 1)
                scatter_before(i)
                pe.wait_ge(sem("gpicks"), NT * i + NT)
                bank = bank_claim(pe, T_, i)
                for t in range(NT):
                    last = pe.transpose(bank[:, t * P:(t + 1) * P], gpick[:, t, :, :].rearrange("p a j -> p (a j)"),
                                        ident[:, :])
                last.then_inc(banks.full[T_], 1)
                pe.wait_ge(sem("acted"), i + 1)
                bank = bank_claim(pe, AT, i)
                for c in range(4):
                    last = pe.transpose(bank[:, c * P:(c + 1) * P], gt[:, c * P:(c + 1) * P], ident[:, :])
                last.then_inc(banks.full[AT], 1)
                gather(pe.snap(i + 1))
                bank_moved(pe, AT, i)
                bank = bank_claim(pe, DN, i)
                for kh in range(2):
                    g = EXPERT + 4 + kh
                    pe.wait_ge(ring.loaded[g % SLOTS], 16 * ring.nth(g) + 16 + 16 * i)
                    w = ring.slot(g).rearrange("p (c n) -> p c n", c=4)
                    for c in range(4):
                        for h in range(2):
                            last = pe.matmul(bank[h * CAP:(h + 1) * CAP, :], aT[:, c, kh, :],
                                             w[:, c, h * 512:(h + 1) * 512], start=kh == 0 and c == 0,
                                             stop=kh == 1 and c == 3)
                    if kh == 0:
                        last.then_inc(sem("first_half_used2"), 1)
                last.then_inc(banks.full[DN], 1)
            scatter_before(steps)


HG = 4
LEVELS = 7
FQ, FK, FV, FF, GQ, GK, GV, GA, GZ, GATE_F, GATE_G = (
    0, 1024, 2048, 3072, 3080, 4104, 5128, 6152, 6168, 7192, 8216)
PIECES_C = [("w_in_2", c + 512 * hg) for hg in range(2)
            for c in (GQ, GK, GV, FQ, FK, FV, GZ)]
PIECES_C += [p for n in range(2) for p in (
    ("w_in_2", GATE_F + 512 * n), ("w_branch_fox_2", 512 * n), ("w_in_2", GATE_G + 512 * n),
    ("w_branch_gdn_2", 512 * n))]
PIECES_C += [("w_out_2", 512 * n) for n in range(2)]


def load_c(sp, A, ring, g):
    name, c0 = PIECES_C[g]
    ring.load(sp, g, ring.slot(g).rearrange("p (c n) -> p c n", c=KC),
              A[name][0][:, c0:c0 + 512].rearrange("(c p) n -> p c n", p=P))


FF_CHUNKS = 22
NUP = FF_CHUNKS // 2
NDOWN = (FF_CHUNKS + 3) // 4
UP0 = len(PIECES_C)
DOWN0 = UP0 + NUP


def landed_c(g):
    return 16 * sum(2 if UP0 <= q < DOWN0 else 1 for q in range(g % 2, g + 1, 2))


def plan_units(units):
    g = 0
    def piece(kind, keys):
        nonlocal g
        units.plan(g, kind, keys)
        g += 1
    for hg in range(2):
        for w in ("gq", "gk", "gv", "fq", "fk"):
            piece("columns", (None, (w, hg, 0), None, (w, hg, 1)))
        for w in ("fv", "gz"):
            piece("rows", (None, None, None, (w, hg, 1)))
    for n in range(2):
        for w in ("gf", "bf", "gg", "bg"):
            piece("columns", (None, (w, n, 0), None, (w, n, 1)))
    for n in range(2):
        piece("rows", (None, None, None, ("out", n, 1)))
    for j in range(NUP):
        piece("up", (None, ("up", j, 0), None, ("up", j, 1)))
    for j in range(NDOWN):
        n = min(4, FF_CHUNKS - 4 * j)
        piece("rows", (None,) * n if j < NDOWN - 1 else (None,) * (n - 1) + (("dn", 1, 1),))


UNITS_GROUP, UNITS_E, UNITS_OUT = 28, 56, 88


def product(pe, units, u, out, xh, xl, c, start, stop):
    wh = units.buf(units.high, u)[:, c * P:(c + 1) * P]
    wl = units.buf(units.low, u)[:, c * P:(c + 1) * P]
    pe.matmul(out, wh, xh, start=start, stop=False)
    pe.matmul(out, wh, xl, start=False, stop=False)
    return pe.matmul(out, wl, xh, start=False, stop=stop)


def columns(pe, units, banks, u, keys, xh, xl):
    for q in range(4):
        if q % 2 == 0:
            bank = banks.claim(pe, keys[q // 2])
        units.ready(pe, u + q)
        for c in range(KC):
            last = product(pe, units, u + q, bank[:, (q % 2) * S:(q % 2 + 1) * S], xh[:, c, :], xl[:, c, :], c,
                           c == 0, c == KC - 1)
        units.finish(last, u + q)


def rows(pe, units, banks, u, keys, xh, xl):
    bank = [banks.claim(pe, key) for key in keys]
    for q in range(4):
        units.ready(pe, u + q)
        for t in range(NT):
            for c in range(2):
                wh = units.buf(units.high, u + q)[:, c * 512:(c + 1) * 512]
                wl = units.buf(units.low, u + q)[:, c * 512:(c + 1) * 512]
                a = slice(t * P, (t + 1) * P)
                kc = 2 * q + c
                pe.matmul(bank[t], xh[:, kc, a], wh, start=kc == 0, stop=False)
                pe.matmul(bank[t], xh[:, kc, a], wl, start=False, stop=False)
                last = pe.matmul(bank[t], xl[:, kc, a], wh, start=False, stop=kc == KC - 1)
            if q == 3 and t == 0:
                banks.filled(last, keys[0])
        units.finish(last, u + q)


def load_up(sp, A, ring, j):
    w = A["w_up_2"][0].rearrange("(c p) (h n) -> p c h n", p=P, h=2)
    dst = ring.slot(UP0 + j).rearrange("p (c h n) -> p c h n", c=KC, h=2)
    for h in range(2):
        ring.load(sp, UP0 + j, dst[:, :, h, :], w[:, :, h, j * 2 * P:(j + 1) * 2 * P])


def load_down(sp, A, ring, j):
    n = min(4, FF_CHUNKS - 4 * j)
    ring.load(sp, DOWN0 + j, ring.slot(DOWN0 + j).rearrange("p (c n) -> p c n", c=4)[:, 0:n, :],
              A["w_down_2"][0][4 * j * P:(4 * j + n) * P, :].rearrange("(c p) n -> p c n", p=P))


def phase_c(nc, A, sem, sb, ring, banks, k, env):
    x, xn, hT, ident, tri, ustrict, ones, sel, prm2, gain, units, hTh, hTl, yfT, ygT = (
        env[n] for n in "x xn hT ident tri ustrict ones sel prm2 gain units hTh hTl yfT ygT".split())
    wg2 = sb("wg2", [P, KC, 24])
    rb = sb("rb", [8, 3])
    rowp = sb("rowp", [8, 3, S])
    NEGC, GC, BETA = range(3)
    temp = xn[0:8, :, :].rearrange("p t (a s) -> p (t a) s", s=S)
    TA, TB, TC, TD, TE, BEG, KD, TF = range(8)
    cols = sb("cols", [P, 6, 8])
    lm = sb("lm", [P, LEVELS, P])
    gT = sb("gT2", [P, 3, HG, S])
    fqk = hT[:, :, :].rearrange("p (a h) s -> p a h s", a=2)
    fv = sb("fv", [P, NT, 512])
    gz = sb("gz", [P, NT, 512])
    X = sb("X", [P, NT, HG, P])
    XT = sb("XT", [P, NT, HG, P])
    work = sb("work", [P, 2, NT, HG * P])
    ATm, T1 = work[:, 0], work[:, 1]
    AT = xn[:, 0, :].rearrange("p (t h n) -> p t h n", t=NT, h=HG)
    attnT = xn[:, 1, :].rearrange("p (t h n) -> p t h n", t=NT, h=HG)
    sq = X[:, :, :, :].rearrange("p t h n -> p (t h n)").rearrange("p (b n) -> p b n", b=2)
    vb = sb("vb", [P, NT, HG, P])
    kbg = sb("kbg", [P, HG, P])
    kdec = sb("kdec", [P, HG, P])
    egb = sb("egb", [P, HG, P])
    u = gT[:, 2].rearrange("p h (t n) -> p t h n", t=NT)
    wTn = sb("wTn", [P, HG, P])
    state = sb("state", [P, HG, P])
    o = gT[:, 1].rearrange("p h (t n) -> p t h n", t=NT)
    osum = sb("osum", [P, NT, HG])
    prob = work[:, :, :, :].rearrange("p a t n -> p (a t n)")[:, 0:HG * 384].rearrange("p (h n) -> p h n", h=HG)
    probT = hT[:, :, :].rearrange("p c s -> p (c s)")[:, 0:HG * 384].rearrange("p (h n) -> p h n", h=HG)
    negmask = sb("negmask", [P, P])
    fmax = sb("fmax", [P, HG, NT])
    fsum = sb("fsum", [P, HG, NT])

    banks.plan(*[("nm", j) for j in range(4)], ("rw", 0), ("rw", 1))
    for hg in range(2):
        banks.plan(("gq", hg, 0), ("gq", hg, 1), ("gk", hg, 0), ("gk", hg, 1), *([] if hg else ["cols"]),
                   ("gv", hg, 0), ("gv", hg, 1), *[("ss", hg, j) for j in range(4)],
                   ("fq", hg, 0), ("fq", hg, 1), *[("rb", hg, h) for h in range(HG)],
                   ("fk", hg, 0), ("fk", hg, 1), *[("kq", hg, h) for h in range(HG)],
                   *[(w, hg, t) for w in ("kt", "vt") for t in range(NT)],
                   *[("x1", hg, t) for t in range(NT)], ("fv", hg, 0), ("fv", hg, 1),
                   ("gz", hg, 0), ("gz", hg, 1))
        for l in range(1, LEVELS):
            banks.plan(*[("t1", hg, l, t) for t in range(NT)])
            for t in range(NT):
                banks.plan(*([("xx", hg, l, t)] if l < LEVELS - 1 else []), ("xt", hg, l, t))
        banks.plan(*[("lo", hg, h) for h in range(HG)], ("u0", hg), ("wT", hg), ("st", hg), ("o0", hg), ("u1", hg),
                   *[("pt", hg, h) for h in range(HG)], ("o1", hg), ("pv", hg, 0), ("pv", hg, 1),
                   ("oT", hg, 0), ("oT", hg, 1))

    def heads(bank):
        return bank.rearrange("p (h n) -> p h n", h=HG)

    flat = hT[:, :, :].rearrange("p (t c) n -> p t (c n)", t=NT)

    with nc.Block() as block:
        @block.sync
        def _(sp):
            sp.dma_start(wg2[:, :, 0:8], A["w_in_2"][0][:, FF:FF + 8].rearrange("(c p) n -> p c n", p=P))\
                .then_inc(sem("wg2_in"), 16)
            sp.dma_start(wg2[:, :, 8:24], A["w_in_2"][0][:, GA:GA + 16].rearrange("(c p) n -> p c n", p=P))\
                .then_inc(sem("wg2_in"), 16)
            for i, name in enumerate(("fox_f_bias_2", "gdn_a_log_2", "gdn_dt_bias_2")):
                sp.dma_start(rb[:, i:i + 1], A[name].rearrange("a h -> h a")).then_inc(sem("rb_in"), 16)
            for g in range(2, 14 + 2):
                units.freed(sp, g - 2)
                load_c(sp, A, ring, g)

        @block.scalar
        def _(act):
            chain = Chain(act, sem("actC"))

            def ahead(n):
                units.ahead(act, "high", n)

            k.squares(act, "nf", 2, flat)
            k.root(act, "nf", 2)
            act.wait_ge(sem("norm_scaled"), NT * k.nth("nf"))
            k.squares(act, "nm", 3, flat)
            k.root(act, "nm", 3)
            ahead(0)
            high_parts(k, act, banks, "nm", hTh)
            act.wait_ge(sem("rb_in"), 48)
            chain(act.activation(rb[:, 1:2], rb[:, 1:2], ACT.Exp))
            banks.moved(act, ("rw", 0))
            for a, b in ((TA, TC), (TB, TD)):
                chain(act.activation(temp[:, b, :], temp[:, a, :], ACT.Abs))
                chain(act.activation(temp[:, b, :], temp[:, b, :], ACT.Exp, scale=-1.0))
            for b in (TC, TD):
                act.activation(temp[:, b, :], temp[:, b, :], ACT.Ln, bias=1.0).then_inc(sem("rows_ln"), 1)
            bank = banks.take(act, ("rw", 1))
            banks.release(act.activation(rowp[:, BETA, :], bank[0:8, 0:S], ACT.Sigmoid), ("rw", 1))
            act.wait_ge(sem("gc_rows"), 2)
            act.activation(temp[:, BEG, P:S], rowp[:, GC, P:S], ACT.Exp).then_inc(sem("eg_rows"), 1)
            act.activation(temp[:, KD, 0:P], temp[:, KD, 0:P], ACT.Exp).then_inc(sem("eg_rows"), 1)

            for hg in range(2):
                u0 = UNITS_GROUP * hg
                for w in range(3):
                    for j in range(2):
                        ahead(u0 + 4 * w + 2 * j + 2)
                        banks.moved(act, (("gq", "gk", "gv")[w], hg, j))
                        part = gT[:, w, 2 * j:2 * j + 2, :]
                        act.activation(part, part, ACT.Silu).then_inc(sem("g_silu"), 1)
                ahead(u0 + 12)
                for j in range(4):
                    act.wait_ge(sem("g_silu"), 6 * hg + 4)
                    if j >= 2:
                        banks.done(act, ("ss", hg, j - 2))
                    act.activation(sq[:, j % 2, :], gT[:, j // 2, 2 * (j % 2):2 * (j % 2) + 2, :].rearrange("p h s -> p (h s)"),
                                   ACT.Square).then_inc(sem("g_sq"), 1)
                for j in range(4):
                    act.wait_ge(sem("ss_eps"), 4 * hg + j + 1)
                    act.activation(work[:, j // 2, j % 2, :], work[:, j // 2, j % 2, :], ACT.Sqrt)\
                        .then_inc(sem("ss_root"), 1)
                if hg == 0:
                    act.wait_ge(sem("nm_low"), 4)
                for j in range(2):
                    ahead(u0 + 12 + 2 * j + 2)
                    bank = banks.take(act, ("fq", hg, j))
                    last = act.activation(fqk[:, 0, 2 * j:2 * j + 2, :], bank.rearrange("p (h s) -> p h s", h=2),
                                          ACT.Copy, scale=float(P) ** -0.5)
                    banks.release(last, ("fq", hg, j))
                for h in range(HG):
                    act.wait_ge(sem("dlog"), 4 * hg + h + 1)
                    act.activation(attnT[:, :, h, :], attnT[:, :, h, :], ACT.Exp).then_inc(sem("dexp"), 1)
                    bank = banks.take(act, ("rb", hg, h))
                    act.activation(egb[:, h, :], bank[:, P:S], ACT.Exp).then_inc(sem("egb"), 1)
                for j in range(2):
                    ahead(u0 + 16 + 2 * j + 2)
                    bank = banks.take(act, ("fk", hg, j))
                    last = act.copy(fqk[:, 1, 2 * j:2 * j + 2, :], bank.rearrange("p (h s) -> p h s", h=2))
                    banks.release(last, ("fk", hg, j))
                for t in range(NT):
                    bank = banks.take(act, ("x1", hg, t))
                    banks.release(act.copy(X[:, t], heads(bank)), ("x1", hg, t))
                for t in range(NT):
                    ahead(u0 + 20 + (3, 4)[t])
                    bank = banks.take(act, ("fv", hg, t))
                    banks.release(act.copy(fv[:, t, :], bank), ("fv", hg, t))
                for t in range(NT):
                    ahead(u0 + 24 + (3, 4)[t])
                    bank = banks.take(act, ("gz", hg, t))
                    banks.release(act.activation(gz[:, t, :], bank, ACT.Silu), ("gz", hg, t))
                for l in range(1, LEVELS):
                    for t in range(NT):
                        bank = banks.take(act, ("t1", hg, l, t))
                        banks.release(act.copy(T1[:, t, :], bank), ("t1", hg, l, t))
                for h in range(HG):
                    act.wait_ge(sem("fmax"), 4 * hg + h + 1)
                    bank = banks.take(act, ("lo", hg, h))
                    act.activation(prob[:, h, 0:P], bank[:, 0:P], ACT.Exp, bias=fmax[:, h, 0:1],
                                   accum_out=fsum[:, h, 0:1])
                    last = act.activation(prob[:, h, P:384], bank[:, P:384], ACT.Exp, bias=fmax[:, h, 1:2],
                                          accum_out=fsum[:, h, 1:2])
                    banks.release(last, ("lo", hg, h))
                bank = banks.take(act, ("u0", hg))
                banks.release(act.copy(u[:, 0], heads(bank)), ("u0", hg))
                bank = banks.take(act, ("wT", hg))
                banks.release(act.activation(wTn[:, :, :], heads(bank), ACT.Copy, scale=-1.0), ("wT", hg))
                bank = banks.take(act, ("st", hg))
                banks.release(act.copy(state[:, :, :], heads(bank)), ("st", hg))
                bank = banks.take(act, ("u1", hg))
                banks.release(act.copy(u[:, 1], heads(bank)), ("u1", hg))
                for h in range(HG):
                    bank = banks.take(act, ("pt", hg, h))
                    banks.release(act.copy(probT[:, h, :], bank[:, 0:384]), ("pt", hg, h))
                for j in range(2):
                    bank = banks.take(act, ("pv", hg, j))
                    last = act.copy(yfT[:, HG * hg + 2 * j:HG * hg + 2 * j + 2, :], bank.rearrange("p (h s) -> p h s", h=2))
                    banks.release(last, ("pv", hg, j))
                act.wait_ge(sem("o_mean"), hg + 1)
                act.activation(osum[:, :, :], osum[:, :, :], ACT.Sqrt).then_inc(sem("o_root"), 1)

        @block.gpsimd
        def _(g):
            chain = Chain(g, sem("poolC"))
            chain(g.memset(lm[:, :, :], 0.0))
            for l in range(LEVELS):
                b = 1 << l
                odd = lm[:, l, :].rearrange("p (m o r) -> p m o r", o=2, r=b)[:, :, 1, :]
                m = P // (2 * b)
                chain(g.memset(odd, -1.0))
                chain(g.affine_select(out=odd, in_=odd, compare_op=ALU.is_ge, fill=0.0, base=0,
                                      pattern=[[-2 * b, m], [0, b]], channel_multiplier=1))
                chain(g.affine_select(out=odd, in_=odd, compare_op=ALU.is_ge, fill=0.0, base=b - 1,
                                      pattern=[[2 * b, m], [0, b]], channel_multiplier=-1))
            chain(g.memset(negmask[:, :], 0.0))
            g.affine_select(out=negmask[:, :], in_=negmask[:, :], compare_op=ALU.is_ge, fill=-1e30, base=0,
                            pattern=[[-1, P]], channel_multiplier=1).then_inc(sem("consts2"), 1)
            units.ahead(g, "low1", 0)
            for hg in range(2):
                u0 = UNITS_GROUP * hg
                units.ahead(g, "low1", u0 + 14)
                for h in range(HG):
                    g.wait_ge(sem("dexp"), 4 * hg + h + 1)
                    g.tensor_tensor(AT[:, :, h, :], attnT[:, :, h, :],
                                    ustrict[:, :].unsqueeze(1).to_broadcast([P, NT, P]), ALU.mult)\
                        .then_inc(sem("dstrict"), 1)
                    g.tensor_tensor(attnT[:, :, h, :], attnT[:, :, h, :],
                                    tri[:, :].unsqueeze(1).to_broadcast([P, NT, P]), ALU.mult)\
                        .then_inc(sem("dincl"), 1)
                units.ahead(g, "low1", u0 + 20)
                g.wait_ge(sem("kk"), 4 * hg + 4)
                for l in range(LEVELS):
                    if l == 1:
                        units.ahead(g, "low1", u0 + 28)
                    for t in range(NT):
                        if l > 1:
                            banks.done(g, ("t1", hg, l - 1, t))
                        if l == 1:
                            g.wait_ge(sem("x1T"), NT * hg + t + 1)
                        g.tensor_tensor(heads(ATm[:, t, :]), AT[:, t], lm[:, l, :].unsqueeze(1).to_broadcast([P, HG, P]),
                                        ALU.mult).then_inc(sem("ATm"), 1)

        @block.vector
        def _(v):
            chain = Chain(v, sem("dveC"))
            v.wait_ge(sem("normf_in"), 16)
            k.gained(v, chain, "nf", 2, EPS1, gain[:, :])
            k.scale(v, chain, "nm", 3, EPS2)
            units.ahead(v, "low0", 0)
            evacuate_split(k, v, banks, "nm", prm2[:, 0:8], hTh, hTl)
            v.wait_ge(sem("rb_in"), 48)
            bank = banks.take(v, ("rw", 0))
            v.tensor_scalar(temp[:, TA, :], bank[0:8, 0:S], rb[:, 0:1], None, ALU.add)
            last = v.tensor_scalar(temp[:, TB, :], bank[0:8, S:2 * S], rb[:, 2:3], None, ALU.add)
            banks.release(last, ("rw", 0))
            v.wait_ge(sem("rows_ln"), 2)
            chain.mark(v.scalar_tensor_tensor(temp[:, TE, :], temp[:, TA, :], 0.0, temp[:, TC, :], ALU.min, ALU.subtract))
            chain(v.scalar_tensor_tensor(temp[:, TF, :], temp[:, TB, :], 0.0, temp[:, TD, :], ALU.max, ALU.add))
            chain(v.tensor_scalar(temp[:, TF, :], temp[:, TF, :], rb[:, 1:2], -1.0, ALU.mult, ALU.mult))
            chain(v.tensor_tensor_scan(temp[:, TA, :], ones[0:8, :], temp[:, TE, :], 0.0, ALU.mult, ALU.add))
            v.tensor_scalar(rowp[:, NEGC, :], temp[:, TA, :], -1.0, None, ALU.mult).then_inc(sem("negc"), 1)
            for t in range(NT):
                chain(v.tensor_tensor_scan(rowp[:, GC, t * P:(t + 1) * P], ones[0:8, 0:P],
                                           temp[:, TF, t * P:(t + 1) * P], 0.0, ALU.mult, ALU.add))
            v.tensor_scalar(temp[:, KD, 0:P], rowp[:, GC, 0:P], -1.0, rowp[:, GC, P - 1:P], ALU.mult, ALU.add)\
                .then_inc(sem("gc_rows"), 1)
            v.tensor_copy(temp[:, TC, 0:P], rowp[:, GC, 0:P]).then_inc(sem("gc_rows"), 1)
            v.wait_ge(sem("eg_rows"), 2)
            banks.moved(v, ("rw", 1))
            v.tensor_tensor(temp[:, BEG, P:S], temp[:, BEG, P:S], rowp[:, BETA, P:S], ALU.mult).then_inc(sem("beg"), 1)

            def conv(w, name, hg):
                for j in range(2):
                    bank = banks.take(v, (name, hg, j))
                    units.ahead(v, "low0", UNITS_GROUP * hg + 4 * w + 2 * j + 2)
                    for i in range(4):
                        for a in range(2):
                            ch = 8 * w + HG * hg + 2 * j + a
                            c = gT[:, w, 2 * j + a, :]
                            tap = prm2[:, 17 + 24 * (3 - i) + ch:18 + 24 * (3 - i) + ch]
                            if i == 0:
                                last = v.tensor_scalar(c, bank[:, a * S:(a + 1) * S], tap, None, ALU.mult)
                            else:
                                last = v.scalar_tensor_tensor(c[:, i:], bank[:, a * S:(a + 1) * S - i], tap, c[:, i:],
                                                              ALU.mult, ALU.add)
                            if i < 3:
                                chain.mark(last)
                        if i < 3:
                            chain.wait()
                    banks.release(last, (name, hg, j))

            for hg in range(2):
                if hg:
                    for j in range(2):
                        banks.done(v, ("oT", 0, j))
                conv(0, "gq", hg)
                conv(1, "gk", hg)
                if hg == 0:
                    bank = banks.take(v, "cols")
                    last = v.tensor_copy(cols[:, :, :], bank[:, 0:48].rearrange("p (a h) -> p a h", a=6))
                    banks.release(last, "cols")
                conv(2, "gv", hg)
                for j in range(4):
                    bank = banks.take(v, ("ss", hg, j))
                    wv = work[:, j // 2, j % 2, :]
                    v.tensor_scalar(wv, bank, EPS2, None, ALU.add).then_inc(sem("ss_eps"), 1)
                    v.wait_ge(sem("ss_root"), 4 * hg + j + 1)
                    chain(v.reciprocal(wv, wv))
                    part = gT[:, j // 2, 2 * (j % 2):2 * (j % 2) + 2, :]
                    last = v.scalar_tensor_tensor(part.rearrange("p h s -> p (h s)"), part.rearrange("p h s -> p (h s)"),
                                                  float(P) ** -0.5 if j < 2 else 1.0, wv, ALU.mult, ALU.mult)
                    banks.release(last, ("ss", hg, j))
                if hg == 0:
                    banks.moved(v, "cols")
                units.ahead(v, "low0", UNITS_GROUP * hg + 16)
                for h in range(HG):
                    bank = banks.take(v, ("rb", hg, h))
                    hh = HG * hg + h
                    for t in range(NT):
                        last = v.tensor_scalar(attnT[:, t, h, :], bank[:, t * P:(t + 1) * P], cols[:, t, hh:hh + 1], 0.0,
                                               ALU.subtract, ALU.min)
                    last.then_inc(sem("dlog"), 1)
                units.ahead(v, "low0", UNITS_GROUP * hg + 20)
                for h in range(HG):
                    v.wait_ge(sem("dstrict"), 4 * hg + h + 1)
                    v.wait_ge(sem("egb"), 4 * hg + h + 1)
                    rbk = banks.take(v, ("rb", hg, h))
                    last = v.tensor_tensor(AT[:, :, h, :], AT[:, :, h, :],
                                           rbk[:, S:2 * S].rearrange("p (t n) -> p t n", t=NT), ALU.mult)
                    banks.release(last, ("rb", hg, h))
                    banks.moved(v, ("rb", hg, h))
                    v.wait_ge(sem("dincl"), 4 * hg + h + 1)
                    bank = banks.take(v, ("kq", hg, h))
                    v.tensor_tensor(AT[:, :, h, :], AT[:, :, h, :],
                                    bank[:, 0:S].rearrange("p (t n) -> p t n", t=NT), ALU.mult).then_inc(sem("kk"), 1)
                    last = v.tensor_tensor(attnT[:, :, h, :], attnT[:, :, h, :],
                                           bank[:, S:2 * S].rearrange("p (t n) -> p t n", t=NT), ALU.mult)
                    banks.release(last, ("kq", hg, h))
                    v.tensor_tensor(egb[:, h, :], egb[:, h, :], gT[:, 0, h, P:S], ALU.mult).then_inc(sem("qdec"), 1)
                for t in range(NT):
                    bank = banks.take(v, ("kt", hg, t))
                    col = cols[:, 5 - t, HG * hg:HG * hg + HG]
                    last = v.tensor_tensor((kdec, kbg)[t][:, :, :], heads(bank), bcast(col, P), ALU.mult)
                    banks.release(last, ("kt", hg, t))
                for t in range(NT):
                    bank = banks.take(v, ("vt", hg, t))
                    last = v.tensor_tensor(vb[:, t], heads(bank), bcast(cols[:, 2 + t, HG * hg:HG * hg + HG], P), ALU.mult)
                    banks.release(last, ("vt", hg, t))
                for t in range(NT):
                    v.wait_ge(sem("ATm"), 2 * LEVELS * hg + t + 1)
                    v.tensor_tensor(XT[:, t], heads(ATm[:, t, :]), ident[:, :].unsqueeze(1).to_broadcast([P, HG, P]),
                                    ALU.add).then_inc(sem("x1T"), 1)
                units.ahead(v, "low0", UNITS_GROUP * hg + 28)
                for l in range(1, LEVELS):
                    for t in range(NT):
                        for w, buf in (("xx", X), ("xt", XT)):
                            if w == "xx" and l == LEVELS - 1:
                                continue
                            bank = banks.take(v, (w, hg, l, t))
                            if w == "xx":
                                banks.done(v, ("xt", hg, l, t))
                            banks.release(v.tensor_tensor(buf[:, t], buf[:, t], heads(bank), ALU.add), (w, hg, l, t))
                for h in range(HG):
                    bank = banks.take(v, ("lo", hg, h))
                    chain.mark(v.reduce_max(fmax[:, h, 0:1], bank[:, 0:P], AX.X))
                    chain(v.reduce_max(fmax[:, h, 1:2], bank[:, P:384], AX.X))
                    v.tensor_scalar(fmax[:, h, :], fmax[:, h, :], -1.0, None, ALU.mult).then_inc(sem("fmax"), 1)
                for h in range(HG):
                    banks.moved(v, ("lo", hg, h))
                    chain(v.reciprocal(fsum[:, h, :], fsum[:, h, :]))
                    v.tensor_scalar(prob[:, h, 0:P], prob[:, h, 0:P], fsum[:, h, 0:1], None, ALU.mult)
                    v.tensor_scalar(prob[:, h, P:384], prob[:, h, P:384], fsum[:, h, 1:2], None, ALU.mult)\
                        .then_inc(sem("prob"), 1)
                for t in range(NT):
                    bank = banks.take(v, ("o%d" % t, hg))
                    banks.release(v.tensor_copy(o[:, t], heads(bank)), ("o%d" % t, hg))
                    banks.moved(v, ("o%d" % t, hg))
                    chain(v.tensor_tensor(vb[:, t], o[:, t], o[:, t], ALU.mult))
                    chain(v.tensor_reduce(osum[:, t, :], vb[:, t], AX.X, ALU.add))
                v.tensor_scalar(osum[:, :, :], osum[:, :, :], 1.0 / P, EPS2, ALU.mult, ALU.add).then_inc(sem("o_mean"), 1)
                v.wait_ge(sem("o_root"), hg + 1)
                chain(v.reciprocal(osum[:, :, :], osum[:, :, :]))
                for t in range(NT):
                    chain.mark(v.tensor_tensor(o[:, t], o[:, t], bcast(osum[:, t, :], P), ALU.mult))
                chain.wait()
                for t in range(NT):
                    banks.moved(v, ("gz", hg, t))
                    v.tensor_tensor(o[:, t], o[:, t], heads(gz[:, t, :]), ALU.mult).then_inc(sem("o_done"), 1)
                for j in range(2):
                    bank = banks.take(v, ("oT", hg, j))
                    last = v.tensor_scalar(ygT[:, HG * hg + 2 * j:HG * hg + 2 * j + 2, :],
                                           bank.rearrange("p (h s) -> p h s", h=2), prm2[:, 16:17], None, ALU.mult)
                    banks.release(last, ("oT", hg, j))

        @block.tensor
        def _(pe):
            def both_f(u, name, hg):
                columns(pe, units, banks, u, [(name, hg, j) for j in range(2)], hTh, hTl)

            def both_t(u, name, hg):
                rows(pe, units, banks, u, [(name, hg, t) for t in range(NT)], hTh, hTl)

            k.transposes(pe, banks, "nm")
            pe.wait_ge(sem("wg2_in"), 32)
            for j in range(4):
                banks.moved(pe, ("nm", j))
            for b, parts in ((0, (0, 8)), (1, (16,))):
                bank = banks.claim(pe, ("rw", b))
                for i, w0 in enumerate(parts):
                    for c in range(KC):
                        last = pe.matmul(bank[0:8, i * S:(i + 1) * S], wg2[:, c, w0:w0 + 8], hT[:, c, :],
                                         start=c == 0, stop=c == KC - 1)
                banks.filled(last, ("rw", b))
            pe.wait_ge(sem("nm_low"), 4)
            for hg in range(2):
                u0 = UNITS_GROUP * hg
                both_f(u0 + 0, "gq", hg)
                both_f(u0 + 4, "gk", hg)
                if hg == 0:
                    pe.wait_ge(sem("beg"), 1)
                    bank = banks.claim(pe, "cols")
                    for i, r in enumerate((rowp[:, GC, 0:P], rowp[:, GC, P:S], rowp[:, BETA, 0:P], rowp[:, BETA, P:S],
                                           temp[:, BEG, P:S], temp[:, KD, 0:P])):
                        last = pe.transpose(bank[:, 8 * i:8 * i + 8], r, ident[0:8, 0:8])
                    banks.filled(last, "cols")
                both_f(u0 + 8, "gv", hg)
                for j in range(4):
                    pe.wait_ge(sem("g_sq"), 4 * hg + j + 1)
                    bank = banks.claim(pe, ("ss", hg, j))
                    banks.filled(pe.matmul(bank, ones[:, 0:P], sq[:, j % 2, :], start=True, stop=True), ("ss", hg, j))
                both_f(u0 + 12, "fq", hg)
                pe.wait_ge(sem("negc"), 1)
                for h in range(HG):
                    bank = banks.claim(pe, ("rb", hg, h))
                    pe.matmul(bank[:, 0:S], sel[:, HG * hg + h, :], rowp[:, GC, :], start=True, stop=True)
                    last = pe.matmul(bank[:, S:2 * S], sel[:, HG * hg + h, :], rowp[:, BETA, :], start=True, stop=True)
                    banks.filled(last, ("rb", hg, h))
                both_f(u0 + 16, "fk", hg)
                for j in range(4):
                    banks.moved(pe, ("ss", hg, j))
                for h in range(HG):
                    bank = banks.claim(pe, ("kq", hg, h))
                    for i in (0, 1):
                        for t in range(NT):
                            c = slice(t * P, (t + 1) * P)
                            last = pe.matmul(bank[:, i * S + t * P:i * S + (t + 1) * P], gT[:, 1, h, c],
                                             gT[:, 1 - i, h, c], start=True, stop=True)
                    banks.filled(last, ("kq", hg, h))
                for w, name in ((1, "kt"), (2, "vt")):
                    if w == 2:
                        pe.wait_ge(sem("g_silu"), 6 * hg + 6)
                    for t in range(NT):
                        bank = banks.claim(pe, (name, hg, t))
                        for h in range(HG):
                            last = pe.transpose(bank[:, h * P:(h + 1) * P], gT[:, w, h, t * P:(t + 1) * P], ident[:, :])
                        banks.filled(last, (name, hg, t))
                for t in range(NT):
                    pe.wait_ge(sem("x1T"), NT * hg + t + 1)
                    bank = banks.claim(pe, ("x1", hg, t))
                    for h in range(HG):
                        last = pe.transpose(bank[:, h * P:(h + 1) * P], XT[:, t, h, :], ident[:, :])
                    banks.filled(last, ("x1", hg, t))
                both_t(u0 + 20, "fv", hg)
                both_t(u0 + 24, "gz", hg)
                for l in range(1, LEVELS):
                    for t in range(NT):
                        pe.wait_ge(sem("ATm"), 2 * LEVELS * hg + 2 * l + t + 1)
                        if l == 1:
                            banks.moved(pe, ("x1", hg, t))
                        else:
                            banks.moved(pe, ("xx", hg, l - 1, t))
                        bank = banks.claim(pe, ("t1", hg, l, t))
                        for h in range(HG):
                            last = pe.matmul(bank[:, h * P:(h + 1) * P], ATm[:, t, h * P:(h + 1) * P], X[:, t, h, :],
                                             start=True, stop=True)
                        banks.filled(last, ("t1", hg, l, t))
                    for t in range(NT):
                        banks.moved(pe, ("t1", hg, l, t))
                        if l > 1:
                            banks.moved(pe, ("xt", hg, l - 1, t))
                        if l < LEVELS - 1:
                            bank = banks.claim(pe, ("xx", hg, l, t))
                            for h in range(HG):
                                last = pe.matmul(bank[:, h * P:(h + 1) * P], XT[:, t, h, :], T1[:, t, h * P:(h + 1) * P],
                                                 start=True, stop=True)
                            banks.filled(last, ("xx", hg, l, t))
                        bank = banks.claim(pe, ("xt", hg, l, t))
                        for h in range(HG):
                            last = pe.matmul(bank[:, h * P:(h + 1) * P], T1[:, t, h * P:(h + 1) * P], XT[:, t, h, :],
                                             start=True, stop=True)
                        banks.filled(last, ("xt", hg, l, t))
                for j in range(2):
                    banks.moved(pe, ("fq", hg, j))
                    banks.moved(pe, ("fk", hg, j))
                pe.wait_ge(sem("consts2"), 1)
                for h in range(HG):
                    bank = banks.claim(pe, ("lo", hg, h))
                    for t in range(NT):
                        c = bank[:, 0:P] if t == 0 else bank[:, P:384]
                        pe.matmul(c, fqk[:, 0, h, t * P:(t + 1) * P], fqk[:, 1, h, 0:(t + 1) * P], start=True, stop=False)
                        pe.matmul(c, sel[:, HG * hg + h, :], rowp[:, NEGC, 0:(t + 1) * P], start=False, stop=False)
                        last = pe.matmul(c[:, t * P:(t + 1) * P], ident[:, :], negmask[:, :], start=False, stop=True)
                    banks.filled(last, ("lo", hg, h))
                for t in range(NT):
                    banks.moved(pe, ("kt", hg, t))
                    banks.moved(pe, ("vt", hg, t))
                    banks.moved(pe, ("xt", hg, LEVELS - 1, t))

                def per_head(key, *terms):
                    bank = banks.claim(pe, key)
                    for h in range(HG):
                        for i, (a, b) in enumerate(terms):
                            last = pe.matmul(bank[:, h * P:(h + 1) * P], a[:, h, :], b[:, h, :], start=i == 0,
                                             stop=i == len(terms) - 1)
                    banks.filled(last, key)

                per_head(("u0", hg), (XT[:, 0], vb[:, 0]))
                per_head(("wT", hg), (kbg, XT[:, 1]))
                banks.moved(pe, ("u0", hg))
                per_head(("st", hg), (kdec, u[:, 0]))
                for h in range(HG):
                    banks.moved(pe, ("kq", hg, h))
                per_head(("o0", hg), (attnT[:, 0], u[:, 0]))
                banks.moved(pe, ("wT", hg))
                banks.moved(pe, ("st", hg))
                per_head(("u1", hg), (XT[:, 1], vb[:, 1]), (wTn, state))
                for h in range(HG):
                    pe.wait_ge(sem("prob"), 4 * hg + h + 1)
                    bank = banks.claim(pe, ("pt", hg, h))
                    pe.transpose(bank[:, 0:P], prob[:, h, 0:P], ident[:, :])
                    pe.transpose(bank[:, P:S], prob[:, h, P:S], ident[:, :])
                    last = pe.transpose(bank[:, S:384], prob[:, h, S:384], ident[:, :])
                    banks.filled(last, ("pt", hg, h))
                banks.moved(pe, ("u1", hg))
                pe.wait_ge(sem("qdec"), 4 * hg + 4)
                per_head(("o1", hg), (egb, state), (attnT[:, 1], u[:, 1]))
                for t in range(NT):
                    banks.moved(pe, ("fv", hg, t))
                for j in range(2):
                    bank = banks.claim(pe, ("pv", hg, j))
                    for h in (2 * j, 2 * j + 1):
                        banks.moved(pe, ("pt", hg, h))
                        c = bank[:, (h % 2) * S:(h % 2 + 1) * S]
                        pe.matmul(c, fv[:, 0, h * P:(h + 1) * P], probT[:, h, 0:S], start=True, stop=False)
                        last = pe.matmul(c[:, P:S], fv[:, 1, h * P:(h + 1) * P], probT[:, h, S:384], start=False, stop=True)
                    banks.filled(last, ("pv", hg, j))
                pe.wait_ge(sem("o_done"), NT * hg + NT)
                for j in range(2):
                    bank = banks.claim(pe, ("oT", hg, j))
                    for i in range(2):
                        for t in range(NT):
                            last = pe.transpose(bank[:, i * S + t * P:i * S + (t + 1) * P], o[:, t, 2 * j + i, :], ident[:, :])
                    banks.filled(last, ("oT", hg, j))


def phase_e(nc, A, sem, sb, ring, banks, k, env):
    x, units, hTh, hTl, yfT, ygT = (env[n] for n in "x units hTh hTl yfT ygT".split())
    parts = {(w, p): sb("y%s_%s" % (w, p), [P, KC, S], F32R) for w in "fg" for p in ("high", "low")}
    mix_high = sb("mix_high", [P, KC, S], F32R)
    mix_low = sb("mix_low", [P, KC, S], F32R)
    sgf = sb("sgf", [P, 2, 512])
    sgg = sb("sgg", [P, 2, 512])
    part = sb("part", [P, 2, 512])

    for n in range(2):
        banks.plan(*[(w, n, j) for w in ("gf", "bf", "gg", "bg") for j in range(2)])
    banks.plan(*[("out", n, t) for n in range(2) for t in range(NT)])

    def flat(ap, n, j):
        return ap[:, 4 * n + 2 * j:4 * n + 2 * j + 2, :].rearrange("p h s -> p (h s)")

    with nc.Block() as block:
        @block.sync
        def _(sp):
            for g in range(16, UP0 + 2):
                units.freed(sp, g - 2)
                if g < UP0:
                    load_c(sp, A, ring, g)
                else:
                    load_up(sp, A, ring, g - UP0)

        @block.scalar
        def _(act):
            units.ahead(act, "high", UNITS_E)
            for w, y in (("f", yfT), ("g", ygT)):
                for h in range(2):
                    c = slice(4 * h, 4 * h + 4)
                    act.copy(parts[w, "high"][:, c, :], y[:, c, :]).then_inc(sem("y_high"), 1)
            for n in range(2):
                for i, (w, buf) in enumerate((("gf", sgf), ("gg", sgg))):
                    for j in range(2):
                        units.ahead(act, "high", UNITS_E + 16 * n + 8 * i + 2 * j + 2)
                        bank = banks.take(act, (w, n, j))
                        if n and w == "gf":
                            banks.moved(act, ("bf", 0, j))
                        if n and w == "gg":
                            act.wait_ge(sem("mixed"), j + 1)
                        banks.release(act.activation(buf[:, j, :], bank, ACT.Sigmoid), (w, n, j))
                    for j in range(2):
                        units.ahead(act, "high", UNITS_E + 16 * n + 8 * i + 4 + 2 * j + 2)
                        if w == "gg":
                            act.wait_ge(sem("mixed"), 2 * n + j + 1)
                            act.copy(flat(mix_high, n, j), part[:, j, :]).then_inc(sem("mix_high"), 1)
            units.ahead(act, "high", UNITS_OUT + 8)

        @block.gpsimd
        def _(g):
            for i, (w, y) in enumerate((("f", yfT), ("g", ygT))):
                for h in range(2):
                    if w == "g" and h == 0:
                        units.ahead(g, "low1", UNITS_E + 2)
                    g.wait_ge(sem("y_high"), 2 * i + h + 1)
                    c = slice(4 * h, 4 * h + 4)
                    g.tensor_tensor(parts[w, "low"][:, c, :], y[:, c, :], parts[w, "high"][:, c, :].bitcast(F32),
                                    ALU.subtract).then_inc(sem("y_low"), 1)
            units.ahead(g, "low1", UNITS_OUT + 8)

        @block.vector
        def _(v):
            def ahead(n):
                units.ahead(v, "low0", n)

            ahead(UNITS_E)
            for n in range(2):
                u0 = UNITS_E + 16 * n
                for j in range(2):
                    ahead(u0 + 4 + 2 * j + 2)
                    bank = banks.take(v, ("bf", n, j))
                    banks.moved(v, ("gf", n, j))
                    if n:
                        v.wait_ge(sem("mix_low"), j + 1)
                    banks.release(v.tensor_tensor(part[:, j, :], sgf[:, j, :], bank, ALU.mult), ("bf", n, j))
                for j in range(2):
                    ahead(u0 + 12 + 2 * j + 2)
                    bank = banks.take(v, ("bg", n, j))
                    banks.moved(v, ("gg", n, j))
                    last = v.tensor_tensor(sgg[:, j, :], sgg[:, j, :], bank, ALU.mult)
                    banks.release(last, ("bg", n, j))
                    banks.moved(v, ("bg", n, j))
                    v.tensor_tensor(part[:, j, :], part[:, j, :], sgg[:, j, :], ALU.add).then_inc(sem("mixed"), 1)
                for j in range(2):
                    v.wait_ge(sem("mix_high"), 2 * n + j + 1)
                    v.tensor_tensor(flat(mix_low, n, j), part[:, j, :], flat(mix_high, n, j).bitcast(F32),
                                    ALU.subtract).then_inc(sem("mix_low"), 1)
            for n in range(2):
                for t in range(NT):
                    ahead(UNITS_OUT + 4 * n + 3 + t)
                    bank = banks.take(v, ("out", n, t))
                    xs = x[:, t, n * 512:(n + 1) * 512]
                    banks.release(v.tensor_tensor(xs, xs, bank, ALU.add), ("out", n, t))

        @block.tensor
        def _(pe):
            for n in range(2):
                u0 = UNITS_E + 16 * n
                for i, w in enumerate(("gf", "bf", "gg", "bg")):
                    if n == 0 and i % 2:
                        pe.wait_ge(sem("y_low"), i + 1)
                    xh, xl = (hTh, hTl) if i % 2 == 0 else (parts["fg"[i // 2], "high"], parts["fg"[i // 2], "low"])
                    columns(pe, units, banks, u0 + 4 * i, [(w, n, j) for j in range(2)], xh, xl)
            pe.wait_ge(sem("mix_low"), 4)
            for n in range(2):
                rows(pe, units, banks, UNITS_OUT + 4 * n, [("out", n, t) for t in range(NT)], mix_high, mix_low)


def phase_d(nc, A, out, sem, sb, ring, banks, k, env):
    x, xn, hT, ident, prm2, gain, prow1, prow2, units, hTh, hTl = (
        env[n] for n in "x xn hT ident prm2 gain prow1 prow2 units hTh hTl".split())
    act_high = sb("act_high", [P, FF_CHUNKS, S], F32R)
    act_low = sb("act_low", [P, FF_CHUNKS, S], F32R)
    taps = sb("taps", [P, 2, 3 * FF_CHUNKS])
    cv = sb("cv", [P, 2, 2, 2, S])
    res = xn
    U0 = 4 * UP0
    UD = U0 + 4 * NUP
    prow = (prow1, prow2)

    banks.plan("taps", *[("nn", j) for j in range(4)])
    for j in range(NUP):
        banks.plan(("up", j, 0), ("up", j, 1))
    banks.plan(*[("dn", t, n) for t in range(NT) for n in range(2)])

    with nc.Block() as block:
        @block.sync
        def _(sp):
            sp.dma_start(gain[:, :], A["norm_final_2"].unsqueeze(0).to_broadcast([P, D])).then_inc(sem("norm_final_in"), 16)
            for g in range(UP0 + 2, DOWN0 + NDOWN):
                units.freed(sp, g - 2)
                if g < DOWN0:
                    load_up(sp, A, ring, g - UP0)
                else:
                    load_down(sp, A, ring, g - DOWN0)
            for t in range(NT):
                sp.wait_ge(sem("norm_scaled"), NT * (k.nth("fin") - 1) + t + 1)
                sp.dma_start(out[0, t * P:(t + 1) * P, :], res[:, t, :]).then_inc(sem("out_stored"), 16)
            sp.wait_ge(sem("out_stored"), 16 * NT)

        @block.scalar
        def _(act):
            for h in range(2):
                for i in range(3):
                    act.dma_start(prow[h][FF_CHUNKS * i:FF_CHUNKS * (i + 1), :],
                                  A["ffn_conv_w_2"][0, i, h * FF_CHUNKS * P:(h + 1) * FF_CHUNKS * P]
                                  .rearrange("(c p) -> c p", p=P)).then_inc(sem("taps_in"), 16)
            flat = hT[:, :, :].rearrange("p (t c) n -> p t (c n)", t=NT)
            k.squares(act, "nn", 0, flat)
            k.root(act, "nn", 0)
            units.ahead(act, "high", U0)
            high_parts(k, act, banks, "nn", hTh)
            for j in range(NUP):
                units.ahead(act, "high", U0 + 4 * j + 2)
                banks.moved(act, ("up", j, 0))
                act.activation(cv[:, j % 2, 0], cv[:, j % 2, 0], ACT.Silu).then_inc(sem("up_silu"), 1)
                if j:
                    act.wait_ge(sem("up_act"), j)
                    act.copy(act_high[:, 2 * j - 2:2 * j, :], cv[:, (j - 1) % 2, 1]).then_inc(sem("act_high"), 1)
                units.ahead(act, "high", U0 + 4 * j + 4)
            act.wait_ge(sem("up_act"), NUP)
            act.copy(act_high[:, 2 * NUP - 2:2 * NUP, :], cv[:, (NUP - 1) % 2, 1]).then_inc(sem("act_high"), 1)
            units.ahead(act, "high", len(units.units))
            act.wait_ge(sem("down_added"), 4)
            k.squares(act, "fin", 1, flat)
            k.root(act, "fin", 1)

        @block.gpsimd
        def _(g):
            units.ahead(g, "low1", U0 + 4)
            for j in range(NUP):
                units.ahead(g, "low1", U0 + 4 * j + 4)
                g.wait_ge(sem("act_high"), j + 1)
                g.tensor_tensor(act_low[:, 2 * j:2 * j + 2, :], cv[:, j % 2, 1],
                                act_high[:, 2 * j:2 * j + 2, :].bitcast(F32), ALU.subtract).then_inc(sem("act_low"), 1)
            units.ahead(g, "low1", len(units.units))

        @block.vector
        def _(v):
            chain = Chain(v, sem("dveD"))
            k.scale(v, chain, "nn", 0, EPS2)
            bank = banks.take(v, "taps")
            last = v.tensor_copy(taps[:, :, :], bank[:, 0:6 * FF_CHUNKS].rearrange("p (h n) -> p h n", h=2))
            banks.release(last, "taps")
            units.ahead(v, "low0", U0)
            evacuate_split(k, v, banks, "nn", prm2[:, 8:16], hTh, hTl)
            banks.moved(v, "taps")
            for j in range(NUP):
                if j >= 2:
                    v.wait_ge(sem("act_low"), j - 1)
                for h in range(2):
                    units.ahead(v, "low0", U0 + 4 * j + 2 * h + 2)
                    bank = banks.take(v, ("up", j, h))
                    for i in range(3):
                        for a in range(2):
                            c = cv[:, j % 2, h, a, :]
                            w = taps[:, h, FF_CHUNKS * (2 - i) + 2 * j + a:FF_CHUNKS * (2 - i) + 2 * j + a + 1]
                            if i == 0:
                                last = v.tensor_scalar(c, bank[:, a * S:(a + 1) * S], w, None, ALU.mult)
                            else:
                                last = v.scalar_tensor_tensor(c[:, i:], bank[:, a * S:(a + 1) * S - i], w, c[:, i:],
                                                              ALU.mult, ALU.add)
                            if i < 2:
                                chain.mark(last)
                            elif a == 0:
                                last.then_inc(sem("up_conv_first"), 1)
                        if i < 2:
                            chain.wait()
                    banks.release(last, ("up", j, h))
                banks.moved(v, ("up", j, 1))
                v.wait_ge(sem("up_silu"), j + 1)
                v.tensor_tensor(cv[:, j % 2, 1], cv[:, j % 2, 0], cv[:, j % 2, 1], ALU.mult)\
                    .then_inc(sem("up_act"), 1)
            units.ahead(v, "low0", len(units.units))
            for t in range(NT):
                for n in range(2):
                    bank = banks.take(v, ("dn", t, n))
                    xs = x[:, t, n * 512:(n + 1) * 512]
                    v.tensor_tensor(xs, xs, bank, ALU.add).then_inc(sem("down_added"), 1)
            v.wait_ge(sem("norm_final_in"), 16)
            k.gained(v, chain, "fin", 1, EPS2, gain[:, :], res)

        @block.tensor
        def _(pe):
            pe.wait_ge(sem("taps_in"), 16 * 6)
            bank = banks.claim(pe, "taps")
            for h in range(2):
                n = 3 * FF_CHUNKS
                last = pe.transpose(bank[:, h * n:(h + 1) * n], prow[h][0:n, :], ident[0:n, 0:n])
            banks.filled(last, "taps")
            k.transposes(pe, banks, "nn")
            pe.wait_ge(sem("nn_low"), 4)
            for j in range(NUP):
                columns(pe, units, banks, U0 + 4 * j, [("up", j, h) for h in range(2)], hTh, hTl)
            pe.wait_ge(sem("act_low"), NUP)
            dn = {(t, n): banks.claim(pe, ("dn", t, n)) for t in range(NT) for n in range(2)}
            for c in range(FF_CHUNKS):
                u = UD + c
                units.ready(pe, u)
                for t in range(NT):
                    a = slice(t * P, (t + 1) * P)
                    for n in range(2):
                        wh = units.buf(units.high, u)[:, n * 512:(n + 1) * 512]
                        wl = units.buf(units.low, u)[:, n * 512:(n + 1) * 512]
                        pe.matmul(dn[t, n], act_high[:, c, a], wh, start=c == 0, stop=False)
                        pe.matmul(dn[t, n], act_high[:, c, a], wl, start=False, stop=False)
                        last = pe.matmul(dn[t, n], act_low[:, c, a], wh, start=False, stop=c == FF_CHUNKS - 1)
                        if c == FF_CHUNKS - 1 and (t, n) != (1, 1):
                            banks.filled(last, ("dn", t, n))
                units.finish(last, u)


INS = ("x norm1_g w_in ig_b fg_b conv_w head_norm_g pool_w pool_scale w_out norm2_g w_router b_router w_gate "
       "b_gate w_up b_up w_down b_down normf_g norm_mix_2 w_in_2 fox_f_bias_2 gdn_conv_w_2 gdn_a_log_2 "
       "gdn_dt_bias_2 gdn_norm_2 w_branch_fox_2 w_branch_gdn_2 w_out_2 norm_ffn_2 w_up_2 ffn_conv_w_2 w_down_2 "
       "norm_final_2").split()


def kernel(**inputs):
    import concourse.bacc as bacc
    from concourse.bass_utils import run_bass_kernel_spmd

    nc = bacc.Bacc("TRN2", target_bir_lowering=False, num_devices=1)
    arrays, A = {}, {}
    for name in INS:
        a = np.ascontiguousarray(inputs[name])
        arrays[f"in_{name}"] = a
        A[name] = nc.dram_tensor(f"in_{name}", a.shape, mybir.dt.from_np(a.dtype), kind="ExternalInput").ap()
    out = nc.dram_tensor("out", (1, S, D), F32, kind="ExternalOutput").ap()
    build(nc, A, out)
    r = run_bass_kernel_spmd(nc, [arrays], core_ids=[0])
    return r.results[0]["out"]
```

```python
from contextlib import ExitStack

import numpy as np
import concourse.bass as bass
from concourse import mybir

F32 = mybir.dt.float32
F32R = mybir.dt.float32r
I32 = mybir.dt.int32
U32 = mybir.dt.uint32
ALU = mybir.AluOpType
ACT = mybir.ActivationFunctionType
AX = mybir.AxisListType

P = 128
D = 1024
S = 256
NT = S // P
KC = D // P
SLOTS = 6
PIECE = 4096
NH = 4
NE = 32
TOPK = 4
CAP = 64
EPS1 = 1e-5
EPS2 = 1e-6


class Ring:

    def __init__(self, sem, tag, buf, first=0, slots=SLOTS):
        self.buf, self.slots = buf, slots
        self.loaded = [sem(f"{tag}_loaded{s}") for s in range(slots)]
        self.first = first

    def nth(self, g):
        s = g % self.slots
        return (g - (s if s >= self.first else s + self.slots)) // self.slots

    def slot(self, g):
        s = g % self.slots
        return self.buf[0][:, s, :] if s < 2 else self.buf[1][:, s - 2, :]

    def load(self, eng, g, dst, src):
        eng.dma_start(dst, src).then_inc(self.loaded[g % self.slots], 16)

    def landed(self, pe, g):
        pe.wait_ge(self.loaded[g % self.slots], 16 * (self.nth(g) + 1))


class Banks:

    def __init__(self, sem, tag, ps):
        self.ps = ps
        self.full = [sem(f"{tag}_full{b}") for b in range(8)]
        self.free = [sem(f"{tag}_free{b}") for b in range(8)]
        self.uses = [0] * 8
        self.at = {}
        self.turn = 0

    def plan(self, *keys):
        for key in keys:
            b = self.turn % 8
            self.turn += 1
            self.at[key] = (b, self.uses[b])
            self.uses[b] += 1

    def claim(self, pe, key):
        b, n = self.at[key]
        if n > 0:
            pe.wait_ge(self.free[b], n)
        return self.ps[:, b, :]

    def filled(self, last, key):
        last.then_inc(self.full[self.at[key][0]], 1)

    def take(self, eng, key):
        b, n = self.at[key]
        eng.wait_ge(self.full[b], n + 1)
        return self.ps[:, b, :]

    def release(self, last, key):
        last.then_inc(self.free[self.at[key][0]], 1)

    def moved(self, eng, key):
        b, n = self.at[key]
        eng.wait_ge(self.free[b], n + 1)

    def done(self, eng, key):
        self.take(eng, key)


class Units:

    BUFS = 4

    def __init__(self, sem, ring, banks, high, low):
        self.sem, self.ring, self.banks, self.high, self.low = sem, ring, banks, high, low
        self.units = []
        self.emitted = {}

    def plan(self, g, kind, keys):
        for q, key in enumerate(keys):
            self.units.append((g, kind, q, key))

    def raw(self, u):
        g, kind, q, _ = self.units[u]
        p = self.ring.slot(g)
        if kind == "columns":
            return p.rearrange("p (c n) -> p c n", c=KC)[:, :, q * P:(q + 1) * P]
        if kind == "up":
            return p.rearrange("p (c h n) -> p c h n", c=KC, h=2)[:, :, q // 2, (q % 2) * P:(q % 2 + 1) * P]
        return p[:, q * D:(q + 1) * D].rearrange("p (c n) -> p c n", c=KC)

    def buf(self, which, u):
        return which[:, u % self.BUFS, :]

    def unnamed(self, u):
        return sum(self.units[w][3] is None for w in range(u + 1))

    def used(self, eng, u):
        key = self.units[u][3]
        if key is None:
            eng.wait_ge(self.sem("unit_used"), self.unnamed(u))
        else:
            self.banks.done(eng, key)

    def finish(self, last, u):
        key = self.units[u][3]
        if key is None:
            last.then_inc(self.sem("unit_used"), 1)
        else:
            self.banks.filled(last, key)

    def ahead(self, eng, who, n):
        for u in range(self.emitted.get(who, 0), min(n + self.BUFS, len(self.units))):
            self.emitted[who] = u + 1
            g, _, q, _ = self.units[u]
            hi = self.buf(self.high, u).rearrange("p (c n) -> p c n", c=KC)
            lo = self.buf(self.low, u).rearrange("p (c n) -> p c n", c=KC)
            if who == "high":
                if u >= self.BUFS:
                    self.used(eng, u - self.BUFS)
                eng.wait_ge(self.ring.loaded[g % self.ring.slots], landed_c(g))
                eng.copy(hi, self.raw(u)).then_inc(self.sem("high_split"), 1)
            elif who == ("low0", "low1")[u % 2]:
                eng.wait_ge(self.sem("high_split"), u + 1)
                eng.tensor_tensor(lo, self.raw(u), hi.bitcast(F32), ALU.subtract).then_inc(self.sem(who + "_split"), 1)

    def ready(self, pe, u):
        pe.wait_ge(self.sem("low%d_split" % (u % 2)), u // 2 + 1)

    def freed(self, sp, g):
        for who in (0, 1):
            n = sum(w[0] <= g for w in self.units[who::2])
            sp.wait_ge(self.sem("low%d_split" % who), n)


class Chain:

    def __init__(self, eng, sem, n=0):
        self.eng, self.sem, self.n = eng, sem, n

    def __call__(self, ins):
        self.n += 1
        ins.then_inc(self.sem, 1)
        self.wait()

    def mark(self, ins):
        self.n += 1
        ins.then_inc(self.sem, 1)

    def wait(self):
        self.eng.wait_ge(self.sem, self.n)


def bcast(ap, n):
    return ap.unsqueeze(2).to_broadcast([ap.shape[0], ap.shape[1], n])


def build(nc, A, out):
    top = ExitStack()
    sems = {}

    def sem(name):
        if name not in sems:
            sems[name] = top.enter_context(nc.semaphore(name))
        return sems[name]

    def sb(name, shape, dt=F32, stack=None):
        return (stack or top).enter_context(nc.sbuf_tensor(name, shape, dt))

    with top:
        ps = top.enter_context(nc.psum_tensor("ps", [P, 8, 512], F32))
        ring01 = sb("ring01", [P, 2, PIECE])
        x = sb("x", [P, NT, D])
        xn = sb("xn", [P, NT, D])
        hT = sb("hT", [P, KC, S])
        ident = sb("ident", [P, P])
        tri = sb("tri", [P, P])
        ustrict = sb("ustrict", [P, P])
        ones = sb("ones", [P, 2 * P])
        sel = sb("sel", [8, 8, P])
        stat = sb("stat", [P, 17])
        prow1 = sb("prow1", [P, P])
        prow2 = sb("prow2", [P, P])
        prm1 = sb("prm1", [P, P])
        prm2 = sb("prm2", [P, P])
        slot = sb("slot", [P, NT, NE])
        gate = sb("gate", [P, NT, NE])
        iota_cap = sb("iota_cap", [P, 2, CAP])
        passes = sb("passes", [1, 2], I32)
        gain = sb("gain", [P, D])
        ab = top.enter_context(ExitStack())
        ring25 = sb("ring25", [P, 4, PIECE], stack=ab)
        extra = sb("extra", [P, 2, PIECE], stack=ab)
        f8 = sb("f8", [P, NT, 8], stack=ab)
        e4 = sb("e4", [P, NT, TOPK], stack=ab)
        iota_e = sb("iota_e", [P, NE], stack=ab)
        brow = sb("brow", [1, 2, D], stack=ab)
        bdn = sb("bdn", [NE, D], stack=ab)
        ring = Ring(sem, "ringA", (ring01, ring25), first=5)
        pieces = Pieces(sem, ring, extra)
        banks = Banks(sem, "bankA", ps)
        k = Kit(nc, sem, ident, ones, stat, x, xn, hT)
        with ExitStack() as a:
            phase_a(nc, A, sem, lambda n, s, dt=F32: sb(n, s, dt, a), ring, banks, k, locals())
        ringC = Ring(sem, "ringC", (ring01,), slots=2)
        banksC = Banks(sem, "bankC", ps)
        with ExitStack() as b:
            phase_b(nc, A, sem, lambda n, s, dt=F32: sb(n, s, dt, b), ring, banks, locals())
        ab.close()
        high = sb("high", [P, Units.BUFS, D], F32R)
        low = sb("low", [P, Units.BUFS, D], F32R)
        hTh = sb("hTh", [P, KC, S], F32R)
        hTl = sb("hTl", [P, KC, S], F32R)
        units = Units(sem, ringC, banksC, high, low)
        plan_units(units)
        with ExitStack() as ce:
            yf = [sb("yf_" + w, [P, KC, S], F32R, ce) for w in ("high", "low")]
            yg = [sb("yg_" + w, [P, KC, S], F32R, ce) for w in ("high", "low")]
            with ExitStack() as c:
                phase_c(nc, A, sem, lambda n, s, dt=F32: sb(n, s, dt, c), ringC, banksC, k, locals())
            with ExitStack() as e:
                phase_e(nc, A, sem, lambda n, s, dt=F32: sb(n, s, dt, e), ringC, banksC, k, locals())
        with ExitStack() as d:
            phase_d(nc, A, out, sem, lambda n, s, dt=F32: sb(n, s, dt, d), ringC, banksC, k, locals())


P1 = dict(norm1_g=0, norm2_g=8, head_norm_g=16, pool_scale=20, conv_w=24)
P2 = dict(norm_mix_2=0, norm_ffn_2=8, gdn_norm_2=16, gdn_conv_w_2=17)


class Kit:

    def __init__(self, nc, sem, ident, ones, stat, x, xn, hT):
        self.nc, self.sem, self.ident, self.ones, self.stat = nc, sem, ident, ones, stat
        self.x, self.xn, self.hT = x, xn, hT

    @staticmethod
    def nth(tag):
        return ("n1", "n2", "nf", "nm", "nn", "fin").index(tag) + 1

    @staticmethod
    def squares_by(tag):
        return {"n1": 2, "n2": 4, "nf": 6, "nm": 8, "nn": 12, "fin": 16}[tag]

    def prepare(self, act):
        act.activation(self.stat[:, 16:17], self.ones[:, 0:1], ACT.Sqrt)

    def squares_of(self, act, t, h, n, junk):
        c = slice(h * D // 2, (h + 1) * D // 2)
        i = 4 * n + 2 * h + t
        act.activation(junk[:, t, c], self.x[:, t, c], ACT.Square, accum_out=self.stat[:, i:i + 1])\
            .then_inc(self.sem("norm_squares"), 1)

    def mean(self, v, chain, tag, c, r, eps):
        v.wait_ge(self.sem("norm_squares"), self.squares_by(tag))
        if tag in ("nn", "fin"):
            chain(v.tensor_tensor(c, c, r, ALU.add))
        v.tensor_scalar(c, c, 1.0 / D, eps, ALU.mult, ALU.add).then_inc(self.sem("norm_mean"), 1)
        v.wait_ge(self.sem("norm_root"), self.nth(tag))

    def squares(self, act, tag, n, junk, before=None):
        for t in range(NT):
            if before:
                before(t)
            act.activation(junk[:, t, :], self.x[:, t, :], ACT.Square,
                           accum_out=self.stat[:, 4 * n + t:4 * n + t + 1]).then_inc(self.sem("norm_squares"), 1)

    def root(self, act, tag, n):
        c = self.stat[:, 4 * n:4 * n + 2]
        act.wait_ge(self.sem("norm_mean"), self.nth(tag))
        act.activation(c, c, ACT.Sqrt).then_inc(self.sem("norm_root"), 1)

    def scale(self, v, chain, tag, n, eps):
        c = self.stat[:, 4 * n:4 * n + 2]
        r = self.stat[:, 4 * n + 2:4 * n + 4]
        self.mean(v, chain, tag, c, r, eps)
        chain(v.reciprocal(r, c))
        for t in range(NT):
            v.tensor_scalar(self.xn[:, t, :], self.x[:, t, :], r[:, t:t + 1], None, ALU.mult)\
                .then_inc(self.sem("norm_scaled"), 1)

    def gained(self, v, chain, tag, n, eps, gain, out=None):
        c = self.stat[:, 4 * n:4 * n + 2]
        r = self.stat[:, 4 * n + 2:4 * n + 4]
        self.mean(v, chain, tag, c, r, eps)
        chain(v.reciprocal(r, c))
        for t in range(NT):
            v.scalar_tensor_tensor((self.x if out is None else out)[:, t, :], self.x[:, t, :], r[:, t:t + 1],
                                   gain, ALU.mult, ALU.mult).then_inc(self.sem("norm_scaled"), 1)

    def transposes(self, pe, banks, tag):
        pe.wait_ge(self.sem("norm_scaled"), NT * self.nth(tag))
        for j in range(KC // 2):
            bank = banks.claim(pe, (tag, j))
            for c in (2 * j, 2 * j + 1):
                for t in range(NT):
                    o = (c % 2) * S + t * P
                    last = pe.transpose(bank[:, o:o + P], self.xn[:, t, c * P:(c + 1) * P], self.ident[:, :])
            banks.filled(last, (tag, j))

    def evacuate(self, v, banks, tag, g):
        for j in range(KC // 2):
            bank = banks.take(v, (tag, j))
            last = v.tensor_tensor(self.hT[:, 2 * j:2 * j + 2, :], bank.rearrange("p (c t) -> p c t", c=2),
                                   bcast(g[:, 2 * j:2 * j + 2], S), ALU.mult)
            banks.release(last, (tag, j))


EXPERT = 12


def load_biases(sp, A, brow, sem, e, parity):
    for m, name in enumerate(("b_gate", "b_up")):
        sp.dma_start(brow[0:1, m, :], A[name][0][bass.ds(e, 1), :]).then_inc(sem("brow%d_in" % parity), 16)


def load_extra(sp, A, ringX, p, e):
    w = A[("w_gate", "w_up")[p // 2]][0]
    ringX.load(sp, p, ringX.slot(p).rearrange("p (c n) -> p c n", c=4),
               w[bass.ds(e, 1), (p % 2) * 512:(p % 2 + 1) * 512, :].rearrange("a (c p) n -> p (a c) n", p=P))


class Pieces:

    SLOTS = 8
    ROUND = 4
    PER = 6

    def __init__(self, sem, ring, extra):
        self.loaded = ring.loaded + [sem("extra_loaded%d" % s) for s in range(2)]
        self.before = [ring.nth(EXPERT + s) for s in range(SLOTS)] + [0, 0]
        self.places = [ring.slot(EXPERT + s) for s in range(SLOTS)] + [extra[:, s, :] for s in range(2)]

    def slot(self, n):
        return self.places[n % self.SLOTS].rearrange("p (c n) -> p c n", c=4)

    def load(self, sp, A, n, e):
        m, h = n % self.PER // 2, n % 2
        sp.dma_start(self.slot(n), A[("w_gate", "w_up", "w_down")[m]][0][bass.ds(e, 1), h * 512:(h + 1) * 512, :]
                     .rearrange("a (c p) n -> p (a c) n", p=P)).then_inc(self.loaded[n % self.SLOTS], 16)

    def landed(self, pe, n, rnd):
        s, per_round = n % self.SLOTS, self.ROUND * self.PER // self.SLOTS
        pe.wait_ge(self.loaded[s], 16 * (self.before[s] + n // self.SLOTS + 1) + 16 * per_round * rnd)
        return self.slot(n)


def load_bias_down(sp, A, brow, sem, e):
    sp.dma_start(brow[0:1, 2, :], A["b_down"][0][bass.ds(e, 1), :]).then_inc(sem("bdown_in"), 16)


def load_half(sp, A, ring, m, h, e):
    g = EXPERT + 2 * m + h
    w = A[("w_gate", "w_up", "w_down")[m]][0]
    ring.load(sp, g, ring.slot(g).rearrange("p (c n) -> p c n", c=4),
              w[bass.ds(e, 1), h * 512:(h + 1) * 512, :].rearrange("a (c p) n -> p (a c) n", p=P))


def evacuate_split(k, v, banks, tag, g, high, low):
    def low_part(j):
        v.wait_ge(k.sem(tag + "_high"), j + 1)
        c = slice(2 * j, 2 * j + 2)
        v.tensor_tensor(low[:, c, :], k.hT[:, c, :], high[:, c, :].bitcast(F32), ALU.subtract)\
            .then_inc(k.sem(tag + "_low"), 1)

    for j in range(KC // 2):
        bank = banks.take(v, (tag, j))
        last = v.tensor_tensor(k.hT[:, 2 * j:2 * j + 2, :], bank.rearrange("p (c t) -> p c t", c=2),
                               bcast(g[:, 2 * j:2 * j + 2], S), ALU.mult)
        banks.release(last, (tag, j))
        if j:
            low_part(j - 1)
    low_part(KC // 2 - 1)


def high_parts(k, act, banks, tag, high):
    for j in range(KC // 2):
        banks.moved(act, (tag, j))
        act.copy(high[:, 2 * j:2 * j + 2, :], k.hT[:, 2 * j:2 * j + 2, :]).then_inc(k.sem(tag + "_high"), 1)


def phase_a(nc, A, sem, sb, ring, banks, k, env):
    x, xn, hT, ident, tri, ustrict, ones, sel = (env[n] for n in "x xn hT ident tri ustrict ones sel".split())
    prow1, prow2, prm1, prm2, slot, iota_cap, passes, brow, f8, e4, iota_e = (
        env[n] for n in "prow1 prow2 prm1 prm2 slot iota_cap passes brow f8 e4 iota_e".split())
    pieces, extra = env["pieces"], env["extra"]
    W = NH * P

    def part(slot, at, *shape):
        n = int(np.prod(shape))
        names = "abc"[:len(shape)]
        return extra[:, slot, at:at + n].rearrange("p (%s) -> p %s" % (" ".join(names), " ".join(names)),
                                                   **dict(zip(names, shape)))


    wg = sb("wg", [P, KC, 8])
    tok = sb("tok", [P, NT, 8])
    qkT = part(0, 0, 8, S)
    vext = sb("vext", [P, NT, NH, P + 1])
    og = part(1, 12 * S, NT, W)
    pa = part(1, 0, 4, S)
    pb = part(1, 4 * S, 4, S)
    inv = part(1, 8 * S, 4, S)
    tcount = sb("tcount", [P, S])
    yT = sb("yT", [P, KC, S])
    uT = yT[:, 0:4, :]
    DT = part(0, 8 * S, NT, NH, S)
    hm = qkT[:, 0:4, :].rearrange("p (t a) (b d) -> p t (a b) d", t=NT, b=2)
    den = sb("den", [P, NT, NH])
    bst = sb("bst", [P, NT * NH, 6])
    mv = sb("mv", [P, NT * NH, 2])
    rs = sb("rs", [P, NT * NH])
    rows = sb("rows", [4, 10, S])
    FX, AB, E, L, LF, B, C, M, NM, EM = range(10)
    gb = sb("gb", [4, 2])
    ccol = sb("ccol", [P, 16])
    pool_w = sb("pool_w", [P, 4, P])
    wr = sb("wr", [P, KC, NE])
    brt = sb("brt", [P, NE])
    lg = sb("lg", [P, NT, NE])
    v8 = sb("v8", [P, NT, 8])
    i8 = sb("i8", [P, NT, 8], U32)
    es = sb("es", [P, NT])
    mask = sb("mask", [P, NT, NE])
    cnt = sb("cnt", [1, NE])
    cm = sb("cm", [1, 4])

    w_in, w_out = A["w_in"][0], A["w_out"][0]
    IN_COLS = [0, W, 2 * W, 4 * W + 2 * NH, 3 * W]
    Q_, K_, V_, U_, O_, OUT0, OUT1 = range(5, 12)

    banks.plan("prm1", *[("n1", j) for j in range(4)], "gr", "gates", *[("qk", j) for j in range(4)],
               "cols", ("mb", 0), ("mb", 1), ("v", 0), ("v", 1), *[("sc", h) for h in range(NH)],
               ("u", 0), ("u", 1), ("o", 0), ("o", 1),
               *[("num", j, hp) for j in range(NT) for hp in range(2)],
               "prm2", ("pool", 0), ("pool", 1), *[("out", n, t) for n in range(2) for t in range(NT)],
               ("ym", 0), ("ym", 1),
               *[("n2", j) for j in range(4)], "lg", "rk")

    def piece(g):
        return ring.slot(g).rearrange("p (c n) -> p c n", c=KC)

    with nc.Block() as block:
        @block.sync
        def _(sp):
            sp.dma_start(x[:, :, :], A["x"][0].rearrange("(t p) d -> p t d", p=P)).then_inc(sem("x_in"), 16)
            for name, n in (("norm1_g", 8), ("norm2_g", 8), ("head_norm_g", 4), ("pool_scale", 4)):
                sp.dma_start(prow1[P1[name]:P1[name] + n, :],
                             A[name][0].rearrange("(c p) -> c p", p=P)).then_inc(sem("prow1_in"), 16)
            sp.dma_start(prow1[24:56, :], A["conv_w"][0].rearrange("i (c p) -> (i c) p", p=P))\
                .then_inc(sem("prow1_in"), 16)
            sp.dma_start(wg[:, :, :], w_in[:, 4 * W:4 * W + 8].rearrange("(c p) n -> p c n", p=P))\
                .then_inc(sem("wg_in"), 16)
            sp.dma_start(gb[:, 0:1], A["ig_b"].rearrange("a h -> h a")).then_inc(sem("gb_in"), 16)
            sp.dma_start(gb[:, 1:2], A["fg_b"].rearrange("a h -> h a")).then_inc(sem("gb_in"), 16)
            for j, c0 in enumerate(IN_COLS):
                ring.load(sp, Q_ + j, piece(Q_ + j), w_in[:, c0:c0 + 512].rearrange("(c p) n -> p c n", p=P))
            for n in range(2):
                if n == 1:
                    banks.done(sp, ("qk", 1))
                ring.load(sp, OUT0 + n, piece(OUT0 + n),
                          w_out[:, n * 512:(n + 1) * 512].rearrange("(c p) n -> p c n", p=P))
                if n == 0:
                    sp.dma_start(pool_w[:, :, :], A["pool_w"][0].rearrange("g c d -> c g d")).then_inc(sem("pool_w_in"), 16)
                    for name, m in (("norm_mix_2", 8), ("norm_ffn_2", 8), ("gdn_norm_2", 1)):
                        sp.dma_start(prow2[P2[name]:P2[name] + m, :],
                                     A[name][0].rearrange("(c p) -> c p", p=P)).then_inc(sem("prow2_in"), 16)
                    sp.dma_start(prow2[17:113, :], A["gdn_conv_w_2"][0].rearrange("i (c p) -> (i c) p", p=P))\
                        .then_inc(sem("prow2_in"), 16)
                    sp.dma_start(wr[:, :, :], A["w_router"][0].rearrange("(c p) n -> p c n", p=P)).then_inc(sem("wr_in"), 16)
                    sp.dma_start(brt[:, :], A["b_router"].to_broadcast([P, NE])).then_inc(sem("wr_in"), 16)
            load_biases(sp, A, brow, sem, 0, 0)
            sp.dma_start(env["bdn"][:, :], A["b_down"][0]).then_inc(sem("bdn_in"), 16)
            for n, use in ((0, ("qk", 3)), (1, ("v", 1)), (2, ("u", 1)), (3, ("o", 1)), (6, ("ym", 1)), (7, ("ym", 1)),
                           (4, ("out", 0, 1)), (5, ("out", 1, 1))):
                banks.done(sp, use)
                pieces.load(sp, A, n, n // 6)

        @block.scalar
        def _(act):
            act.wait_ge(sem("consts"), 1)
            k.prepare(act)
            act.wait_ge(sem("x_in"), 16)
            k.squares(act, "n1", 0, hT[:, :, :].rearrange("p (t c) n -> p t (c n)", t=NT))
            k.root(act, "n1", 0)
            bank = banks.take(act, "gr")
            banks.release(act.copy(tok[:, :, :], bank[:, 0:NT * 8].rearrange("p (t n) -> p t n", t=NT)), "gr")
            chain = Chain(act, sem("actA"))
            act.wait_ge(sem("fx"), 1)
            chain(act.activation(rows[:, AB, :], rows[:, FX, :], ACT.Abs))
            chain(act.activation(rows[:, E, :], rows[:, AB, :], ACT.Exp, scale=-1.0))
            act.activation(rows[:, L, :], rows[:, E, :], ACT.Ln, bias=1.0).then_inc(sem("ln1p"), 1)
            act.wait_ge(sem("nm"), 1)
            act.activation(rows[:, EM, :], rows[:, NM, :], ACT.Exp).then_inc(sem("em"), 1)
            for j in range(4):
                banks.moved(act, ("qk", j))
                act.activation(qkT[:, 2 * j:2 * j + 2, :], qkT[:, 2 * j:2 * j + 2, :], ACT.Silu)\
                    .then_inc(sem("qk_silu"), 1)
            banks.moved(act, ("mb", 0))
            banks.moved(act, ("mb", 1))
            for t in range(NT):
                act.activation(DT[:, t, :, t * P:], DT[:, t, :, t * P:], ACT.Exp).then_inc(sem("decay"), 1)
            for j in range(2):
                bank = banks.take(act, ("u", j))
                last = act.copy(uT[:, 2 * j:2 * j + 2, :], bank.rearrange("p (c t) -> p c t", c=2))
                banks.release(last, ("u", j))
            for t in range(NT):
                bank = banks.take(act, ("o", t))
                last = act.activation(og[:, t, :], bank, ACT.Sigmoid)
                banks.release(last, ("o", t))
            act.wait_ge(sem("hvar"), 1)
            act.activation(rs[:, :], rs[:, :], ACT.Sqrt).then_inc(sem("hroot"), 1)
            for g in range(4):
                if g % 2 == 0:
                    bank = banks.take(act, ("pool", g // 2))
                last = act.activation(yT[:, 4 + g, :], bank[:, (g % 2) * S:(g % 2 + 1) * S], ACT.Copy,
                                      scale=prm1[:, P1["pool_scale"] + g:P1["pool_scale"] + g + 1])
                if g % 2:
                    banks.release(last, ("pool", g // 2))
            k.prepare(act)

            def summed(t):
                for n in range(2):
                    banks.moved(act, ("out", n, t))

            k.squares(act, "n2", 1, hT[:, :, :].rearrange("p (t c) n -> p t (c n)", t=NT), summed)
            k.root(act, "n2", 1)
            act.wait_ge(sem("v8neg"), 1)
            for t in range(NT):
                act.activation(e4[:, t, :], v8[:, t, 0:4], ACT.Exp, bias=f8[:, t, 7:8],
                               accum_out=es[:, t:t + 1]).then_inc(sem("e4"), 1)

        @block.gpsimd
        def _(g):
            chain = Chain(g, sem("poolA"))
            chain.mark(g.memset(ones[:, :], 1.0))
            chain.mark(g.memset(vext[:, :, :, P:P + 1], 1.0))
            chain(g.memset(sel[:, :, :], 1.0))
            g.affine_select(out=ident[:, :], in_=ones[:, 0:P], compare_op=ALU.is_equal, fill=0.0, base=0,
                            pattern=[[-1, P]], channel_multiplier=1).then_inc(sem("consts"), 1)
            g.affine_select(out=tri[:, :], in_=ones[:, 0:P], compare_op=ALU.is_ge, fill=0.0, base=0,
                            pattern=[[1, P]], channel_multiplier=-1).then_inc(sem("consts"), 1)
            g.affine_select(out=ustrict[:, :], in_=ones[:, 0:P], compare_op=ALU.is_gt, fill=0.0, base=0,
                            pattern=[[1, P]], channel_multiplier=-1).then_inc(sem("consts"), 1)
            g.affine_select(out=sel[:, :, :], in_=sel[:, :, :], compare_op=ALU.is_equal, fill=0.0, base=0,
                            pattern=[[-1, 8], [0, P]], channel_multiplier=1).then_inc(sem("consts"), 1)
            g.iota(iota_cap[:, :, :], pattern=[[0, 2], [1, CAP]], base=0, channel_multiplier=0,
                   allow_small_or_imprecise_dtypes=True).then_inc(sem("consts"), 1)
            g.iota(iota_e[:, :], pattern=[[1, NE]], base=0, channel_multiplier=0,
                   allow_small_or_imprecise_dtypes=True).then_inc(sem("consts"), 1)
            g.iota(tcount[:, :], pattern=[[1, S]], base=1, channel_multiplier=0,
                   allow_small_or_imprecise_dtypes=True).then_inc(sem("tcount"), 1)
            for t in range(NT):
                g.wait_ge(sem("decay"), t + 1)
                g.tensor_tensor(DT[:, t, :, t * P:t * P + P], DT[:, t, :, t * P:t * P + P],
                                tri[:, :].unsqueeze(1).to_broadcast([P, NH, P]), ALU.mult)\
                    .then_inc(sem("decay_masked"), 1)
            for j in range(2):
                banks.moved(g, ("u", j))
            g.wait_ge(sem("inv"), 4)
            src = uT
            for n in range(4):
                dst = (pa, pb)[n % 2]
                w = 1 << n
                chain.mark(g.tensor_tensor(dst[:, n:, w:], src[:, n:, w:], src[:, n:, :S - w], ALU.add))
                chain(g.tensor_copy(dst[:, n:, 0:w], src[:, n:, 0:w]))
                src = dst
                chain(g.tensor_tensor(inv[:, n, :], inv[:, n, :], dst[:, n, :], ALU.mult))
            g.tensor_tensor(inv[:, :, :], inv[:, :, :], uT[:, :, :], ALU.subtract).then_inc(sem("pooled"), 1)

        @block.vector
        def _(v):
            chain = Chain(v, sem("dveA"))
            k.scale(v, chain, "n1", 0, EPS1)
            bank = banks.take(v, "prm1")
            last = v.tensor_copy(prm1[:, 0:56], bank[:, 0:56])
            banks.release(last, "prm1")
            banks.moved(v, "prm1")
            k.evacuate(v, banks, "n1", prm1[:, 0:8])
            v.wait_ge(sem("gb_in"), 32)
            bank = banks.take(v, "gates")
            v.tensor_scalar(rows[:, FX, :], bank[0:4, S:2 * S], gb[:, 1:2], None, ALU.add).then_inc(sem("fx"), 1)
            v.wait_ge(sem("tcount"), 1)
            chain(v.reciprocal(tcount[:, :], tcount[:, :]))
            for n in range(4):
                v.tensor_scalar(inv[:, n, :], tcount[:, :], 1.0 / (2 << n), None, ALU.max).then_inc(sem("inv"), 1)
            v.wait_ge(sem("ln1p"), 1)
            chain(v.scalar_tensor_tensor(rows[:, LF, :], rows[:, FX, :], 0.0, rows[:, L, :], ALU.min, ALU.subtract))
            v.wait_ge(sem("consts"), 6)
            chain(v.tensor_tensor_scan(rows[:, B, :], ones[0:4, :], rows[:, LF, :], 0.0, ALU.mult, ALU.add))
            last = v.scalar_tensor_tensor(rows[:, C, :], bank[0:4, 0:S], gb[:, 0:1], rows[:, B, :],
                                          ALU.add, ALU.subtract)
            banks.release(last, "gates")
            banks.moved(v, "gates")
            chain(v.tensor_tensor_scan(rows[:, M, :], rows[:, C, :], rows[:, C, :], 0.0, ALU.max, ALU.max))
            v.scalar_tensor_tensor(rows[:, NM, :], rows[:, M, :], -1.0, rows[:, B, :], ALU.mult, ALU.subtract)\
                .then_inc(sem("nm"), 1)
            v.tensor_scalar(rows[:, M, :], rows[:, M, :], -1.0, None, ALU.mult).then_inc(sem("negm"), 1)
            for j in range(4):
                bank = banks.take(v, ("qk", j))
                for i in range(4):
                    for c in (2 * j, 2 * j + 1):
                        o = (c % 2) * S
                        w = prm1[:, 24 + 8 * (3 - i) + c:25 + 8 * (3 - i) + c]
                        if i == 0:
                            last = v.tensor_scalar(qkT[:, c, :], bank[:, o:o + S], w, None, ALU.mult)
                        else:
                            last = v.scalar_tensor_tensor(qkT[:, c, i:], bank[:, o:o + S - i], w, qkT[:, c, i:],
                                                          ALU.mult, ALU.add)
                        if i < 3:
                            chain.mark(last)
                    if i < 3:
                        chain.wait()
                banks.release(last, ("qk", j))
            bank = banks.take(v, "cols")
            last = v.tensor_copy(ccol[:, :], bank[:, 0:16])
            banks.release(last, "cols")
            banks.moved(v, "cols")
            for h in range(NH):
                if h % 2 == 0:
                    bank = banks.take(v, ("mb", h // 2))
                for t in range(NT):
                    o = (h % 2) * S
                    last = v.tensor_scalar(DT[:, t, h, t * P:], bank[:, o + t * P:o + S],
                                           ccol[:, 4 * t + h:4 * t + h + 1], 0.0, ALU.add, ALU.min)
                if h % 2:
                    banks.release(last, ("mb", h // 2))
            for j in (2, 3):
                v.wait_ge(sem("qk_silu"), j + 1)
                v.tensor_scalar(qkT[:, 2 * j:2 * j + 2, :], qkT[:, 2 * j:2 * j + 2, :], float(P) ** -0.5, None,
                                ALU.mult).then_inc(sem("k_scaled"), 1)
            for t in range(NT):
                bank = banks.take(v, ("v", t))
                last = v.tensor_copy(vext[:, t, :, 0:P], bank.rearrange("p (h d) -> p h d", h=NH))
                banks.release(last, ("v", t))
            v.wait_ge(sem("decay_masked"), NT)
            for h in range(NH):
                bank = banks.take(v, ("sc", h))
                v.tensor_tensor(DT[:, 0, h, :], bank[:, 0:S], DT[:, 0, h, :], ALU.mult)
                last = v.tensor_tensor(DT[:, 1, h, P:], bank[:, S:S + P], DT[:, 1, h, P:], ALU.mult)
                banks.release(last, ("sc", h))
            for j in range(NT):
                for hp in range(2):
                    bank = banks.take(v, ("num", j, hp))
                    pair = bank[:, 0:2 * (P + 1)].rearrange("p (h d) -> p h d", h=2)
                    dd = den[:, j, 2 * hp:2 * hp + 2]
                    em = ccol[:, 8 + 4 * j + 2 * hp:8 + 4 * j + 2 * hp + 2].unsqueeze(2)
                    chain(v.scalar_tensor_tensor(dd.unsqueeze(2), pair[:, :, P:P + 1], -1.0, em, ALU.mult, ALU.max))
                    chain(v.tensor_tensor(dd.unsqueeze(2), pair[:, :, P:P + 1], dd.unsqueeze(2), ALU.max))
                    chain(v.reciprocal(dd, dd))
                    for h in range(2):
                        last = v.tensor_scalar(hm[:, j, 2 * hp + h, :], pair[:, h, 0:P],
                                               den[:, j, 2 * hp + h:2 * hp + h + 1], None, ALU.mult)
                    banks.release(last, ("num", j, hp))
                    banks.moved(v, ("num", j, hp))
                    for h in range(2):
                        n = j * NH + 2 * hp + h
                        chain.mark(v.bn_stats(bst[:, n, :], hm[:, j, 2 * hp + h, :]))
            chain.wait()
            for n in range(NT * NH):
                chain.mark(v.bn_aggr(mv[:, n, :], bst[:, n, :]))
            chain.wait()
            v.tensor_scalar(rs[:, :].unsqueeze(2), mv[:, :, 1:2], EPS1, None, ALU.add).then_inc(sem("hvar"), 1)
            v.wait_ge(sem("hroot"), 1)
            chain(v.reciprocal(rs[:, :], rs[:, :]))
            for n in range(NT * NH):
                v1 = hm[:, n // NH, n % NH, :]
                chain.mark(v.tensor_scalar(v1, v1, mv[:, n, 0:1], rs[:, n:n + 1], ALU.subtract, ALU.mult))
            chain.wait()
            for t in range(NT):
                banks.moved(v, ("o", t))
                v.tensor_tensor(og[:, t, :], og[:, t, :], hm[:, t, :, :].rearrange("p h d -> p (h d)"), ALU.mult)\
                    .then_inc(sem("ym"), 1)
            bank = banks.take(v, "prm2")
            last = v.tensor_copy(prm2[:, 0:113], bank[:, 0:113])
            banks.release(last, "prm2")
            for j in range(2):
                bank = banks.take(v, ("ym", j))
                last = v.tensor_tensor(yT[:, 2 * j:2 * j + 2, :], bank.rearrange("p (c t) -> p c t", c=2),
                                       bcast(prm1[:, 16 + 2 * j:18 + 2 * j], S), ALU.mult)
                banks.release(last, ("ym", j))
            for t in range(NT):
                for n in range(2):
                    bank = banks.take(v, ("out", n, t))
                    xs = x[:, t, n * 512:(n + 1) * 512]
                    last = v.tensor_tensor(xs, xs, bank, ALU.add)
                    banks.release(last, ("out", n, t))
            k.scale(v, chain, "n2", 1, EPS1)
            k.evacuate(v, banks, "n2", prm1[:, 8:16])
            v.wait_ge(sem("wr_in"), 32)
            bank = banks.take(v, "lg")
            last = v.tensor_tensor(lg[:, :, :], bank[:, 0:NT * NE].rearrange("p (t e) -> p t e", t=NT),
                                   brt[:, :].unsqueeze(1).to_broadcast([P, NT, NE]), ALU.add)
            banks.release(last, "lg")
            banks.moved(v, "lg")
            for t in range(NT):
                chain.mark(v.max(v8[:, t, :], lg[:, t, :]))
            chain.wait()
            for t in range(NT):
                chain.mark(v.max_index(i8[:, t, :], v8[:, t, :], lg[:, t, :]))
            chain.wait()
            chain(v.tensor_copy(f8[:, :, :], i8[:, :, :]))
            v.tensor_scalar(f8[:, :, 7:8], v8[:, :, 0:1], -1.0, None, ALU.mult).then_inc(sem("v8neg"), 1)
            for q in range(TOPK):
                for t in range(NT):
                    i = f8[:, t, q:q + 1]
                    if q == 0:
                        last = v.tensor_scalar(mask[:, t, :], iota_e[:, :], i, None, ALU.is_equal)
                    else:
                        last = v.scalar_tensor_tensor(mask[:, t, :], iota_e[:, :], i, mask[:, t, :], ALU.is_equal, ALU.add)
                    if q < TOPK - 1:
                        chain.mark(last)
                    else:
                        last.then_inc(sem("mask"), 1)
                if q < TOPK - 1:
                    chain.wait()
            v.wait_ge(sem("e4"), NT)
            chain(v.reciprocal(es[:, :], es[:, :]))
            v.tensor_tensor(e4[:, :, :], e4[:, :, :], bcast(es[:, :], TOPK), ALU.mult).then_inc(sem("top_gates"), 1)

            bank = banks.take(v, "rk")
            rk = bank[:, 0:NT * NE].rearrange("p (t e) -> p t e", t=NT)
            chain.mark(v.scalar_tensor_tensor(slot[:, :, :], rk, 1.0, mask[:, :, :], ALU.add, ALU.mult))
            last = v.tensor_copy(cnt[:, :], bank[0:1, 256:256 + NE])
            banks.release(last, "rk")
            banks.moved(v, "rk")
            chain.mark(v.tensor_scalar(slot[:, :, :], slot[:, :, :], -1.0, None, ALU.add))
            chain(v.reduce_max(cm[:, 0:1], cnt[:, :], AX.X))
            chain.mark(v.tensor_scalar(cm[:, 2:3], cm[:, 0:1], 2.0 * CAP, 1.0, ALU.is_gt, ALU.add))
            chain(v.tensor_scalar(cm[:, 1:2], cm[:, 0:1], 1.0 * CAP, None, ALU.is_gt))
            chain(v.tensor_tensor(cm[:, 1:2], cm[:, 1:2], cm[:, 2:3], ALU.add))
            chain(v.tensor_scalar(cm[:, 3:4], cm[:, 0:1], 3.0 * CAP, None, ALU.is_gt))
            chain(v.tensor_tensor(cm[:, 1:2], cm[:, 1:2], cm[:, 3:4], ALU.add))
            v.tensor_scalar(passes[:, 0:1], cm[:, 1:2], 1.0, None, ALU.mult).then_inc(sem("passes"), 1)
            v.tensor_scalar(passes[:, 1:2], cm[:, 1:2], float(NE // Pieces.ROUND), -1.0, ALU.mult, ALU.add)\
                .then_inc(sem("passes"), 1)
        @block.tensor
        def _(pe):
            pe.wait_ge(sem("consts"), 4)
            pe.wait_ge(sem("prow1_in"), 16 * 5)
            bank = banks.claim(pe, "prm1")
            banks.filled(pe.transpose(bank[:, 0:56], prow1[0:56, :], ident[0:56, 0:56]), "prm1")
            k.transposes(pe, banks, "n1")
            pe.wait_ge(sem("wg_in"), 16)
            for j in range(4):
                banks.moved(pe, ("n1", j))
            bank = banks.claim(pe, "gr")
            for t in range(NT):
                for c in range(KC):
                    last = pe.matmul(bank[:, 8 * t:8 * t + 8], hT[:, c, t * P:(t + 1) * P], wg[:, c, :],
                                     start=c == 0, stop=c == KC - 1)
            banks.filled(last, "gr")
            banks.moved(pe, "gr")
            bank = banks.claim(pe, "gates")
            for n in range(2):
                for t in range(NT):
                    last = pe.transpose(bank[0:4, n * S + t * P:n * S + (t + 1) * P], tok[:, t, 4 * n:4 * n + 4], ident[:, :])
            banks.filled(last, "gates")

            def feature_major(g, key, m):
                bank = banks.claim(pe, key)
                for i in range(2):
                    for c in range(KC):
                        last = pe.matmul(bank[:, i * S:(i + 1) * S], piece(g)[:, c, (m + i) * P:(m + i + 1) * P],
                                         hT[:, c, :], start=c == 0, stop=c == KC - 1)
                banks.filled(last, key)
                return last

            def token_major(g, key, t):
                bank = banks.claim(pe, key)
                for c in range(KC):
                    last = pe.matmul(bank, hT[:, c, t * P:(t + 1) * P], piece(g)[:, c, :],
                                     start=c == 0, stop=c == KC - 1)
                banks.filled(last, key)
                return last

            for g in (Q_, K_):
                ring.landed(pe, g)
                for m in (0, 2):
                    last = feature_major(g, ("qk", 2 * (g - Q_) + m // 2), m)
            pe.wait_ge(sem("em"), 1)
            pe.wait_ge(sem("negm"), 1)
            bank = banks.claim(pe, "cols")
            for n, r in enumerate((C, EM)):
                for t in range(NT):
                    o = 8 * n + 4 * t
                    last = pe.transpose(bank[:, o:o + 4], rows[:, r, t * P:(t + 1) * P], ident[0:4, 0:4])
            banks.filled(last, "cols")
            for h in range(NH):
                if h % 2 == 0:
                    bank = banks.claim(pe, ("mb", h // 2))
                last = pe.matmul(bank[:, (h % 2) * S:(h % 2 + 1) * S], sel[0:4, h, :], rows[:, M, :],
                                 start=True, stop=True)
                if h % 2:
                    banks.filled(last, ("mb", h // 2))
            ring.landed(pe, V_)
            for t in range(NT):
                last = token_major(V_, ("v", t), t)
            pe.wait_ge(sem("qk_silu"), 4)
            pe.wait_ge(sem("k_scaled"), 2)
            for h in range(NH):
                bank = banks.claim(pe, ("sc", h))
                pe.matmul(bank[:, 0:S], qkT[:, 4 + h, 0:P], qkT[:, h, :], start=True, stop=True)
                last = pe.matmul(bank[:, S:S + P], qkT[:, 4 + h, P:S], qkT[:, h, P:S], start=True, stop=True)
                banks.filled(last, ("sc", h))
            ring.landed(pe, U_)
            for m in (0, 2):
                last = feature_major(U_, ("u", m // 2), m)
            ring.landed(pe, O_)
            for t in range(NT):
                last = token_major(O_, ("o", t), t)
            for t in range(NT):
                banks.moved(pe, ("v", t))
            for h in range(NH):
                banks.moved(pe, ("sc", h))
            for j in range(NT):
                for hp in range(2):
                    bank = banks.claim(pe, ("num", j, hp))
                    for h in (2 * hp, 2 * hp + 1):
                        for i in range(j + 1):
                            o = (h % 2) * (P + 1)
                            last = pe.matmul(bank[:, o:o + P + 1], DT[:, i, h, j * P:(j + 1) * P], vext[:, i, h, :],
                                             start=i == 0, stop=i == j)
                    banks.filled(last, ("num", j, hp))
            pe.wait_ge(sem("prow2_in"), 16 * 4)
            bank = banks.claim(pe, "prm2")
            banks.filled(pe.transpose(bank[:, 0:113], prow2[0:113, :], ident[0:113, 0:113]), "prm2")
            pe.wait_ge(sem("pool_w_in"), 16)
            pe.wait_ge(sem("pooled"), 1)
            for g in range(4):
                if g % 2 == 0:
                    bank = banks.claim(pe, ("pool", g // 2))
                last = pe.matmul(bank[:, (g % 2) * S:(g % 2 + 1) * S], pool_w[:, g, :], inv[:, g, :],
                                 start=True, stop=True)
                if g % 2:
                    banks.filled(last, ("pool", g // 2))
            for j in range(2):
                banks.moved(pe, ("pool", j))
            outs = {}
            for n in range(2):
                ring.landed(pe, OUT0 + n)
                for t in range(NT):
                    outs[n, t] = banks.claim(pe, ("out", n, t))
                    for c in range(4, KC):
                        pe.matmul(outs[n, t], yT[:, c, t * P:(t + 1) * P], piece(OUT0 + n)[:, c, :],
                                  start=c == 4, stop=False)
            pe.wait_ge(sem("ym"), NT)
            for j in range(2):
                bank = banks.claim(pe, ("ym", j))
                for i in range(2):
                    for t in range(NT):
                        c = 2 * j + i
                        last = pe.transpose(bank[:, i * S + t * P:i * S + (t + 1) * P], og[:, t, c * P:(c + 1) * P],
                                            ident[:, :])
                banks.filled(last, ("ym", j))
            for j in range(2):
                banks.moved(pe, ("ym", j))
            for t in range(NT):
                for n in range(2):
                    for c in range(4):
                        last = pe.matmul(outs[n, t], yT[:, c, t * P:(t + 1) * P], piece(OUT0 + n)[:, c, :],
                                         start=False, stop=c == 3)
                    banks.filled(last, ("out", n, t))
            k.transposes(pe, banks, "n2")
            for j in range(4):
                banks.moved(pe, ("n2", j))
            pe.wait_ge(sem("wr_in"), 32)
            bank = banks.claim(pe, "lg")
            for t in range(NT):
                for c in range(KC):
                    last = pe.matmul(bank[:, t * NE:(t + 1) * NE], hT[:, c, t * P:(t + 1) * P], wr[:, c, :],
                                     start=c == 0, stop=c == KC - 1)
            banks.filled(last, "lg")
            pe.wait_ge(sem("mask"), NT)
            bank = banks.claim(pe, "rk")
            pe.matmul(bank[:, 0:NE], ustrict[:, :], mask[:, 0, :], start=True, stop=True)
            pe.matmul(bank[:, NE:2 * NE], ones[:, 0:P], mask[:, 0, :], start=True, stop=False)
            pe.matmul(bank[:, NE:2 * NE], ustrict[:, :], mask[:, 1, :], start=False, stop=True)
            pe.matmul(bank[0:1, 256:256 + NE], ones[:, 0:1], mask[:, 0, :], start=True, stop=False)
            last = pe.matmul(bank[0:1, 256:256 + NE], ones[:, 0:1], mask[:, 1, :], start=False, stop=True)
            banks.filled(last, "rk")


def phase_b(nc, A, sem, sb, ring, banks, env):
    x, xn, ident, prm1, slot, gate, iota_cap, passes, brow, f8, e4, iota_e = (
        env[n] for n in "x xn ident prm1 slot gate iota_cap passes brow f8 e4 iota_e".split())
    tmp = sb("tmp", [P, NT, NE])
    pieces, bdn = env["pieces"], env["bdn"]
    brows = (brow, sb("brow1", [1, 2, D]))
    gT = sb("gT", [NE, NT, P])
    ones_row = sb("ones_row", [1, CAP])
    pass0 = sb("pass0", [P, S // CAP + 1])
    pick = sb("pick", [P, NT, CAP])
    gpick = sb("gpick", [P, NT, 2, CAP])
    gpickT = sb("gpickT", [P, NT, P])
    xg = sb("xg", [P, KC, CAP])
    gt, sg, up, y = (env["hT"][:, 2 * n:2 * n + 2, :].rearrange("p c s -> p (c s)") for n in range(4))
    aT = sb("aT", [P, 4, 2, CAP])
    G_, T_, GATE, UP, AT, DN, SC0, SC1 = range(8)
    uses = [1, 1, 1, 1, 1, 1, 2, 2]
    banks.turn = T_
    banks.plan("gt")
    first = list(banks.uses)

    def bank_claim(pe, b, i, nth=0):
        pe.wait_ge(banks.free[b], first[b] + uses[b] * i + nth)
        return banks.ps[:, b, :]

    def bank_take(eng, b, i, nth=0):
        eng.wait_ge(banks.full[b], first[b] + uses[b] * i + nth + 1)
        return banks.ps[:, b, :]

    def bank_moved(eng, b, i):
        eng.wait_ge(banks.free[b], first[b] + uses[b] * (i + 1))

    def bank_done(eng, b, i):
        eng.wait_ge(banks.full[b], first[b] + uses[b] * i)

    def passes_of(eng):
        eng.wait_ge(sem("passes"), 2)
        return eng.value_load(passes[0:1, 0:1], min_val=1, max_val=S // CAP)

    with nc.Block() as block:
        @block.sync
        def _(sp):
            sp.wait_ge(sem("passes"), 2)
            n = NE // Pieces.ROUND
            last = sp.value_load(passes[0:1, 1:2], min_val=n - 1, max_val=S // CAP * n - 1)

            def load_next(n, rnd, more=True):
                i0 = sp.snap(Pieces.ROUND * rnd + (n - Pieces.SLOTS) // Pieces.PER)
                used = sp.snap(i0 + 1)
                m, h = (n - Pieces.SLOTS) % Pieces.PER // 2, n % 2
                if h == 0:
                    sp.wait_ge(sem(f"first_half_used{m}"), used)
                else:
                    bank_done(sp, (GATE, UP, DN)[m], used)
                i = sp.snap(Pieces.ROUND * rnd + n // Pieces.PER)
                e = sp.snap(i % NE)
                if n % Pieces.PER == 4 and more:
                    load_biases(sp, A, brows[1 - n // Pieces.PER % 2], sem, sp.snap(sp.snap(i + 1) % NE),
                                1 - n // Pieces.PER % 2)
                pieces.load(sp, A, n, e)

            load_biases(sp, A, brows[1], sem, 1, 1)
            with sp.Fori(0, last) as rnd:
                for n in range(8, 32):
                    load_next(n, rnd)
            for n in range(8, 24):
                load_next(n, last, more=n // Pieces.PER < Pieces.ROUND - 1)
            before_last = sp.snap(Pieces.ROUND * last + Pieces.ROUND - 1)
            sp.wait_ge(sem("first_half_used2"), before_last)
            load_c(sp, A, env["ringC"], 0)
            bank_done(sp, DN, before_last)
            load_c(sp, A, env["ringC"], 1)

        @block.vector
        def _(v):
            for t in range(NT):
                v.tensor_scalar(pick[:, t, :], iota_cap[:, 0, :], slot[:, t, 0:1], None, ALU.is_equal)\
                    .then_inc(sem("picks"), 1)
            chain = Chain(v, sem("dveB"))
            v.wait_ge(sem("top_gates"), 1)

            def weights(q):
                for t in range(NT):
                    chain.mark(v.tensor_scalar((gate, tmp)[q > 0][:, t, :], iota_e[:, :], f8[:, t, q:q + 1], e4[:, t, q:q + 1],
                                               ALU.is_equal, ALU.mult))
                chain.wait()
                if 0 < q < TOPK - 1:
                    chain(v.tensor_tensor(gate[:, :, :], gate[:, :, :], tmp[:, :, :], ALU.add))
                elif q:
                    v.tensor_tensor(gate[:, :, :], gate[:, :, :], tmp[:, :, :], ALU.add).then_inc(sem("gates_done"), 1)

            for q in range(TOPK):
                weights(q)
            v.memset(ones_row[:, :], 1.0).then_inc(sem("ones_row"), 1)
            v.memset(y[:, :], 0.0).then_inc(sem("zeroed"), 1)
            v.memset(gpickT[:, :, :], 0.0).then_inc(sem("zeroed"), 1)
            for p in range(S // CAP + 1):
                v.memset(pass0[:, p:p + 1], -float(p * CAP)).then_inc(sem("pass0"), 1)
            v.wait_ge(sem("pass0"), S // CAP + 1)
            steps = v.snap(passes_of(v) * NE)

            def picks(e, p):
                for t in range(NT):
                    v.tensor_scalar(pick[:, t, :], iota_cap[:, 0, :], slot[:, t, bass.ds(e, 1)],
                                    pass0[:, bass.ds(p, 1)], ALU.subtract, ALU.is_equal).then_inc(sem("picks"), 1)

            def gathered(i):
                bank = bank_take(v, G_, i)
                v.tensor_tensor(xg[:, :, :], bank.rearrange("p (c j) -> p c j", c=KC), bcast(prm1[:, 8:16], CAP),
                                ALU.mult).then_inc(banks.free[G_], 1)

            def summed(i):
                for t in range(NT):
                    for h in range(2):
                        bank = bank_take(v, SC0 + h, i, t)
                        xs = x[:, t, h * 512:(h + 1) * 512]
                        v.tensor_tensor(xs, xs, bank, ALU.add).then_inc(banks.free[SC0 + h], 1)

            gathered(0)
            v.wait_ge(sem("gates_done"), 1)
            bank = banks.take(v, "gt")
            banks.release(v.tensor_copy(gT[:, :, :], bank[0:NE, 0:S].rearrange("p (t n) -> p t n", t=NT)), "gt")
            with v.Fori(0, steps) as i:
                e = v.snap(i % NE)
                bank_done(v, T_, i)
                v.wait_ge(sem("picks"), NT * i + NT)
                for t in range(NT):
                    v.tensor_scalar(gpick[:, t, :, :], pick[:, t, :].unsqueeze(1).to_broadcast([P, 2, CAP]),
                                    gate[:, t, bass.ds(e, 1)], None, ALU.mult).then_inc(sem("gpicks"), 1)
                bank_done(v, G_, i + 1)
                v.wait_ge(sem("gpicks"), NT * i + NT)
                nxt = v.snap(i + 1)
                picks(v.snap(nxt % NE), v.snap(nxt // NE))
                bank = bank_take(v, GATE, i)
                v.tensor_scalar(gt[:, :], bank, 7.0, None, ALU.min).then_inc(banks.free[GATE], 1)
                v.wait_ge(sem("sig"), i + 1)
                v.tensor_tensor(gt[:, :], gt[:, :], sg[:, :], ALU.mult).then_inc(sem("glu"), 1)
                bank = bank_take(v, UP, i)
                v.tensor_scalar(up[:, :], bank, 7.0, -7.0, ALU.min, ALU.max).then_inc(banks.free[UP], 1)
                v.wait_ge(sem("glu"), i + 1)
                bank_moved(v, UP, i)
                v.scalar_tensor_tensor(gt[:, :], up[:, :], 1.0, gt[:, :], ALU.add, ALU.mult).then_inc(sem("acted"), 1)
                summed(i)
                bank = bank_take(v, AT, i)
                v.tensor_copy(aT[:, :, :, :], bank.rearrange("p (c h j) -> p c h j", c=4, h=2))\
                    .then_inc(banks.free[AT], 1)
                gathered(nxt)
            summed(steps)

        @block.scalar
        def _(act):
            act.dma_start(env["gain"][:, :], A["normf_g"].unsqueeze(0).to_broadcast([P, D]))\
                .then_inc(sem("normf_in"), 16)
            steps = act.snap(passes_of(act) * NE)
            with act.Fori(0, steps) as i:
                bank_moved(act, GATE, i)
                act.activation(sg[:, :], gt[:, :], ACT.Sigmoid, scale=1.702).then_inc(sem("sig"), 1)
                bank_done(act, SC1, i + 1)
                bank = bank_take(act, T_, i)
                act.copy(gpickT[:, :, :], bank[:, 0:NT * P].rearrange("p (t n) -> p t n", t=NT))\
                    .then_inc(banks.free[T_], 1)
                bank = bank_take(act, DN, i)
                act.copy(y[:, :], bank).then_inc(banks.free[DN], 1)
            env["k"].prepare(act)

        @block.tensor
        def _(pe):
            steps = pe.snap(passes_of(pe) * NE)

            def gather(i):
                pe.wait_ge(sem("picks"), NT * i + NT)
                bank = bank_claim(pe, G_, i)
                for c in range(KC):
                    for t in range(NT):
                        last = pe.matmul(bank[:, c * CAP:(c + 1) * CAP], xn[:, t, c * P:(c + 1) * P],
                                         pick[:, t, :], start=t == 0, stop=t == NT - 1)
                last.then_inc(banks.full[G_], 1)

            def scatter_before(i, biases=False):
                if not biases:
                    pe.wait_ge(banks.free[T_], first[T_] + i)
                    pe.wait_ge(banks.free[DN], first[DN] + i)
                for t in range(NT):
                    for h in range(2):
                        bank = bank_claim(pe, SC0 + h, i, t)
                        if biases:
                            pe.matmul(bank, gT[:, t, :], bdn[:, h * 512:(h + 1) * 512], start=True, stop=False)
                            if t == h == 0:
                                pe.wait_ge(banks.free[T_], first[T_] + i)
                                pe.wait_ge(banks.free[DN], first[DN] + i)
                        pe.matmul(bank, gpickT[h * CAP:(h + 1) * CAP, t, :], y[h * CAP:(h + 1) * CAP, :],
                                  start=not biases, stop=True).then_inc(banks.full[SC0 + h], 1)

            gather(0)
            pe.wait_ge(sem("gates_done"), 1)
            bank = banks.claim(pe, "gt")
            for t in range(NT):
                last = pe.transpose(bank[0:NE, t * P:(t + 1) * P], gate[:, t, :], ident[:, :])
            banks.filled(last, "gt")
            pe.wait_ge(sem("ones_row"), 1)
            pe.wait_ge(sem("zeroed"), 2)
            def expert(r, i, rnd):
                bank_moved(pe, G_, i)
                pe.wait_ge(sem("brow%d_in" % (r % 2)), 32 * (Pieces.ROUND // 2) * rnd + 32 * (r // 2) + 32)
                for m, b in ((0, GATE), (1, UP)):
                    bank = bank_claim(pe, b, i)
                    for h in range(2):
                        last = pe.matmul(bank[h * CAP:(h + 1) * CAP, :], ones_row[:, :],
                                         brows[r % 2][0:1, m, h * 512:(h + 1) * 512], start=True, stop=False)
                    for kh in range(2):
                        w = pieces.landed(pe, 6 * r + 2 * m + kh, rnd)
                        for c in range(4):
                            for h in range(2):
                                last = pe.matmul(bank[h * CAP:(h + 1) * CAP, :], xg[:, 4 * kh + c, :],
                                                 w[:, c, h * 512:(h + 1) * 512], start=False,
                                                 stop=kh == 1 and c == 3)
                        if kh == 0:
                            last.then_inc(sem(f"first_half_used{m}"), 1)
                    last.then_inc(banks.full[b], 1)
                scatter_before(i)
                pe.wait_ge(sem("gpicks"), NT * i + NT)
                bank = bank_claim(pe, T_, i)
                for t in range(NT):
                    last = pe.transpose(bank[:, t * P:(t + 1) * P], gpick[:, t, :, :].rearrange("p a j -> p (a j)"),
                                        ident[:, :])
                last.then_inc(banks.full[T_], 1)
                pe.wait_ge(sem("acted"), i + 1)
                bank = bank_claim(pe, AT, i)
                for c in range(4):
                    last = pe.transpose(bank[:, c * P:(c + 1) * P], gt[:, c * P:(c + 1) * P], ident[:, :])
                last.then_inc(banks.full[AT], 1)
                gather(pe.snap(i + 1))
                bank_moved(pe, AT, i)
                bank = bank_claim(pe, DN, i)
                for kh in range(2):
                    w = pieces.landed(pe, 6 * r + 4 + kh, rnd)
                    for c in range(4):
                        for h in range(2):
                            last = pe.matmul(bank[h * CAP:(h + 1) * CAP, :], aT[:, c, kh, :],
                                             w[:, c, h * 512:(h + 1) * 512], start=kh == 0 and c == 0,
                                             stop=kh == 1 and c == 3)
                    if kh == 0:
                        last.then_inc(sem("first_half_used2"), 1)
                last.then_inc(banks.full[DN], 1)

            with pe.Fori(0, pe.snap(passes_of(pe) * (NE // Pieces.ROUND))) as rnd:
                for r in range(Pieces.ROUND):
                    expert(r, pe.snap(Pieces.ROUND * rnd + r), rnd)
            pe.wait_ge(sem("bdn_in"), 16)
            banks.moved(pe, "gt")
            scatter_before(steps, biases=True)


HG = 4
LEVELS = 7
FQ, FK, FV, FF, GQ, GK, GV, GA, GZ, GATE_F, GATE_G = (
    0, 1024, 2048, 3072, 3080, 4104, 5128, 6152, 6168, 7192, 8216)
PIECES_C = [("w_in_2", c + 512 * hg) for hg in range(2)
            for c in (GQ, GK, GV, FQ, FK, FV, GZ)]
PIECES_C += [p for n in range(2) for p in (
    ("w_in_2", GATE_F + 512 * n), ("w_branch_fox_2", 512 * n), ("w_in_2", GATE_G + 512 * n),
    ("w_branch_gdn_2", 512 * n))]
PIECES_C += [("w_out_2", 512 * n) for n in range(2)]


def load_c(sp, A, ring, g):
    name, c0 = PIECES_C[g]
    ring.load(sp, g, ring.slot(g).rearrange("p (c n) -> p c n", c=KC),
              A[name][0][:, c0:c0 + 512].rearrange("(c p) n -> p c n", p=P))


FF_CHUNKS = 22
NUP = FF_CHUNKS // 2
NDOWN = (FF_CHUNKS + 3) // 4
UP0 = len(PIECES_C)
DOWN0 = UP0 + NUP


def landed_c(g):
    return 16 * sum(2 if UP0 <= q < DOWN0 else 1 for q in range(g % 2, g + 1, 2))


def plan_units(units):
    g = 0
    def piece(kind, keys):
        nonlocal g
        units.plan(g, kind, keys)
        g += 1
    for hg in range(2):
        for w in ("gq", "gk", "gv", "fq", "fk"):
            piece("columns", (None, (w, hg, 0), None, (w, hg, 1)))
        for w in ("fv", "gz"):
            piece("rows", (None, None, None, (w, hg, 1)))
    for n in range(2):
        for w in ("gf", "bf", "gg", "bg"):
            piece("columns", (None, (w, n, 0), None, (w, n, 1)))
    for n in range(2):
        piece("rows", (None, None, None, ("out", n, 1)))
    for j in range(NUP):
        piece("up", (None, ("up", j, 0), None, ("up", j, 1)))
    for j in range(NDOWN):
        n = min(4, FF_CHUNKS - 4 * j)
        piece("rows", (None,) * n if j < NDOWN - 1 else (None,) * (n - 1) + (("dn", 1, 1),))


UNITS_GROUP, UNITS_E, UNITS_OUT = 28, 56, 88


def product(pe, units, u, out, xh, xl, c, start, stop):
    wh = units.buf(units.high, u)[:, c * P:(c + 1) * P]
    wl = units.buf(units.low, u)[:, c * P:(c + 1) * P]
    pe.matmul(out, wh, xh, start=start, stop=False)
    pe.matmul(out, wh, xl, start=False, stop=False)
    return pe.matmul(out, wl, xh, start=False, stop=stop)


def columns(pe, units, banks, u, keys, xh, xl, before=None):
    for q in range(4):
        if q % 2 == 0:
            bank = banks.claim(pe, keys[q // 2])
        units.ready(pe, u + q)
        for c in range(KC):
            if before and q == 0:
                before(c)
            last = product(pe, units, u + q, bank[:, (q % 2) * S:(q % 2 + 1) * S], xh[:, c, :], xl[:, c, :], c,
                           c == 0, c == KC - 1)
        units.finish(last, u + q)


def rows(pe, units, banks, u, keys, xh, xl, before=None):
    bank = [banks.claim(pe, key) for key in keys]
    for q in range(4):
        if before:
            before(q)
        units.ready(pe, u + q)
        for t in range(NT):
            for c in range(2):
                wh = units.buf(units.high, u + q)[:, c * 512:(c + 1) * 512]
                wl = units.buf(units.low, u + q)[:, c * 512:(c + 1) * 512]
                a = slice(t * P, (t + 1) * P)
                kc = 2 * q + c
                pe.matmul(bank[t], xh[:, kc, a], wh, start=kc == 0, stop=False)
                pe.matmul(bank[t], xh[:, kc, a], wl, start=False, stop=False)
                last = pe.matmul(bank[t], xl[:, kc, a], wh, start=False, stop=kc == KC - 1)
            if q == 3 and t == 0:
                banks.filled(last, keys[0])
        units.finish(last, u + q)


def load_up(sp, A, ring, j):
    w = A["w_up_2"][0].rearrange("(c p) (h n) -> p c h n", p=P, h=2)
    dst = ring.slot(UP0 + j).rearrange("p (c h n) -> p c h n", c=KC, h=2)
    for h in range(2):
        ring.load(sp, UP0 + j, dst[:, :, h, :], w[:, :, h, j * 2 * P:(j + 1) * 2 * P])


def load_down(sp, A, ring, j):
    n = min(4, FF_CHUNKS - 4 * j)
    ring.load(sp, DOWN0 + j, ring.slot(DOWN0 + j).rearrange("p (c n) -> p c n", c=4)[:, 0:n, :],
              A["w_down_2"][0][4 * j * P:(4 * j + n) * P, :].rearrange("(c p) n -> p c n", p=P))


def phase_c(nc, A, sem, sb, ring, banks, k, env):
    x, xn, hT, ident, tri, ustrict, ones, sel, prm2, gain, units, hTh, hTl, yf, yg, prm1, prow1, prow2, stat = (
        env[n] for n in "x xn hT ident tri ustrict ones sel prm2 gain units hTh hTl yf yg prm1 prow1 prow2 stat".split())
    tok = prm1[:, 0:NT * 24].rearrange("p (t n) -> p t n", t=NT)
    eps2 = sb("eps2", [P, 1])
    wg2 = sb("wg2", [P, KC, 24])
    rb = sb("rb", [8, 3])
    rowp = sb("rowp", [8, 3, S])
    NEGC, GC, BETA = range(3)
    temp = xn[0:8, :, :].rearrange("p t (a s) -> p (t a) s", s=S)
    TA, TB, TC, TD, TE, BEG, KD, TF = range(8)
    cols = sb("cols", [P, 6, 8])
    lm = sb("lm", [P, LEVELS, P])
    gT = sb("gT2", [P, 3, HG, S])
    fqk = hT[:, :, :].rearrange("p (a h) s -> p a h s", a=2)
    fv = sb("fv", [P, NT, 512])
    gz = sb("gz", [P, NT, 512])
    X = sb("X", [P, NT, HG, P])
    XT = sb("XT", [P, NT, HG, P])
    work = sb("work", [P, 2, NT, HG * P])
    ATm, T1 = work[:, 0], work[:, 1]
    AT = xn[:, 0, :].rearrange("p (t h n) -> p t h n", t=NT, h=HG)
    attnT = xn[:, 1, :].rearrange("p (t h n) -> p t h n", t=NT, h=HG)

    def sq(j):
        return (X, XT)[j // 2][:, j % 2].rearrange("p h n -> p (h n)")

    vb = sb("vb", [P, NT, HG, P])
    kbg = sb("kbg", [P, HG, P])
    kdec = sb("kdec", [P, HG, P])
    egb = sb("egb", [P, HG, P])
    u = gT[:, 2].rearrange("p h (t n) -> p t h n", t=NT)
    wTn = sb("wTn", [P, HG, P])
    state = sb("state", [P, HG, P])
    o = gT[:, 1].rearrange("p h (t n) -> p t h n", t=NT)
    osum = sb("osum", [P, NT, HG])
    prob = work[:, :, :, :].rearrange("p a t n -> p (a t n)")[:, 0:HG * 384].rearrange("p (h n) -> p h n", h=HG)
    probT = hT[:, :, :].rearrange("p c s -> p (c s)")[:, 0:HG * 384].rearrange("p (h n) -> p h n", h=HG)
    negmask = sb("negmask", [P, P])
    fmax = sb("fmax", [P, HG, NT])
    fsum = sb("fsum", [P, HG, NT])

    banks.plan(*[("nm", j) for j in range(4)], "rt", ("rw", 0), ("rw", 1))
    for hg in range(2):
        banks.plan(("gq", hg, 0), ("gq", hg, 1), *([("oT", 0, 0), ("oT", 0, 1)] if hg else []),
                   ("gk", hg, 0), ("gk", hg, 1), *([] if hg else ["cols"]),
                   ("gv", hg, 0), ("gv", hg, 1),
                   ("fq", hg, 0), ("fq", hg, 1), *[("ss", hg, j) for j in range(4)], *[("rb", hg, h) for h in range(HG)],
                   ("fk", hg, 0), ("fk", hg, 1), *[("kq", hg, h) for h in range(HG)],
                   *[(w, hg, t) for w in ("kt", "vt") for t in range(NT)],
                   ("fv", hg, 0), ("fv", hg, 1), *[("x1", hg, t) for t in range(NT)],
                   ("gz", hg, 0), ("gz", hg, 1))
        for l in range(1, LEVELS):
            banks.plan(*[("t1", hg, l, t) for t in range(NT)])
            for t in range(NT):
                banks.plan(*([("xx", hg, l, t)] if l < LEVELS - 1 else []), ("xt", hg, l, t))
        banks.plan(*[("lo", hg, h) for h in range(HG)], ("u0", hg), ("wT", hg), ("st", hg), ("o0", hg), ("u1", hg),
                   *[("pt", hg, h) for h in range(HG)], ("o1", hg), ("pv", hg, 0), ("pv", hg, 1))
    banks.plan(("gf", 0, 0), ("gf", 0, 1), ("oT", 1, 0), ("oT", 1, 1))

    def heads(bank):
        return bank.rearrange("p (h n) -> p h n", h=HG)

    flat = hT[:, :, :].rearrange("p (t c) n -> p t (c n)", t=NT)

    with nc.Block() as block:
        @block.sync
        def _(sp):
            sp.dma_start(wg2[:, :, 0:8], A["w_in_2"][0][:, FF:FF + 8].rearrange("(c p) n -> p c n", p=P))\
                .then_inc(sem("wg2_in"), 16)
            sp.dma_start(wg2[:, :, 8:24], A["w_in_2"][0][:, GA:GA + 16].rearrange("(c p) n -> p c n", p=P))\
                .then_inc(sem("wg2_in"), 16)
            for i, name in enumerate(("fox_f_bias_2", "gdn_a_log_2", "gdn_dt_bias_2")):
                sp.dma_start(rb[:, i:i + 1], A[name].rearrange("a h -> h a")).then_inc(sem("rb_in"), 16)
            for h, prow in enumerate((prow1, prow2)):
                for i in range(3):
                    sp.dma_start(prow[FF_CHUNKS * i:FF_CHUNKS * (i + 1), :],
                                 A["ffn_conv_w_2"][0, i, h * FF_CHUNKS * P:(h + 1) * FF_CHUNKS * P]
                                 .rearrange("(c p) -> c p", p=P)).then_inc(sem("taps_in"), 16)
            for g in range(2, 14 + 2):
                units.freed(sp, g - 2)
                load_c(sp, A, ring, g)

        @block.scalar
        def _(act):
            chain = Chain(act, sem("actC"))

            def ahead(n):
                units.ahead(act, "high", n)

            k.squares(act, "nf", 2, flat)
            for t in range(NT):
                act.wait_ge(sem("norm_scaled"), NT * (k.nth("nf") - 1) + t + 1)
                act.activation(work[:, t].rearrange("p t n -> p (t n)"), xn[:, t, :], ACT.Square, accum_out=stat[:, 12 + t:13 + t])\
                    .then_inc(sem("norm_squares"), 1)
                if t == 0:
                    k.root(act, "nf", 2)
            k.root(act, "nm", 3)
            ahead(0)
            high_parts(k, act, banks, "nm", hTh)
            bank = banks.take(act, "rt")
            banks.release(act.copy(tok[:, :, :], bank[:, 0:NT * 24].rearrange("p (t n) -> p t n", t=NT)), "rt")
            act.wait_ge(sem("rb_in"), 48)
            chain(act.activation(rb[:, 1:2], rb[:, 1:2], ACT.Exp))
            banks.moved(act, ("rw", 0))
            for a, b in ((TA, TC), (TB, TD)):
                chain(act.activation(temp[:, b, :], temp[:, a, :], ACT.Abs))
                chain(act.activation(temp[:, b, :], temp[:, b, :], ACT.Exp, scale=-1.0))
            for b in (TC, TD):
                act.activation(temp[:, b, :], temp[:, b, :], ACT.Ln, bias=1.0).then_inc(sem("rows_ln"), 1)
            bank = banks.take(act, ("rw", 1))
            banks.release(act.activation(rowp[:, BETA, :], bank[0:8, 0:S], ACT.Sigmoid), ("rw", 1))
            act.wait_ge(sem("gc_rows"), 2)
            act.activation(temp[:, BEG, P:S], rowp[:, GC, P:S], ACT.Exp).then_inc(sem("eg_rows"), 1)
            act.activation(temp[:, KD, 0:P], temp[:, KD, 0:P], ACT.Exp).then_inc(sem("eg_rows"), 1)

            def delta_high(hg):
                for j in range(2):
                    bank = banks.take(act, ("oT", hg, j))
                    act.activation(yg[0][:, HG * hg + 2 * j:HG * hg + 2 * j + 2, :],
                                   bank.rearrange("p (h s) -> p h s", h=2), ACT.Copy, scale=prm2[:, 16:17])\
                        .then_inc(sem("yg_high"), 1)

            for hg in range(2):
                u0 = UNITS_GROUP * hg
                for w in range(3):
                    if hg and w == 1:
                        delta_high(0)
                    for j in range(2):
                        ahead(u0 + 4 * w + 2 * j + 3)
                        banks.moved(act, (("gq", "gk", "gv")[w], hg, j))
                        part = gT[:, w, 2 * j:2 * j + 2, :]
                        act.activation(part, part, ACT.Silu).then_inc(sem("g_silu"), 1)
                ahead(u0 + 12)
                act.wait_ge(sem("g_silu"), 6 * hg + 4)
                for j in range(4):
                    act.activation(sq(j), gT[:, j // 2, 2 * (j % 2):2 * (j % 2) + 2, :].rearrange("p h s -> p (h s)"),
                                   ACT.Square).then_inc(sem("g_sq"), 1)
                if hg == 0:
                    act.wait_ge(sem("nm_low"), 4)
                for j in range(2):
                    ahead(u0 + 12 + 2 * j + 2)
                    bank = banks.take(act, ("fq", hg, j))
                    last = act.activation(fqk[:, 0, 2 * j:2 * j + 2, :], bank.rearrange("p (h s) -> p h s", h=2),
                                          ACT.Copy, scale=float(P) ** -0.5)
                    banks.release(last, ("fq", hg, j))
                act.wait_ge(sem("consts2"), 1)
                for j in range(4):
                    bank = banks.take(act, ("ss", hg, j))
                    banks.release(act.activation(work[:, j // 2, j % 2, :], bank, ACT.Ln, bias=eps2[:, 0:1]),
                                  ("ss", hg, j))
                for j in range(4):
                    banks.moved(act, ("ss", hg, j))
                    act.activation(work[:, j // 2, j % 2, :], work[:, j // 2, j % 2, :], ACT.Exp, scale=-0.5)\
                        .then_inc(sem("ss_root"), 1)
                for h in range(HG):
                    act.wait_ge(sem("dlog"), 4 * hg + h + 1)
                    act.activation(attnT[:, :, h, :], attnT[:, :, h, :], ACT.Exp).then_inc(sem("dexp"), 1)
                    bank = banks.take(act, ("rb", hg, h))
                    act.activation(egb[:, h, :], bank[:, P:S], ACT.Exp).then_inc(sem("egb"), 1)
                for j in range(2):
                    ahead(u0 + 16 + 2 * j + 2)
                    bank = banks.take(act, ("fk", hg, j))
                    last = act.copy(fqk[:, 1, 2 * j:2 * j + 2, :], bank.rearrange("p (h s) -> p h s", h=2))
                    banks.release(last, ("fk", hg, j))
                for t in range(NT):
                    ahead(u0 + 20 + (3, 4)[t])
                    bank = banks.take(act, ("fv", hg, t))
                    banks.release(act.copy(fv[:, t, :], bank), ("fv", hg, t))
                for t in range(NT):
                    bank = banks.take(act, ("x1", hg, t))
                    banks.release(act.copy(X[:, t], heads(bank)), ("x1", hg, t))
                for t in range(NT):
                    ahead(u0 + 24 + (3, 4)[t])
                    bank = banks.take(act, ("gz", hg, t))
                    banks.release(act.activation(gz[:, t, :], bank, ACT.Silu), ("gz", hg, t))
                for l in range(1, LEVELS):
                    for t in range(NT):
                        bank = banks.take(act, ("t1", hg, l, t))
                        banks.release(act.copy(T1[:, t, :], bank), ("t1", hg, l, t))
                for h in range(HG):
                    act.wait_ge(sem("fmax"), 4 * hg + h + 1)
                    bank = banks.take(act, ("lo", hg, h))
                    act.activation(prob[:, h, 0:P], bank[:, 0:P], ACT.Exp, bias=fmax[:, h, 0:1],
                                   accum_out=fsum[:, h, 0:1])
                    last = act.activation(prob[:, h, P:384], bank[:, P:384], ACT.Exp, bias=fmax[:, h, 1:2],
                                          accum_out=fsum[:, h, 1:2])
                    banks.release(last, ("lo", hg, h))
                bank = banks.take(act, ("u0", hg))
                banks.release(act.copy(u[:, 0], heads(bank)), ("u0", hg))
                bank = banks.take(act, ("wT", hg))
                banks.release(act.activation(wTn[:, :, :], heads(bank), ACT.Copy, scale=-1.0), ("wT", hg))
                bank = banks.take(act, ("st", hg))
                banks.release(act.copy(state[:, :, :], heads(bank)), ("st", hg))
                bank = banks.take(act, ("u1", hg))
                banks.release(act.copy(u[:, 1], heads(bank)), ("u1", hg))
                for h in range(HG):
                    bank = banks.take(act, ("pt", hg, h))
                    banks.release(act.copy(probT[:, h, :], bank[:, 0:384]), ("pt", hg, h))
                for j in range(2):
                    bank = banks.take(act, ("pv", hg, j))
                    act.copy(yf[0][:, HG * hg + 2 * j:HG * hg + 2 * j + 2, :], bank.rearrange("p (h s) -> p h s", h=2))\
                        .then_inc(sem("yf_high"), 1)
                k.prepare(act)
                act.wait_ge(sem("o_mean"), hg + 1)
                act.activation(osum[:, :, :], osum[:, :, :], ACT.Sqrt).then_inc(sem("o_root"), 1)
                if hg:
                    ahead(UNITS_E + 2)
                    delta_high(1)

        @block.gpsimd
        def _(g):
            chain = Chain(g, sem("poolC"))
            chain(g.memset(eps2[:, :], EPS2))
            chain(g.memset(lm[:, :, :], 0.0))
            for l in range(LEVELS):
                b = 1 << l
                odd = lm[:, l, :].rearrange("p (m o r) -> p m o r", o=2, r=b)[:, :, 1, :]
                m = P // (2 * b)
                chain(g.memset(odd, -1.0))
                chain(g.affine_select(out=odd, in_=odd, compare_op=ALU.is_ge, fill=0.0, base=0,
                                      pattern=[[-2 * b, m], [0, b]], channel_multiplier=1))
                chain(g.affine_select(out=odd, in_=odd, compare_op=ALU.is_ge, fill=0.0, base=b - 1,
                                      pattern=[[2 * b, m], [0, b]], channel_multiplier=-1))
            chain(g.memset(negmask[:, :], 0.0))
            g.affine_select(out=negmask[:, :], in_=negmask[:, :], compare_op=ALU.is_ge, fill=-1e30, base=0,
                            pattern=[[-1, P]], channel_multiplier=1).then_inc(sem("consts2"), 1)
            units.ahead(g, "low1", 0)
            for hg in range(2):
                u0 = UNITS_GROUP * hg
                units.ahead(g, "low1", u0 + 20)
                g.wait_ge(sem("kk"), 4 * hg + 4)
                for l in range(LEVELS):
                    if l == 1:
                        units.ahead(g, "low1", u0 + 24)
                    if l in (4, 5):
                        units.ahead(g, "low1", u0 + 24 + 2 * (l - 3))
                    if l in (2, 3):
                        for h in (2 * l - 4, 2 * l - 3):
                            banks.moved(g, ("kq", hg, h))
                            g.tensor_tensor(attnT[:, :, h, :], attnT[:, :, h, :],
                                            tri[:, :].unsqueeze(1).to_broadcast([P, NT, P]), ALU.mult)\
                                .then_inc(sem("attn_masked"), 1)
                    for t in range(NT):
                        if l > 1:
                            banks.done(g, ("t1", hg, l - 1, t))
                        if l == 1:
                            g.wait_ge(sem("x1T"), NT * hg + t + 1)
                        g.tensor_tensor(heads(ATm[:, t, :]), AT[:, t], lm[:, l, :].unsqueeze(1).to_broadcast([P, HG, P]),
                                        ALU.mult).then_inc(sem("ATm"), 1)

        @block.vector
        def _(v):
            chain = Chain(v, sem("dveC"))
            v.wait_ge(sem("normf_in"), 16)
            for t in range(NT):
                v.tensor_tensor(xn[:, t, :], x[:, t, :], gain[:, :], ALU.mult).then_inc(sem("norm_scaled"), 1)
            c1, r1, c2, r2 = (stat[:, i:i + 2] for i in (8, 10, 12, 14))
            k.mean(v, chain, "nf", c1, r1, EPS1)
            chain(v.reciprocal(r1, c1))
            v.wait_ge(sem("norm_squares"), k.squares_by("nm"))
            chain(v.tensor_tensor(c2, c2, r1, ALU.mult))
            chain(v.tensor_tensor(c2, c2, r1, ALU.mult))
            k.mean(v, chain, "nm", c2, r2, EPS2)
            chain(v.reciprocal(r2, c2))
            chain(v.tensor_tensor(r2, r2, r1, ALU.mult))
            for t in range(NT):
                v.tensor_scalar(xn[:, t, :], xn[:, t, :], r2[:, t:t + 1], None, ALU.mult).then_inc(sem("norm_scaled"), 1)
            units.ahead(v, "low0", 0)
            evacuate_split(k, v, banks, "nm", prm2[:, 0:8], hTh, hTl)
            for t in range(NT):
                v.scalar_tensor_tensor(x[:, t, :], x[:, t, :], r1[:, t:t + 1], gain[:, :], ALU.mult, ALU.mult)\
                    .then_inc(sem("residual"), 1)
            v.wait_ge(sem("rb_in"), 48)
            bank = banks.take(v, ("rw", 0))
            v.tensor_scalar(temp[:, TA, :], bank[0:8, 0:S], rb[:, 0:1], None, ALU.add)
            last = v.tensor_scalar(temp[:, TB, :], bank[0:8, S:2 * S], rb[:, 2:3], None, ALU.add)
            banks.release(last, ("rw", 0))
            v.wait_ge(sem("rows_ln"), 2)
            chain.mark(v.scalar_tensor_tensor(temp[:, TE, :], temp[:, TA, :], 0.0, temp[:, TC, :], ALU.min, ALU.subtract))
            chain(v.scalar_tensor_tensor(temp[:, TF, :], temp[:, TB, :], 0.0, temp[:, TD, :], ALU.max, ALU.add))
            chain(v.tensor_scalar(temp[:, TF, :], temp[:, TF, :], rb[:, 1:2], -1.0, ALU.mult, ALU.mult))
            chain(v.tensor_tensor_scan(temp[:, TA, :], ones[0:8, :], temp[:, TE, :], 0.0, ALU.mult, ALU.add))
            v.tensor_scalar(rowp[:, NEGC, :], temp[:, TA, :], -1.0, None, ALU.mult).then_inc(sem("negc"), 1)
            for t in range(NT):
                chain(v.tensor_tensor_scan(rowp[:, GC, t * P:(t + 1) * P], ones[0:8, 0:P],
                                           temp[:, TF, t * P:(t + 1) * P], 0.0, ALU.mult, ALU.add))
            v.tensor_scalar(temp[:, KD, 0:P], rowp[:, GC, 0:P], -1.0, rowp[:, GC, P - 1:P], ALU.mult, ALU.add)\
                .then_inc(sem("gc_rows"), 1)
            v.tensor_copy(temp[:, TC, 0:P], rowp[:, GC, 0:P]).then_inc(sem("gc_rows"), 1)
            v.wait_ge(sem("eg_rows"), 2)
            banks.moved(v, ("rw", 1))
            v.tensor_tensor(temp[:, BEG, P:S], temp[:, BEG, P:S], rowp[:, BETA, P:S], ALU.mult).then_inc(sem("beg"), 1)

            def conv(w, name, hg):
                for j in range(2):
                    units.ahead(v, "low0", UNITS_GROUP * hg + 4 * w + 2 * j + 2)
                    bank = banks.take(v, (name, hg, j))
                    for i in range(4):
                        for a in range(2):
                            ch = 8 * w + HG * hg + 2 * j + a
                            c = gT[:, w, 2 * j + a, :]
                            tap = prm2[:, 17 + 24 * (3 - i) + ch:18 + 24 * (3 - i) + ch]
                            if i == 0:
                                last = v.tensor_scalar(c, bank[:, a * S:(a + 1) * S], tap, None, ALU.mult)
                            else:
                                last = v.scalar_tensor_tensor(c[:, i:], bank[:, a * S:(a + 1) * S - i], tap, c[:, i:],
                                                              ALU.mult, ALU.add)
                            if i < 3:
                                chain.mark(last)
                        if i < 3:
                            chain.wait()
                    banks.release(last, (name, hg, j))

            def delta_low(hg):
                for j in range(2):
                    bank = banks.take(v, ("oT", hg, j))
                    v.wait_ge(sem("yg_high"), 2 * hg + j + 1)
                    c = slice(HG * hg + 2 * j, HG * hg + 2 * j + 2)
                    last = v.scalar_tensor_tensor(yg[1][:, c, :], bank.rearrange("p (h s) -> p h s", h=2), prm2[:, 16:17],
                                                  yg[0][:, c, :].bitcast(F32), ALU.mult, ALU.subtract)
                    banks.release(last, ("oT", hg, j))

            for hg in range(2):
                conv(0, "gq", hg)
                if hg:
                    delta_low(0)
                conv(1, "gk", hg)
                if hg == 0:
                    bank = banks.take(v, "cols")
                    last = v.tensor_copy(cols[:, :, :], bank[:, 0:48].rearrange("p (a h) -> p a h", a=6))
                    banks.release(last, "cols")
                conv(2, "gv", hg)
                if hg == 0:
                    banks.moved(v, "cols")
                units.ahead(v, "low0", UNITS_GROUP * hg + 16)
                for h in range(HG):
                    bank = banks.take(v, ("rb", hg, h))
                    hh = HG * hg + h
                    for t in range(NT):
                        last = v.tensor_scalar(attnT[:, t, h, :], bank[:, t * P:(t + 1) * P], cols[:, t, hh:hh + 1], 0.0,
                                               ALU.subtract, ALU.min)
                    last.then_inc(sem("dlog"), 1)
                for j in range(4):
                    v.wait_ge(sem("ss_root"), 4 * hg + j + 1)
                    part = gT[:, j // 2, 2 * (j % 2):2 * (j % 2) + 2, :].rearrange("p h s -> p (h s)")
                    v.scalar_tensor_tensor(part, part, float(P) ** -0.5 if j < 2 else 1.0, work[:, j // 2, j % 2, :],
                                           ALU.mult, ALU.mult).then_inc(sem("g_unit"), 1)
                units.ahead(v, "low0", UNITS_GROUP * hg + 17)
                v.wait_ge(sem("g_unit"), 4 * hg + 2)
                for h in range(HG):
                    v.wait_ge(sem("dexp"), 4 * hg + h + 1)
                    v.wait_ge(sem("egb"), 4 * hg + h + 1)
                    bank = banks.take(v, ("rb", hg, h))
                    last = v.tensor_tensor(AT[:, :, h, :], attnT[:, :, h, :],
                                           bank[:, S:2 * S].rearrange("p (t n) -> p t n", t=NT), ALU.mult)
                    banks.release(last, ("rb", hg, h))
                    v.tensor_tensor(egb[:, h, :], egb[:, h, :], gT[:, 0, h, P:S], ALU.mult).then_inc(sem("qdec"), 1)
                units.ahead(v, "low0", UNITS_GROUP * hg + 20)
                for h in range(HG):
                    banks.moved(v, ("rb", hg, h))
                    bank = banks.take(v, ("kq", hg, h))
                    v.tensor_tensor(AT[:, :, h, :], AT[:, :, h, :],
                                    bank[:, 0:S].rearrange("p (t n) -> p t n", t=NT), ALU.mult).then_inc(sem("kk"), 1)
                    last = v.tensor_tensor(attnT[:, :, h, :], attnT[:, :, h, :],
                                           bank[:, S:2 * S].rearrange("p (t n) -> p t n", t=NT), ALU.mult)
                    banks.release(last, ("kq", hg, h))
                for t in range(NT):
                    bank = banks.take(v, ("kt", hg, t))
                    col = cols[:, 5 - t, HG * hg:HG * hg + HG]
                    last = v.tensor_tensor((kdec, kbg)[t][:, :, :], heads(bank), bcast(col, P), ALU.mult)
                    banks.release(last, ("kt", hg, t))
                for t in range(NT):
                    bank = banks.take(v, ("vt", hg, t))
                    last = v.tensor_tensor(vb[:, t], heads(bank), bcast(cols[:, 2 + t, HG * hg:HG * hg + HG], P), ALU.mult)
                    banks.release(last, ("vt", hg, t))
                for t in range(NT):
                    v.wait_ge(sem("ATm"), 2 * LEVELS * hg + t + 1)
                    v.tensor_tensor(XT[:, t], heads(ATm[:, t, :]), ident[:, :].unsqueeze(1).to_broadcast([P, HG, P]),
                                    ALU.add).then_inc(sem("x1T"), 1)
                units.ahead(v, "low0", UNITS_GROUP * hg + 28)
                for l in range(1, LEVELS):
                    for t in range(NT):
                        for w, buf in (("xx", X), ("xt", XT)):
                            if w == "xx" and l == LEVELS - 1:
                                continue
                            bank = banks.take(v, (w, hg, l, t))
                            if w == "xx":
                                banks.done(v, ("xt", hg, l, t))
                            banks.release(v.tensor_tensor(buf[:, t], buf[:, t], heads(bank), ALU.add), (w, hg, l, t))
                for h in range(HG):
                    bank = banks.take(v, ("lo", hg, h))
                    chain.mark(v.reduce_max(fmax[:, h, 0:1], bank[:, 0:P], AX.X))
                    chain(v.reduce_max(fmax[:, h, 1:2], bank[:, P:384], AX.X))
                    v.tensor_scalar(fmax[:, h, :], fmax[:, h, :], -1.0, None, ALU.mult).then_inc(sem("fmax"), 1)
                for h in range(HG):
                    banks.moved(v, ("lo", hg, h))
                    chain(v.reciprocal(fsum[:, h, :], fsum[:, h, :]))
                    v.tensor_scalar(prob[:, h, 0:P], prob[:, h, 0:P], fsum[:, h, 0:1], None, ALU.mult)
                    v.tensor_scalar(prob[:, h, P:384], prob[:, h, P:384], fsum[:, h, 1:2], None, ALU.mult)\
                        .then_inc(sem("prob"), 1)
                def attention_low():
                    for j in range(2):
                        bank = banks.take(v, ("pv", hg, j))
                        v.wait_ge(sem("yf_high"), 2 * hg + j + 1)
                        c = slice(HG * hg + 2 * j, HG * hg + 2 * j + 2)
                        last = v.tensor_tensor(yf[1][:, c, :], bank.rearrange("p (h s) -> p h s", h=2),
                                               yf[0][:, c, :].bitcast(F32), ALU.subtract)
                        banks.release(last, ("pv", hg, j))

                for t in range(NT):
                    bank = banks.take(v, ("o%d" % t, hg))
                    banks.release(v.tensor_copy(o[:, t], heads(bank)), ("o%d" % t, hg))
                    banks.moved(v, ("o%d" % t, hg))
                    chain(v.tensor_tensor(vb[:, t], o[:, t], o[:, t], ALU.mult))
                    chain(v.tensor_reduce(osum[:, t, :], vb[:, t], AX.X, ALU.add))
                v.tensor_scalar(osum[:, :, :], osum[:, :, :], 1.0 / P, EPS2, ALU.mult, ALU.add).then_inc(sem("o_mean"), 1)
                v.wait_ge(sem("o_root"), hg + 1)
                chain(v.reciprocal(osum[:, :, :], osum[:, :, :]))
                for t in range(NT):
                    chain.mark(v.tensor_tensor(o[:, t], o[:, t], bcast(osum[:, t, :], P), ALU.mult))
                chain.wait()
                for t in range(NT):
                    banks.moved(v, ("gz", hg, t))
                    v.tensor_tensor(o[:, t], o[:, t], heads(gz[:, t, :]), ALU.mult).then_inc(sem("o_done"), 1)
                attention_low()
            delta_low(1)

        @block.tensor
        def _(pe):
            def both_f(u, name, hg, before=None):
                columns(pe, units, banks, u, [(name, hg, j) for j in range(2)], hTh, hTl, before)

            def both_t(u, name, hg):
                rows(pe, units, banks, u, [(name, hg, t) for t in range(NT)], hTh, hTl)

            k.transposes(pe, banks, "nm")
            pe.wait_ge(sem("wg2_in"), 32)
            for j in range(4):
                banks.moved(pe, ("nm", j))
            bank = banks.claim(pe, "rt")
            for t in range(NT):
                for c in range(KC):
                    last = pe.matmul(bank[:, 24 * t:24 * t + 24], hT[:, c, t * P:(t + 1) * P], wg2[:, c, :],
                                     start=c == 0, stop=c == KC - 1)
            banks.filled(last, "rt")
            banks.moved(pe, "rt")
            for b, parts in ((0, (0, 8)), (1, (16,))):
                bank = banks.claim(pe, ("rw", b))
                for i, w0 in enumerate(parts):
                    for t in range(NT):
                        last = pe.transpose(bank[0:8, i * S + t * P:i * S + (t + 1) * P], tok[:, t, w0:w0 + 8], ident[:, :])
                banks.filled(last, ("rw", b))

            def outputs_transposed(hg):
                pe.wait_ge(sem("o_done"), NT * hg + NT)
                for j in range(2):
                    bank = banks.claim(pe, ("oT", hg, j))
                    for i in range(2):
                        for t in range(NT):
                            last = pe.transpose(bank[:, i * S + t * P:i * S + (t + 1) * P], o[:, t, 2 * j + i, :], ident[:, :])
                    banks.filled(last, ("oT", hg, j))

            for hg in range(2):
                u0 = UNITS_GROUP * hg
                both_f(u0 + 0, "gq", hg, None if hg else lambda c: pe.wait_ge(sem("nm_low"), c // 2 + 1))
                if hg:
                    outputs_transposed(0)
                both_f(u0 + 4, "gk", hg)
                if hg == 0:
                    pe.wait_ge(sem("beg"), 1)
                    bank = banks.claim(pe, "cols")
                    for i, r in enumerate((rowp[:, GC, 0:P], rowp[:, GC, P:S], rowp[:, BETA, 0:P], rowp[:, BETA, P:S],
                                           temp[:, BEG, P:S], temp[:, KD, 0:P])):
                        last = pe.transpose(bank[:, 8 * i:8 * i + 8], r, ident[0:8, 0:8])
                    banks.filled(last, "cols")
                both_f(u0 + 8, "gv", hg)
                both_f(u0 + 12, "fq", hg)
                for j in range(4):
                    pe.wait_ge(sem("g_sq"), 4 * hg + j + 1)
                    bank = banks.claim(pe, ("ss", hg, j))
                    banks.filled(pe.matmul(bank, ones[:, 0:P], sq(j), start=True, stop=True), ("ss", hg, j))
                pe.wait_ge(sem("negc"), 1)
                for h in range(HG):
                    bank = banks.claim(pe, ("rb", hg, h))
                    pe.matmul(bank[:, 0:S], sel[:, HG * hg + h, :], rowp[:, GC, :], start=True, stop=True)
                    last = pe.matmul(bank[:, S:2 * S], sel[:, HG * hg + h, :], rowp[:, BETA, :], start=True, stop=True)
                    banks.filled(last, ("rb", hg, h))
                both_f(u0 + 16, "fk", hg)
                pe.wait_ge(sem("g_unit"), 4 * hg + 4)
                for h in range(HG):
                    bank = banks.claim(pe, ("kq", hg, h))
                    for i in (0, 1):
                        for t in range(NT):
                            c = slice(t * P, (t + 1) * P)
                            last = pe.matmul(bank[:, i * S + t * P:i * S + (t + 1) * P], gT[:, 1, h, c],
                                             gT[:, 1 - i, h, c], start=True, stop=True)
                    banks.filled(last, ("kq", hg, h))
                for w, name in ((1, "kt"), (2, "vt")):
                    if w == 2:
                        pe.wait_ge(sem("g_silu"), 6 * hg + 6)
                    for t in range(NT):
                        bank = banks.claim(pe, (name, hg, t))
                        for h in range(HG):
                            last = pe.transpose(bank[:, h * P:(h + 1) * P], gT[:, w, h, t * P:(t + 1) * P], ident[:, :])
                        banks.filled(last, (name, hg, t))
                both_t(u0 + 20, "fv", hg)
                for t in range(NT):
                    pe.wait_ge(sem("x1T"), NT * hg + t + 1)
                    bank = banks.claim(pe, ("x1", hg, t))
                    for h in range(HG):
                        last = pe.transpose(bank[:, h * P:(h + 1) * P], XT[:, t, h, :], ident[:, :])
                    banks.filled(last, ("x1", hg, t))
                both_t(u0 + 24, "gz", hg)
                for l in range(1, LEVELS):
                    for t in range(NT):
                        pe.wait_ge(sem("ATm"), 2 * LEVELS * hg + 2 * l + t + 1)
                        if l == 1:
                            banks.moved(pe, ("x1", hg, t))
                        else:
                            banks.moved(pe, ("xx", hg, l - 1, t))
                        bank = banks.claim(pe, ("t1", hg, l, t))
                        for h in range(HG):
                            last = pe.matmul(bank[:, h * P:(h + 1) * P], ATm[:, t, h * P:(h + 1) * P], X[:, t, h, :],
                                             start=True, stop=True)
                        banks.filled(last, ("t1", hg, l, t))
                    for t in range(NT):
                        banks.moved(pe, ("t1", hg, l, t))
                        if l > 1:
                            banks.moved(pe, ("xt", hg, l - 1, t))
                        if l < LEVELS - 1:
                            bank = banks.claim(pe, ("xx", hg, l, t))
                            for h in range(HG):
                                last = pe.matmul(bank[:, h * P:(h + 1) * P], XT[:, t, h, :], T1[:, t, h * P:(h + 1) * P],
                                                 start=True, stop=True)
                            banks.filled(last, ("xx", hg, l, t))
                        bank = banks.claim(pe, ("xt", hg, l, t))
                        for h in range(HG):
                            last = pe.matmul(bank[:, h * P:(h + 1) * P], T1[:, t, h * P:(h + 1) * P], XT[:, t, h, :],
                                             start=True, stop=True)
                        banks.filled(last, ("xt", hg, l, t))
                for j in range(2):
                    banks.moved(pe, ("fq", hg, j))
                    banks.moved(pe, ("fk", hg, j))
                pe.wait_ge(sem("consts2"), 1)
                for h in range(HG):
                    bank = banks.claim(pe, ("lo", hg, h))
                    for t in range(NT):
                        c = bank[:, 0:P] if t == 0 else bank[:, P:384]
                        pe.matmul(c, fqk[:, 0, h, t * P:(t + 1) * P], fqk[:, 1, h, 0:(t + 1) * P], start=True, stop=False)
                        pe.matmul(c, sel[:, HG * hg + h, :], rowp[:, NEGC, 0:(t + 1) * P], start=False, stop=False)
                        last = pe.matmul(c[:, t * P:(t + 1) * P], ident[:, :], negmask[:, :], start=False, stop=True)
                    banks.filled(last, ("lo", hg, h))
                for t in range(NT):
                    banks.moved(pe, ("kt", hg, t))
                    banks.moved(pe, ("vt", hg, t))
                    banks.moved(pe, ("xt", hg, LEVELS - 1, t))

                def per_head(key, *terms):
                    bank = banks.claim(pe, key)
                    for h in range(HG):
                        for i, (a, b) in enumerate(terms):
                            last = pe.matmul(bank[:, h * P:(h + 1) * P], a[:, h, :], b[:, h, :], start=i == 0,
                                             stop=i == len(terms) - 1)
                    banks.filled(last, key)

                per_head(("u0", hg), (XT[:, 0], vb[:, 0]))
                per_head(("wT", hg), (kbg, XT[:, 1]))
                banks.moved(pe, ("u0", hg))
                per_head(("st", hg), (kdec, u[:, 0]))
                pe.wait_ge(sem("attn_masked"), 4 * hg + 4)
                per_head(("o0", hg), (attnT[:, 0], u[:, 0]))
                banks.moved(pe, ("wT", hg))
                banks.moved(pe, ("st", hg))
                per_head(("u1", hg), (XT[:, 1], vb[:, 1]), (wTn, state))
                for h in range(HG):
                    pe.wait_ge(sem("prob"), 4 * hg + h + 1)
                    bank = banks.claim(pe, ("pt", hg, h))
                    pe.transpose(bank[:, 0:P], prob[:, h, 0:P], ident[:, :])
                    pe.transpose(bank[:, P:S], prob[:, h, P:S], ident[:, :])
                    last = pe.transpose(bank[:, S:384], prob[:, h, S:384], ident[:, :])
                    banks.filled(last, ("pt", hg, h))
                banks.moved(pe, ("u1", hg))
                pe.wait_ge(sem("qdec"), 4 * hg + 4)
                per_head(("o1", hg), (egb, state), (attnT[:, 1], u[:, 1]))
                for t in range(NT):
                    banks.moved(pe, ("fv", hg, t))
                for j in range(2):
                    bank = banks.claim(pe, ("pv", hg, j))
                    for h in (2 * j, 2 * j + 1):
                        banks.moved(pe, ("pt", hg, h))
                        c = bank[:, (h % 2) * S:(h % 2 + 1) * S]
                        pe.matmul(c, fv[:, 0, h * P:(h + 1) * P], probT[:, h, 0:S], start=True, stop=False)
                        last = pe.matmul(c[:, P:S], fv[:, 1, h * P:(h + 1) * P], probT[:, h, S:384], start=False, stop=True)
                    banks.filled(last, ("pv", hg, j))
            both_f(UNITS_E, "gf", 0)
            outputs_transposed(1)


def phase_e(nc, A, sem, sb, ring, banks, k, env):
    x, hT, ident, prm2, prow1, prow2, units, hTh, hTl, yf, yg = (
        env[n] for n in "x hT ident prm2 prow1 prow2 units hTh hTl yf yg".split())
    mix_high = sb("mix_high", [P, KC, S], F32R)
    mix_low = sb("mix_low", [P, KC, S], F32R)
    sgf = sb("sgf", [P, 2, 512])
    sgg = sb("sgg", [P, 2, 512])
    part = sb("part", [P, 2, 512])

    for n in range(2):
        banks.plan(*[(w, n, j) for w in ("gf", "bf", "gg", "bg")[n == 0:] for j in range(2)])
    banks.plan(*[("out", n, t) for n in range(2) for t in range(NT)])
    banks.plan("taps", *[("nn", j) for j in range(4)], ("up", 0, 0), ("up", 0, 1))
    junk = hT[:, :, :].rearrange("p (t c) n -> p t (c n)", t=NT)

    def flat(ap, n, j):
        return ap[:, 4 * n + 2 * j:4 * n + 2 * j + 2, :].rearrange("p h s -> p (h s)")

    with nc.Block() as block:
        @block.sync
        def _(sp):
            for g in range(16, UP0 + 3):
                units.freed(sp, g - 2)
                if g < UP0:
                    load_c(sp, A, ring, g)
                else:
                    load_up(sp, A, ring, g - UP0)

        @block.scalar
        def _(act):
            for n in range(2):
                for i, (w, buf) in enumerate((("gf", sgf), ("gg", sgg))):
                    for j in range(2):
                        units.ahead(act, "high", UNITS_E + 16 * n + 8 * i + 2 * j + 2)
                        bank = banks.take(act, (w, n, j))
                        if n and w == "gf":
                            banks.moved(act, ("bf", 0, j))
                        if n and w == "gg":
                            act.wait_ge(sem("mixed"), j + 1)
                        banks.release(act.activation(buf[:, j, :], bank, ACT.Sigmoid), (w, n, j))
                    for j in range(2):
                        units.ahead(act, "high", UNITS_E + 16 * n + 8 * i + 4 + 2 * j + 2)
                        if w == "gg":
                            act.wait_ge(sem("mixed"), 2 * n + j + 1)
                            act.copy(flat(mix_high, n, j), part[:, j, :]).then_inc(sem("mix_high"), 1)
            units.ahead(act, "high", UNITS_OUT + 4)
            k.prepare(act)
            for n in range(2):
                for t in range(NT):
                    banks.moved(act, ("out", n, t))
                    k.squares_of(act, t, n, 0, junk)
                if n == 0:
                    units.ahead(act, "high", UNITS_OUT + 8)
            k.root(act, "nn", 0)
            high_parts(k, act, banks, "nn", hTh)
            units.ahead(act, "high", 4 * UP0 + 3)

        @block.gpsimd
        def _(g):
            units.ahead(g, "low1", 4 * UP0 + 3)

        @block.vector
        def _(v):
            def ahead(n):
                units.ahead(v, "low0", n)

            for n in range(2):
                u0 = UNITS_E + 16 * n
                for j in range(2):
                    ahead(u0 + 4 + 2 * j + 2)
                    bank = banks.take(v, ("bf", n, j))
                    banks.moved(v, ("gf", n, j))
                    if n:
                        v.wait_ge(sem("mix_low"), j + 1)
                    banks.release(v.tensor_tensor(part[:, j, :], sgf[:, j, :], bank, ALU.mult), ("bf", n, j))
                for j in range(2):
                    ahead(u0 + 12 + 2 * j + 2)
                    bank = banks.take(v, ("bg", n, j))
                    banks.moved(v, ("gg", n, j))
                    last = v.tensor_tensor(sgg[:, j, :], sgg[:, j, :], bank, ALU.mult)
                    banks.release(last, ("bg", n, j))
                    banks.moved(v, ("bg", n, j))
                    v.tensor_tensor(part[:, j, :], part[:, j, :], sgg[:, j, :], ALU.add).then_inc(sem("mixed"), 1)
                for j in range(2):
                    v.wait_ge(sem("mix_high"), 2 * n + j + 1)
                    v.tensor_tensor(flat(mix_low, n, j), part[:, j, :], flat(mix_high, n, j).bitcast(F32),
                                    ALU.subtract).then_inc(sem("mix_low"), 1)
            for n in range(2):
                for t in range(NT):
                    ahead(UNITS_OUT + 4 * n + 3 + t)
                    bank = banks.take(v, ("out", n, t))
                    xs = x[:, t, n * 512:(n + 1) * 512]
                    banks.release(v.tensor_tensor(xs, xs, bank, ALU.add), ("out", n, t))
            chain = Chain(v, sem("dveE"))
            k.scale(v, chain, "nn", 0, EPS2)
            evacuate_split(k, v, banks, "nn", prm2[:, 8:16], hTh, hTl)
            units.ahead(v, "low0", 4 * UP0 + 3)

        @block.tensor
        def _(pe):
            for n in range(2):
                u0 = UNITS_E + 16 * n
                for i, w in enumerate(("gf", "bf", "gg", "bg")):
                    if n == 0 and i == 0:
                        continue
                    xh, xl = ((hTh, hTl), yf, (hTh, hTl), yg)[i]
                    columns(pe, units, banks, u0 + 4 * i, [(w, n, j) for j in range(2)], xh, xl)
            for n in range(2):
                rows(pe, units, banks, UNITS_OUT + 4 * n, [("out", n, t) for t in range(NT)], mix_high, mix_low,
                     lambda q: pe.wait_ge(sem("mix_low"), q + 1))
            pe.wait_ge(sem("taps_in"), 16 * 6)
            bank = banks.claim(pe, "taps")
            for h in range(2):
                n = 3 * FF_CHUNKS
                last = pe.transpose(bank[:, h * n:(h + 1) * n], (prow1, prow2)[h][0:n, :], ident[0:n, 0:n])
            banks.filled(last, "taps")
            k.transposes(pe, banks, "nn")
            columns(pe, units, banks, 4 * UP0, [("up", 0, h) for h in range(2)], hTh, hTl,
                    lambda c: pe.wait_ge(sem("nn_low"), c // 2 + 1))


def phase_d(nc, A, out, sem, sb, ring, banks, k, env):
    x, xn, hT, ident, prm2, gain, prow1, prow2, units, hTh, hTl = (
        env[n] for n in "x xn hT ident prm2 gain prow1 prow2 units hTh hTl".split())
    act_high = sb("act_high", [P, FF_CHUNKS, S], F32R)
    act_low = sb("act_low", [P, FF_CHUNKS, S], F32R)
    taps = sb("taps", [P, 2, 3 * FF_CHUNKS])
    cv = sb("cv", [P, 2, 2, 2, S])
    res = xn
    U0 = 4 * UP0
    UD = U0 + 4 * NUP

    for j in range(1, NUP):
        banks.plan(("up", j, 0), ("up", j, 1))
    banks.plan(*[("dn", t, n) for t in range(NT) for n in range(2)])

    with nc.Block() as block:
        @block.sync
        def _(sp):
            for g in range(UP0 + 3, DOWN0 + NDOWN):
                units.freed(sp, g - 2)
                if g < DOWN0:
                    load_up(sp, A, ring, g - UP0)
                else:
                    load_down(sp, A, ring, g - DOWN0)
                if g == UP0 + 3:
                    sp.dma_start(gain[:, :], A["norm_final_2"].unsqueeze(0).to_broadcast([P, D]))\
                        .then_inc(sem("norm_final_in"), 16)
            for t in range(NT):
                sp.wait_ge(sem("norm_scaled"), NT * (k.nth("fin") - 1) + t + 1)
                sp.dma_start(out[0, t * P:(t + 1) * P, :], res[:, t, :]).then_inc(sem("out_stored"), 16)
            sp.wait_ge(sem("out_stored"), 16 * NT)

        @block.scalar
        def _(act):
            flat = hT[:, :, :].rearrange("p (t c) n -> p t (c n)", t=NT)
            for j in range(NUP):
                units.ahead(act, "high", U0 + 4 * j + 2)
                banks.moved(act, ("up", j, 0))
                act.activation(cv[:, j % 2, 0], cv[:, j % 2, 0], ACT.Silu).then_inc(sem("up_silu"), 1)
                if j:
                    act.wait_ge(sem("up_act"), j)
                    act.copy(act_high[:, 2 * j - 2:2 * j, :], cv[:, (j - 1) % 2, 1]).then_inc(sem("act_high"), 1)
                units.ahead(act, "high", U0 + 4 * j + 4)
            act.wait_ge(sem("up_act"), NUP)
            act.copy(act_high[:, 2 * NUP - 2:2 * NUP, :], cv[:, (NUP - 1) % 2, 1]).then_inc(sem("act_high"), 1)
            units.ahead(act, "high", len(units.units))
            k.prepare(act)
            for t in range(NT):
                for n in range(2):
                    act.wait_ge(sem("down_added"), 2 * t + n + 1)
                    k.squares_of(act, t, n, 1, flat)
            k.root(act, "fin", 1)

        @block.gpsimd
        def _(g):
            units.ahead(g, "low1", U0 + 4)
            for j in range(NUP):
                units.ahead(g, "low1", U0 + 4 * j + 4)
                g.wait_ge(sem("act_high"), j + 1)
                g.tensor_tensor(act_low[:, 2 * j:2 * j + 2, :], cv[:, j % 2, 1],
                                act_high[:, 2 * j:2 * j + 2, :].bitcast(F32), ALU.subtract).then_inc(sem("act_low"), 1)
            units.ahead(g, "low1", len(units.units))

        @block.vector
        def _(v):
            chain = Chain(v, sem("dveD"))
            bank = banks.take(v, "taps")
            last = v.tensor_copy(taps[:, :, :], bank[:, 0:6 * FF_CHUNKS].rearrange("p (h n) -> p h n", h=2))
            banks.release(last, "taps")
            banks.moved(v, "taps")
            for j in range(NUP):
                if j >= 2:
                    v.wait_ge(sem("act_low"), j - 1)
                for h in range(2):
                    units.ahead(v, "low0", U0 + 4 * j + 2 * h + 2)
                    bank = banks.take(v, ("up", j, h))
                    for i in range(3):
                        for a in range(2):
                            c = cv[:, j % 2, h, a, :]
                            w = taps[:, h, FF_CHUNKS * (2 - i) + 2 * j + a:FF_CHUNKS * (2 - i) + 2 * j + a + 1]
                            if i == 0:
                                last = v.tensor_scalar(c, bank[:, a * S:(a + 1) * S], w, None, ALU.mult)
                            else:
                                last = v.scalar_tensor_tensor(c[:, i:], bank[:, a * S:(a + 1) * S - i], w, c[:, i:],
                                                              ALU.mult, ALU.add)
                            if i < 2:
                                chain.mark(last)
                            elif a == 0:
                                last.then_inc(sem("up_conv_first"), 1)
                        if i < 2:
                            chain.wait()
                    banks.release(last, ("up", j, h))
                banks.moved(v, ("up", j, 1))
                v.wait_ge(sem("up_silu"), j + 1)
                v.tensor_tensor(cv[:, j % 2, 1], cv[:, j % 2, 0], cv[:, j % 2, 1], ALU.mult)\
                    .then_inc(sem("up_act"), 1)
            units.ahead(v, "low0", len(units.units))
            for t in range(NT):
                for n in range(2):
                    bank = banks.take(v, ("dn", t, n))
                    xs = x[:, t, n * 512:(n + 1) * 512]
                    v.tensor_tensor(xs, xs, bank, ALU.add).then_inc(sem("down_added"), 1)
            v.wait_ge(sem("norm_final_in"), 16)
            k.gained(v, chain, "fin", 1, EPS2, gain[:, :], res)

        @block.tensor
        def _(pe):
            for j in range(1, NUP):
                columns(pe, units, banks, U0 + 4 * j, [("up", j, h) for h in range(2)], hTh, hTl)
            dn = {(t, n): banks.claim(pe, ("dn", t, n)) for t in range(NT) for n in range(2)}
            for c in range(FF_CHUNKS):
                u = UD + c
                if c % 2 == 0:
                    pe.wait_ge(sem("act_low"), c // 2 + 1)
                units.ready(pe, u)
                for t in range(NT):
                    a = slice(t * P, (t + 1) * P)
                    for n in range(2):
                        wh = units.buf(units.high, u)[:, n * 512:(n + 1) * 512]
                        wl = units.buf(units.low, u)[:, n * 512:(n + 1) * 512]
                        pe.matmul(dn[t, n], act_high[:, c, a], wh, start=c == 0, stop=False)
                        pe.matmul(dn[t, n], act_high[:, c, a], wl, start=False, stop=False)
                        last = pe.matmul(dn[t, n], act_low[:, c, a], wh, start=False, stop=c == FF_CHUNKS - 1)
                        if c == FF_CHUNKS - 1 and (t, n) != (1, 1):
                            banks.filled(last, ("dn", t, n))
                units.finish(last, u)


INS = ("x norm1_g w_in ig_b fg_b conv_w head_norm_g pool_w pool_scale w_out norm2_g w_router b_router w_gate "
       "b_gate w_up b_up w_down b_down normf_g norm_mix_2 w_in_2 fox_f_bias_2 gdn_conv_w_2 gdn_a_log_2 "
       "gdn_dt_bias_2 gdn_norm_2 w_branch_fox_2 w_branch_gdn_2 w_out_2 norm_ffn_2 w_up_2 ffn_conv_w_2 w_down_2 "
       "norm_final_2").split()


def kernel(**inputs):
    import concourse.bacc as bacc
    from concourse.bass_utils import run_bass_kernel_spmd

    nc = bacc.Bacc("TRN2", target_bir_lowering=False, num_devices=1)
    arrays, A = {}, {}
    for name in INS:
        a = np.ascontiguousarray(inputs[name])
        arrays[f"in_{name}"] = a
        A[name] = nc.dram_tensor(f"in_{name}", a.shape, mybir.dt.from_np(a.dtype), kind="ExternalInput").ap()
    out = nc.dram_tensor("out", (1, S, D), F32, kind="ExternalOutput").ap()
    build(nc, A, out)
    r = run_bass_kernel_spmd(nc, [arrays], core_ids=[0])
    return r.results[0]["out"]
```
